# Optimizing a Trainium2 kernel written in Bass

```python
import math
import jax, jax.numpy as jnp
from jax import lax
import numpy as np

D_MODEL = 1024
BATCH = 1
SEQ = 512
DEPTH = 2

N_MIXERS = 2
ROPE_THETA = 10000.0
LN_EPS = 1e-5
DN_ALPHA = (2 * DEPTH) ** 0.25
DN_BETA = (8 * DEPTH) ** -0.25

DA_HEAD_DIM = 64
DA_HEADS = D_MODEL // (2 * DA_HEAD_DIM)
DA_Q_BLOCK = 128

SW_HEAD_DIM = 64
SW_HEADS = D_MODEL // SW_HEAD_DIM
SW_KV_HEADS = max(1, SW_HEADS // 8)
SW_GROUP = SW_HEADS // SW_KV_HEADS
SW_WINDOW = 128
SW_BLOCK = 128

PK_HEADS = 8
PK_N_KEYS = 128
PK_N_EXPERTS = PK_N_KEYS * PK_N_KEYS
PK_KEY_DIM = 128
PK_TOPK = 16
PK_TOKEN_BLOCK = 128

N_DIFF_LAYERS = (DEPTH + 1) // 2
N_SWA_LAYERS = DEPTH // 2

kernel_name = 'hybrid_diffattn_swa_sinks_peer_deepnorm'

def layer_norm(x, g, b):
    xf = x.astype(jnp.float32)
    mu = xf.mean(-1, keepdims=True)
    var = jnp.square(xf - mu).mean(-1, keepdims=True)
    return ((xf - mu) * lax.rsqrt(var + LN_EPS) * g.astype(jnp.float32) + b.astype(jnp.float32)).astype(x.dtype)

def rms_norm(x, g):
    xf = x.astype(jnp.float32)
    y = xf * lax.rsqrt(jnp.mean(xf * xf, -1, keepdims=True) + LN_EPS) * g.astype(jnp.float32)
    return y.astype(x.dtype)

def rope_tables(seq, dim):
    inv = 1.0 / (ROPE_THETA ** (jnp.arange(0, dim, 2, dtype=jnp.float32) / dim))
    ang = jnp.arange(seq, dtype=jnp.float32)[:, None] * inv[None, :]
    return jnp.cos(ang), jnp.sin(ang)

def apply_rope(t, cos, sin):
    t1, t2 = jnp.split(t.astype(jnp.float32), 2, axis=-1)
    c = cos[None, :, None, :]
    s = sin[None, :, None, :]
    return jnp.concatenate([t1 * c - t2 * s, t2 * c + t1 * s], axis=-1).astype(t.dtype)

def diff_attention(x, w_qkv, lam_params, subln_g, w_o, lambda_init, cos, sin):
    B, S, _ = x.shape
    H, d = DA_HEADS, DA_HEAD_DIM
    q, k, v = jnp.split(x @ w_qkv, 3, axis=-1)
    q = apply_rope(q.reshape(B, S, 2 * H, d), cos, sin).reshape(B, S, H, 2, d)
    k = apply_rope(k.reshape(B, S, 2 * H, d), cos, sin).reshape(B, S, H, 2, d)
    v = v.reshape(B, S, H, 2 * d)
    lp = lam_params.astype(jnp.float32)
    lam = jnp.exp(jnp.sum(lp[0] * lp[1])) - jnp.exp(jnp.sum(lp[2] * lp[3])) + lambda_init
    nb = S // DA_Q_BLOCK
    qb = q.reshape(B, nb, DA_Q_BLOCK, H, 2, d).transpose(1, 0, 2, 3, 4, 5)
    kpos = jnp.arange(S)
    scale = d ** -0.5

    def one_block(args):
        qi, bi = args
        s = jnp.einsum('bqhpd,bkhpd->bhpqk', qi, k, preferred_element_type=jnp.float32) * scale
        qpos = bi * DA_Q_BLOCK + jnp.arange(DA_Q_BLOCK)
        s = jnp.where((kpos[None, :] <= qpos[:, None])[None, None, None], s, -jnp.inf)
        p = jax.nn.softmax(s, axis=-1)
        a = p[:, :, 0] - lam * p[:, :, 1]
        return jnp.einsum('bhqk,bkhe->bqhe', a.astype(v.dtype), v)

    o = lax.map(one_block, (qb, jnp.arange(nb)))
    o = o.transpose(1, 0, 2, 3, 4).reshape(B, S, H, 2 * d)
    o = rms_norm(o, subln_g) * (1.0 - lambda_init)
    return o.reshape(B, S, H * 2 * d) @ w_o

def swa_attention(x, w_qkv, b_qkv, sinks, w_o, b_o, cos, sin):
    B, S, _ = x.shape
    H, KV, G, d, L = SW_HEADS, SW_KV_HEADS, SW_GROUP, SW_HEAD_DIM, SW_BLOCK
    qkv = x @ w_qkv + b_qkv
    q, k, v = jnp.split(qkv, [H * d, (H + KV) * d], axis=-1)
    q = apply_rope(q.reshape(B, S, H, d), cos, sin)
    k = apply_rope(k.reshape(B, S, KV, d), cos, sin)
    v = v.reshape(B, S, KV, d)
    nb = S // L
    qb = q.reshape(B, nb, L, KV, G, d)

    def banded(t):
        tb = t.reshape(B, nb, L, KV, d)
        prev = jnp.pad(tb, ((0, 0), (1, 0), (0, 0), (0, 0), (0, 0)))[:, :-1]
        return jnp.concatenate([prev, tb], axis=2)

    kb, vb = banded(k), banded(v)
    s = jnp.einsum('bnqkgd,bnjkd->bnkgqj', qb, kb, preferred_element_type=jnp.float32) * (d ** -0.5)
    qi = jnp.arange(L)[:, None] + L
    kj = jnp.arange(2 * L)[None, :]
    rel = qi - kj
    local = (rel >= 0) & (rel < SW_WINDOW)
    valid = local[None] & ((jnp.arange(nb)[:, None, None] > 0) | (kj[None] >= L))
    s = jnp.where(valid[None, :, None, None], s, -jnp.inf)
    sink = sinks.astype(jnp.float32).reshape(KV, G)[None, None, :, :, None, None]
    m = jnp.maximum(s.max(-1, keepdims=True), sink)
    e = jnp.exp(s - m)
    p = e / (e.sum(-1, keepdims=True) + jnp.exp(sink - m))
    o = jnp.einsum('bnkgqj,bnjkd->bnqkgd', p.astype(vb.dtype), vb).reshape(B, S, H * d)
    return o @ w_o + b_o

def peer(x, w_query, sub_keys, u_emb, v_emb):
    B, S, D = x.shape
    K = PK_TOPK
    xt = x.reshape((B * S) // PK_TOKEN_BLOCK, PK_TOKEN_BLOCK, D)

    def one_block(xb):
        Tb = xb.shape[0]
        q = (xb @ w_query).reshape(Tb, PK_HEADS, 2, PK_KEY_DIM // 2)
        sc = jnp.einsum('thcd,hcnd->thcn', q, sub_keys, preferred_element_type=jnp.float32)
        s1, i1 = lax.top_k(sc[:, :, 0], K)
        s2, i2 = lax.top_k(sc[:, :, 1], K)
        cand = (s1[..., :, None] + s2[..., None, :]).reshape(Tb, PK_HEADS, K * K)
        cidx = (i1[..., :, None] * PK_N_KEYS + i2[..., None, :]).reshape(Tb, PK_HEADS, K * K)
        top_s, pos = lax.top_k(cand, K)
        eidx = jnp.take_along_axis(cidx, pos, axis=-1)
        g = jax.nn.softmax(top_s, axis=-1)
        u = u_emb[eidx]
        hval = jax.nn.gelu(jnp.einsum('thkd,td->thk', u, xb, preferred_element_type=jnp.float32), approximate=False)
        w = (g * hval).astype(xb.dtype)
        return jnp.einsum('thk,thkd->td', w, v_emb[eidx])

    return lax.map(one_block, xt).reshape(B, S, D)

def setup_inputs(seed: int = 0) -> dict:
    key = jax.random.key(seed)
    ks = jax.random.split(key, 20)
    f32 = jnp.float32
    D = D_MODEL

    def nrm(k, shape, scale):
        return jax.random.normal(k, shape, f32) * scale

    x = nrm(ks[0], (BATCH, SEQ, D), 1.0)
    da_w_qkv = nrm(ks[1], (N_DIFF_LAYERS, D, 3 * D), D ** -0.5)
    da_w_qkv = da_w_qkv.at[..., 2 * D:].multiply(DN_BETA)
    da_lambda = nrm(ks[2], (N_DIFF_LAYERS, 4, DA_HEAD_DIM), 0.1)
    da_subln_g = 1.0 + nrm(ks[3], (N_DIFF_LAYERS, 2 * DA_HEAD_DIM), 0.02)
    da_w_o = nrm(ks[4], (N_DIFF_LAYERS, D, D), D ** -0.5 * DN_BETA)
    sw_width = (SW_HEADS + 2 * SW_KV_HEADS) * SW_HEAD_DIM
    sw_w_qkv = nrm(ks[5], (N_SWA_LAYERS, D, sw_width), D ** -0.5)
    sw_w_qkv = sw_w_qkv.at[..., (SW_HEADS + SW_KV_HEADS) * SW_HEAD_DIM:].multiply(DN_BETA)
    sw_b_qkv = nrm(ks[6], (N_SWA_LAYERS, sw_width), 0.02)
    sw_sinks = nrm(ks[7], (N_SWA_LAYERS, SW_HEADS), 0.5)
    sw_w_o = nrm(ks[8], (N_SWA_LAYERS, SW_HEADS * SW_HEAD_DIM, D), (SW_HEADS * SW_HEAD_DIM) ** -0.5 * DN_BETA)
    sw_b_o = nrm(ks[9], (N_SWA_LAYERS, D), 0.02)
    pk_w_query = nrm(ks[10], (DEPTH, D, PK_HEADS * PK_KEY_DIM), D ** -0.5)
    pk_sub_keys = nrm(ks[11], (DEPTH, PK_HEADS, 2, PK_N_KEYS, PK_KEY_DIM // 2), (PK_KEY_DIM // 2) ** -0.5)
    pk_u = nrm(ks[12], (DEPTH, PK_N_EXPERTS, D), D ** -0.5)
    pk_v = nrm(ks[13], (DEPTH, PK_N_EXPERTS, D), DN_BETA * PK_HEADS ** -0.5)
    ln1_g = 1.0 + nrm(ks[14], (DEPTH, D), 0.02)
    ln1_b = nrm(ks[15], (DEPTH, D), 0.02)
    ln2_g = 1.0 + nrm(ks[16], (DEPTH, D), 0.02)
    ln2_b = nrm(ks[17], (DEPTH, D), 0.02)
    return {'x': x, 'da_w_qkv': da_w_qkv, 'da_lambda': da_lambda, 'da_subln_g': da_subln_g,
            'da_w_o': da_w_o, 'sw_w_qkv': sw_w_qkv, 'sw_b_qkv': sw_b_qkv, 'sw_sinks': sw_sinks,
            'sw_w_o': sw_w_o, 'sw_b_o': sw_b_o, 'pk_w_query': pk_w_query, 'pk_sub_keys': pk_sub_keys,
            'pk_u': pk_u, 'pk_v': pk_v, 'ln1_g': ln1_g, 'ln1_b': ln1_b, 'ln2_g': ln2_g, 'ln2_b': ln2_b}

def reference(x, da_w_qkv, da_lambda, da_subln_g, da_w_o, sw_w_qkv, sw_b_qkv, sw_sinks, sw_w_o, sw_b_o,
              pk_w_query, pk_sub_keys, pk_u, pk_v, ln1_g, ln1_b, ln2_g, ln2_b):
    S = x.shape[1]
    cos, sin = rope_tables(S, DA_HEAD_DIM)
    for i in range(DEPTH):
        j = i // N_MIXERS
        if i % N_MIXERS == 0:
            lambda_init = 0.8 - 0.6 * math.exp(-0.3 * i)
            mix = diff_attention(x, da_w_qkv[j], da_lambda[j], da_subln_g[j], da_w_o[j], lambda_init, cos, sin)
        else:
            mix = swa_attention(x, sw_w_qkv[j], sw_b_qkv[j], sw_sinks[j], sw_w_o[j], sw_b_o[j], cos, sin)
        x = layer_norm(DN_ALPHA * x + mix, ln1_g[i], ln1_b[i])
        x = layer_norm(DN_ALPHA * x + peer(x, pk_w_query[i], pk_sub_keys[i], pk_u[i], pk_v[i]), ln2_g[i], ln2_b[i])
    return x


_drawn_inputs = setup_inputs


def setup_inputs(seed=0):
    import zlib

    import numpy as np

    out = dict(_drawn_inputs(seed))
    spreads = {}
    factors = {'da_subln_g': 5.787, 'sw_b_qkv': 6.861, 'sw_sinks': 37.107, 'sw_b_o': 3.514}
    for name, (base, spread) in spreads.items():
        noise = np.random.default_rng([zlib.crc32(name.encode()), seed]).standard_normal(out[name].shape)
        drawn = base * np.exp(spread * noise) if base else spread * noise
        out[name] = __import__('jax').numpy.asarray(drawn.astype(out[name].dtype))
    for name, factor in factors.items():
        out[name] = (out[name] * factor).astype(out[name].dtype)
    return out
```

```python
import math
from contextlib import ExitStack

import concourse.bass as bass
from concourse import mybir

ALU = mybir.AluOpType
ACT = mybir.ActivationFunctionType
AX = mybir.AxisListType
F32 = mybir.dt.float32
F32R = mybir.dt.float32r
U32 = mybir.dt.uint32

P = 128
T = 512
NT = T // P
D = 1024
C = D // P
DEPTH = 2
ALPHA = (2 * DEPTH) ** 0.25
EPS = 1e-5
HD = 64
SCALE = HD ** -0.5
NEG = -1e30
LAMBDA_INIT = 0.8 - 0.6 * math.exp(0.0)

PH = 8
NK = 128
K = 16
TG = 64
JG = 2
GROUPS = NK // JG


def dense(nc, xT, u_l, v_l, g_dram, acc, tag):
    with ExitStack() as ctx:
        def sb(name, shape, dt):
            return ctx.enter_context(nc.sbuf_tensor(name + tag, shape, dt))

        def sem(name):
            return ctx.enter_context(nc.semaphore(name + tag))

        xh = sb("xh", [P, C, T], F32R)
        xl = sb("xl", [P, C, T], F32R)
        ur = sb("ur", [P, 2, JG, C * P], F32)
        uh = sb("uh", [P, JG, C, P], F32R)
        ul = sb("ul", [P, JG, C, P], F32R)
        vr = sb("vr", [P, 2, JG, D], F32)
        vh = sb("vh", [P, 2, JG, D], F32R)
        vl = sb("vl", [P, 2, JG, D], F32R)
        gt = sb("gt", [P, 2, T // TG, JG, TG], F32)
        act_h = sb("act_h", [P, 2, T], F32)
        wf = sb("wf", [P, 2, T], F32)
        wh = sb("wh", [P, 2, JG, T], F32R)
        wl = sb("wl", [P, 2, JG, T], F32R)
        ph = [ctx.enter_context(nc.psum_tensor(f"ph{n}{tag}", [P, T], F32)) for n in range(2)]
        pv = [ctx.enter_context(nc.psum_tensor(f"pv{n}{tag}", [P, T], F32)) for n in range(4)]

        u_loaded = [sem(f"u_loaded{n}") for n in range(2)]
        v_loaded = [sem(f"v_loaded{n}") for n in range(2)]
        g_loaded = [sem(f"g_loaded{n}") for n in range(2)]
        xh_ready = sem("xh_ready")
        xl_ready = sem("xl_ready")
        uh_ready = sem("uh_ready")
        ul_ready = sem("ul_ready")
        vh_ready = sem("vh_ready")
        vl_ready = sem("vl_ready")
        h_done = sem("h_done")
        gelu_done = sem("gelu_done")
        wf_ready = sem("wf_ready")
        wh_ready = sem("wh_ready")
        wl_ready = sem("wl_ready")
        v_done = sem("v_done")
        acc_done = sem("acc_done")
        acc_zero = sem("acc_zero")
        block = ctx.enter_context(nc.Block())

        def pairs(eng, step, first, last):
            for g in range(2):
                step(g, g % 2, g + 1 < GROUPS)
            with eng.Fori(1, GROUPS // 2 - 1) as i:
                for b in range(2):
                    step(i * 2 + b, b, True)
            for g in range(GROUPS - 2, GROUPS):
                step(g, g % 2, g + 1 < GROUPS)

        @block.sync
        def _(sp):
            def load(g, b, more):
                peeled = isinstance(g, int) and g < 2
                if not peeled:
                    sp.wait_ge(ul_ready, (g - 1) * JG)
                    sp.wait_ge(uh_ready, (g - 1) * JG)
                sp.dma_start(ur[:, b], u_l[g]).then_inc(u_loaded[b], 16)
                if not peeled:
                    sp.wait_ge(wf_ready, (g - 1) * JG)
                sp.dma_start(gt[:, b], g_dram[:, :, bass.ds(g * JG, JG), :].rearrange("g i j t -> i g j t")
                             ).then_inc(g_loaded[b], 16)
                if not peeled:
                    sp.wait_ge(vl_ready, (g - 1) * JG)
                    sp.wait_ge(vh_ready, (g - 1) * JG)
                sp.dma_start(vr[:, b], v_l[g]).then_inc(v_loaded[b], 16)
            pairs(sp, load, None, None)

        def count16(g, b):
            if isinstance(g, int):
                return 16 * (g // 2 + 1)
            return (g - b) * 8 + 16

        @block.tensor
        def _(pe):
            pe.wait_ge(xh_ready, 1)
            pe.wait_ge(xl_ready, 1)

            def hidden(g, b):
                for jj in range(JG):
                    pe.wait_ge(uh_ready, g * JG + jj + 1)
                    pe.wait_ge(ul_ready, g * JG + jj + 1)
                    if not (isinstance(g, int) and g == 0):
                        pe.wait_ge(gelu_done, g * JG + jj - 1)
                    for c in range(C):
                        pe.matmul(ph[jj][:], uh[:, jj, c, :], xh[:, c, :], start=(c == 0), stop=False)
                        pe.matmul(ph[jj][:], uh[:, jj, c, :], xl[:, c, :], start=False, stop=False)
                        last = pe.matmul(ph[jj][:], ul[:, jj, c, :], xh[:, c, :], start=False,
                                         stop=(c == C - 1))
                    last.then_inc(h_done, 1)

            def output(g, b):
                pe.wait_ge(vh_ready, (g + 1) * JG)
                pe.wait_ge(vl_ready, (g + 1) * JG)
                pe.wait_ge(wh_ready, (g + 1) * JG)
                pe.wait_ge(wl_ready, (g + 1) * JG)
                for n in range(2 * NT):
                    tt, dh = n // 2, n % 2
                    if not (isinstance(g, int) and g == 0 and n < 4):
                        pe.wait_ge(acc_done, g * 8 + n - 3)
                    for jj in range(JG):
                        w_hi = wh[:, b, jj, tt * P:(tt + 1) * P]
                        w_lo = wl[:, b, jj, tt * P:(tt + 1) * P]
                        v_hi = vh[:, b, jj, dh * 512:(dh + 1) * 512]
                        v_lo = vl[:, b, jj, dh * 512:(dh + 1) * 512]
                        pe.matmul(pv[n % 4][:], w_hi, v_hi, start=(jj == 0), stop=False)
                        pe.matmul(pv[n % 4][:], w_hi, v_lo, start=False, stop=False)
                        last = pe.matmul(pv[n % 4][:], w_lo, v_hi, start=False, stop=(jj == JG - 1))
                    last.then_inc(v_done, 1)

            hidden(0, 0)
            hidden(1, 1)
            output(0, 0)
            with pe.Fori(1, GROUPS // 2) as i:
                hidden(i * 2, 0)
                output(i * 2 - 1, 1)
                hidden(i * 2 + 1, 1)
                output(i * 2, 0)
            output(GROUPS - 1, 1)

        @block.scalar
        def _(act):
            act.activation(xh[:], xT[:], ACT.Copy).then_inc(xh_ready, 1)

            def split_u(g, b, jj):
                act.wait_ge(u_loaded[b], count16(g, b))
                if not (isinstance(g, int) and g == 0):
                    act.wait_ge(h_done, (g - 1) * JG + jj + 1)
                act.activation(uh[:, jj].rearrange("p c n -> p (c n)"), ur[:, b, jj], ACT.Copy
                               ).then_inc(uh_ready, 1)

            for jj in range(JG):
                split_u(0, 0, jj)

            def step(g, b, more):
                for jj in range(JG):
                    if jj == 0:
                        act.wait_ge(v_loaded[b], count16(g, b))
                        if not (isinstance(g, int) and g < 2):
                            act.wait_ge(v_done, (g - 1) * 8)
                    act.activation(vh[:, b, jj], vr[:, b, jj], ACT.Copy).then_inc(vh_ready, 1)
                    act.wait_ge(h_done, g * JG + jj + 1)
                    if not (isinstance(g, int) and g == 0):
                        act.wait_ge(wf_ready, g * JG + jj - 1)
                    act.activation(act_h[:, jj], ph[jj][:], ACT.Gelu).then_inc(gelu_done, 1)
                    if more:
                        split_u(g + 1, 1 - b, jj)
                    act.wait_ge(wf_ready, g * JG + jj + 1)
                    act.activation(wh[:, b, jj], wf[:, jj], ACT.Copy).then_inc(wh_ready, 1)
            pairs(act, step, None, None)

        @block.vector
        def _(dve):
            dve.memset(acc[:], 0.0).then_inc(acc_zero, 1)
            dve.wait_ge(acc_zero, 1)
            dve.wait_ge(xh_ready, 1)
            dve.tensor_tensor(xl[:], xT[:], xh[:].bitcast(F32), ALU.subtract).then_inc(xl_ready, 1)

            def split_u(g, b, jj):
                dve.wait_ge(uh_ready, g * JG + jj + 1)
                if not (isinstance(g, int) and g == 0):
                    dve.wait_ge(h_done, (g - 1) * JG + jj + 1)
                dve.tensor_tensor(ul[:, jj].rearrange("p c n -> p (c n)"), ur[:, b, jj],
                                  uh[:, jj].rearrange("p c n -> p (c n)").bitcast(F32),
                                  ALU.subtract).then_inc(ul_ready, 1)

            for jj in range(JG):
                split_u(0, 0, jj)

            def add_sums(g):
                for n in range(2 * NT):
                    tt, dh = n // 2, n % 2
                    part = acc[:, tt, dh * 512:(dh + 1) * 512]
                    dve.wait_ge(v_done, g * 8 + n + 1)
                    if not (isinstance(g, int) and g == 0):
                        dve.wait_ge(acc_done, g * 8 + n - 7)
                    dve.tensor_tensor(part, pv[n % 4][:], part, ALU.add).then_inc(acc_done, 1)

            def step(g, b, more):
                for jj in range(JG):
                    dve.wait_ge(vh_ready, g * JG + jj + 1)
                    dve.tensor_tensor(vl[:, b, jj], vr[:, b, jj], vh[:, b, jj].bitcast(F32),
                                      ALU.subtract).then_inc(vl_ready, 1)
                    dve.wait_ge(gelu_done, g * JG + jj + 1)
                    if jj == 0:
                        dve.wait_ge(g_loaded[b], count16(g, b))
                    if not (isinstance(g, int) and g == 0):
                        dve.wait_ge(wh_ready, g * JG + jj - 1)
                        dve.wait_ge(wl_ready, g * JG + jj - 1)
                    dve.tensor_tensor(wf[:, jj].rearrange("p (g t) -> p g t", t=TG),
                                      act_h[:, jj].rearrange("p (g t) -> p g t", t=TG),
                                      gt[:, b, :, jj, :], ALU.mult).then_inc(wf_ready, 1)
                    if more:
                        split_u(g + 1, 1 - b, jj)
                    dve.wait_ge(wh_ready, g * JG + jj + 1)
                    dve.tensor_tensor(wl[:, b, jj], wf[:, jj], wh[:, b, jj].bitcast(F32),
                                      ALU.subtract).then_inc(wl_ready, 1)
                if not (isinstance(g, int) and g == 0):
                    add_sums(g - 1)
            pairs(dve, step, None, None)
            add_sums(GROUPS - 1)


def constants(nc, ctx):
    def sb(name, shape):
        return ctx.enter_context(nc.sbuf_tensor(name, shape, F32))

    ident = sb("ident", [P, P])
    masks = sb("masks", [P, 2, P])
    iota_keys = sb("iota_keys", [P, NK])
    iota_rank = sb("iota_rank", [P, K])
    with ExitStack() as inner:
        cleared = inner.enter_context(nc.semaphore("cleared"))
        block = inner.enter_context(nc.Block())

        @block.gpsimd
        def _(pool):
            pool.memset(ident[:], 0.0).then_inc(cleared, 1)
            pool.memset(masks[:], 0.0).then_inc(cleared, 1)
            pool.iota(iota_keys[:], pattern=[[1, NK]], base=0, channel_multiplier=0,
                      allow_small_or_imprecise_dtypes=True).then_inc(cleared, 1)
            pool.iota(iota_rank[:], pattern=[[1, K]], base=0, channel_multiplier=0,
                      allow_small_or_imprecise_dtypes=True).then_inc(cleared, 1)
            pool.wait_ge(cleared, 4)
            pool.affine_select(out=ident[:], in_=ident[:], compare_op=ALU.not_equal, fill=1.0, base=0,
                               pattern=[[-1, P]], channel_multiplier=1).then_inc(cleared, 1)
            pool.affine_select(out=masks[:, 0], in_=masks[:, 0], compare_op=ALU.is_ge, fill=NEG, base=-1,
                               pattern=[[1, P]], channel_multiplier=-1).then_inc(cleared, 1)
            pool.affine_select(out=masks[:, 1], in_=masks[:, 1], compare_op=ALU.is_ge, fill=NEG, base=0,
                               pattern=[[-1, P]], channel_multiplier=1).then_inc(cleared, 1)
            pool.wait_ge(cleared, 7)
    return ident, masks, iota_keys, iota_rank


def load_tokens(nc, x, x_t, xres, xT):
    with ExitStack() as ctx:
        x_loaded = ctx.enter_context(nc.semaphore("x_loaded"))
        block = ctx.enter_context(nc.Block())

        @block.sync
        def _(sp):
            sp.dma_start(xT[:], x_t).then_inc(x_loaded, 16)
            sp.dma_start(xres[:], x.rearrange("(n p) d -> p n d", p=P)).then_inc(x_loaded, 16)
            sp.wait_ge(x_loaded, 32)


class Chain:

    def __init__(self, eng, s, per=0):
        self.eng, self.s, self.n, self.base, self.per = eng, s, 0, 0, per

    def link(self, ins):
        self.n += 1
        ins.then_inc(self.s, 1)
        self.eng.wait_ge(self.s, self.base + self.n)

    def turn(self, i):
        self.base, self.n = i * self.per, 0

    def turned(self):
        assert self.n == self.per, self.n


def rope(dve, dve_own, a, b, cos, sin, out_a, out_b, tmp):
    dve.tensor_tensor(tmp[:, 0], b, sin, ALU.mult)
    dve.tensor_tensor(tmp[:, 1], a, sin, ALU.mult)
    dve.tensor_tensor(tmp[:, 2], b, cos, ALU.mult)
    dve_own.link(dve.tensor_tensor(tmp[:, 3], a, cos, ALU.mult))
    dve.tensor_tensor(out_a, tmp[:, 3], tmp[:, 0], ALU.subtract)
    return dve.tensor_tensor(out_b, tmp[:, 2], tmp[:, 1], ALU.add)


def diff_attention(nc, xT, w_l, cos_t, sin_t, lam, subln, masks, ident, oT):
    W = 4 * P + 2 * P
    TURNS = 4
    with ExitStack() as ctx:
        def sb(name, shape, dt=F32):
            return ctx.enter_context(nc.sbuf_tensor("da_" + name, shape, dt))

        def sem(name):
            return ctx.enter_context(nc.semaphore("da_" + name))

        w = sb("w", [P, C, W])
        cos, sin = sb("cos", [P, T]), sb("sin", [P, T])
        raw = sb("raw", [P, 4, T])
        rot = sb("rot", [P, 4, T])
        tmp = sb("tmp", [P, 4, T])
        v = sb("v", [P, NT, 2 * P])
        E = sb("E", [P, 2, 2, T])
        A = sb("A", [P, 2, T])
        AT = sb("AT", [P, 2, NT, P])
        o = sb("o", [P, 8, P])
        sq = sb("sq", [P, P])
        ss = sb("ss", [P, 8])
        rms = sb("rms", [P, 8])
        rstd = sb("rstd", [P, 8])
        nmax = sb("nmax", [P, 2, 2])
        rsum = sb("rsum", [P, 2, 2])
        rinv = sb("rinv", [P, 2, 2])
        lam_row = sb("lam_row", [P, 4, HD])
        lam_prod = sb("lam_prod", [P, 2, HD])
        lam_sum = sb("lam_sum", [P, 2])
        lam_exp = sb("lam_exp", [P, 2])
        neg_lam = sb("neg_lam", [P, 1])
        g_row = sb("g_row", [P, P])
        ps = [ctx.enter_context(nc.psum_tensor(f"da_ps{n}", [P, 2, 512], F32)) for n in range(2)]
        pp = [ctx.enter_context(nc.psum_tensor(f"da_pp{n}", [P, 512], F32)) for n in range(2)]
        pt = ctx.enter_context(nc.psum_tensor("da_pt", [P, 512], F32))
        po = ctx.enter_context(nc.psum_tensor("da_po", [P, 512], F32))

        consts_loaded = sem("consts_loaded")
        w_loaded, w_used = sem("w_loaded"), sem("w_used")
        proj_done, proj_out = sem("proj_done"), sem("proj_out")
        rot_ready = sem("rot_ready")
        score_done, nmax_ready, exp_done = sem("score_done"), sem("nmax_ready"), sem("exp_done")
        a_ready, at_done, at_out = sem("a_ready"), sem("at_done"), sem("at_out")
        pv_done, o_out = sem("pv_done"), sem("o_out")
        ms_ready, rms_ready, on_ready = sem("ms_ready"), sem("rms_ready"), sem("on_ready")
        lam_ready, lam_exped, dve_step = sem("lam_ready"), sem("lam_exped"), sem("dve_step")
        block = ctx.enter_context(nc.Block())
        units = [(hl, qb) for hl in range(2) for qb in range(NT)]
        USES = 8

        @block.sync
        def _(sp):
            sp.dma_start(cos[:], cos_t).then_inc(consts_loaded, 16)
            sp.dma_start(sin[:], sin_t).then_inc(consts_loaded, 16)
            sp.dma_start(lam_row[:], lam.partition_broadcast(P)).then_inc(consts_loaded, 16)
            sp.dma_start(g_row[:], subln.partition_broadcast(P)).then_inc(consts_loaded, 16)
            with sp.Fori(0, TURNS) as it:
                sp.wait_ge(w_used, it + 1)
                sp.dma_start(w[:], w_l[it]).then_inc(w_loaded, 16)

        @block.tensor
        def _(pe):
            pe.sem_inc(w_used, 1)
            with pe.Fori(0, TURNS) as it:
                def bank(n):
                    pe.wait_ge(proj_out, it * USES + n + 1)
                    return pp[n % 2]

                pe.wait_ge(w_loaded, it * 16 + 16)
                for n in range(4):
                    dst = bank(n)
                    for c in range(C):
                        last = pe.matmul(dst[:], w[:, c, n * P:(n + 1) * P], xT[:, c, :],
                                         start=(c == 0), stop=(c == C - 1))
                    last.then_inc(proj_done, 1)
                for n in range(4, 6):
                    dst = bank(n)
                    for half in range(2):
                        tt = 2 * (n - 4) + half
                        for c in range(C):
                            last = pe.matmul(dst[:, half * 256:(half + 1) * 256],
                                             xT[:, c, tt * P:(tt + 1) * P], w[:, c, 4 * P:],
                                             start=(c == 0), stop=(c == C - 1))
                    last.then_inc(proj_done, 1)
                pe.wait_ge(proj_done, it * USES + 6)
                pe.sem_inc(w_used, 1)

                def scores(u):
                    hl, qb = units[u]
                    L = (qb + 1) * P
                    if u == 0:
                        pe.wait_ge(rot_ready, it * 2 + 3)
                    pe.wait_ge(exp_done, it * 16 + 2 * u + 2)
                    for p in range(2):
                        m = 2 * hl + p
                        for half in range(2):
                            last = pe.matmul(ps[u % 2][:, p, 0:L],
                                             rot[32 * m:32 * m + 32, half, qb * P:(qb + 1) * P],
                                             rot[32 * m:32 * m + 32, 2 + half, 0:L],
                                             start=(half == 0), stop=(half == 1))
                    last.then_inc(score_done, 1)

                scores(0)
                for u, (hl, qb) in enumerate(units):
                    if u + 1 < 8:
                        scores(u + 1)
                    pe.wait_ge(a_ready, it * 8 + u + 3)
                    pe.wait_ge(at_out, it * 8 + u + 1)
                    for kb in range(qb + 1):
                        last = pe.transpose(pt[:, kb * P:(kb + 1) * P], A[:, u % 2, kb * P:(kb + 1) * P],
                                            ident[:])
                    last.then_inc(at_done, 1)
                    pe.wait_ge(at_out, it * 8 + u + 2)
                    pe.wait_ge(o_out, it * 8 + u + 1)
                    for kb in range(qb + 1):
                        last = pe.matmul(po[:, 0:P], AT[:, u % 2, kb], v[:, kb, hl * P:(hl + 1) * P],
                                         start=(kb == 0), stop=(kb == qb))
                    last.then_inc(pv_done, 1)
                for hl in range(2):
                    dst = bank(6 + hl)
                    pe.wait_ge(on_ready, it * 8 + 4 * hl + 4)
                    for qb in range(NT):
                        last = pe.transpose(dst[:, qb * P:(qb + 1) * P], o[:, 4 * hl + qb], ident[:])
                    last.then_inc(proj_done, 1)

        @block.scalar
        def _(act):
            act.wait_ge(lam_ready, 1)
            act.activation(lam_exp[:], lam_sum[:], ACT.Exp).then_inc(lam_exped, 1)
            act.sem_inc(proj_out, 2)
            act.sem_inc(exp_done, 4)
            act.sem_inc(at_out, 1)
            act.sem_inc(o_out, 1)
            with act.Fori(0, TURNS) as it:
                for n in range(6):
                    act.wait_ge(proj_done, it * USES + n + 1)
                    if n == 0:
                        act.wait_ge(rot_ready, it * 2 + 0 + 1)
                    dst = raw[:, n] if n < 4 else v[:, 2 * (n - 4):2 * (n - 4) + 2].rearrange("p a b -> p (a b)")
                    act.activation(dst, pp[n % 2][:], ACT.Copy).then_inc(proj_out, 1)

                def exps(u):
                    L = (units[u][1] + 1) * P
                    act.wait_ge(nmax_ready, it * 8 + u + 1)
                    act.wait_ge(a_ready, it * 8 + u + 1)
                    for p in range(2):
                        act.activation(E[:, u % 2, p, 0:L], ps[u % 2][:, p, 0:L], ACT.Exp,
                                       bias=nmax[:, u % 2, p:p + 1], scale=SCALE,
                                       accum_out=rsum[:, u % 2, p:p + 1]).then_inc(exp_done, 1)

                exps(0)
                for u, (hl, qb) in enumerate(units):
                    if u + 1 < 8:
                        exps(u + 1)
                    act.wait_ge(at_done, it * 8 + u + 1)
                    act.activation(AT[:, u % 2, 0:qb + 1].rearrange("p a b -> p (a b)"), pt[:, 0:(qb + 1) * P],
                                   ACT.Copy).then_inc(at_out, 1)
                    act.wait_ge(pv_done, it * 8 + u + 1)
                    act.activation(sq[:], po[:, 0:P], ACT.Square, accum_out=ss[:, u:u + 1])
                    act.activation(o[:, u], po[:, 0:P], ACT.Copy).then_inc(o_out, 1)
                act.wait_ge(ms_ready, it + 1)
                act.activation(rms[:], ss[:], ACT.Sqrt).then_inc(rms_ready, 1)
                for hl in range(2):
                    act.wait_ge(proj_done, it * USES + 7 + hl)
                    act.activation(oT[:, it * 2 + hl, :], pp[hl][:], ACT.Copy).then_inc(proj_out, 1)

        @block.vector
        def _(dve):
            own = Chain(dve, dve_step)
            dve.wait_ge(consts_loaded, 64)
            own.link(dve.tensor_tensor(lam_prod[:], lam_row[:, 0:4:2], lam_row[:, 1:4:2], ALU.mult))
            dve.tensor_reduce(lam_sum[:], lam_prod[:], AX.X, ALU.add).then_inc(lam_ready, 1)
            dve.wait_ge(lam_exped, 1)
            own.link(dve.tensor_tensor(neg_lam[:], lam_exp[:, 1:2], lam_exp[:, 0:1], ALU.subtract))
            own.link(dve.tensor_scalar(neg_lam[:], neg_lam[:], -LAMBDA_INIT, None, ALU.add))
            own.link(dve.tensor_scalar(g_row[:], g_row[:], 1.0 - LAMBDA_INIT, None, ALU.mult))
            dve.sem_inc(rot_ready, 1)
            dve.sem_inc(a_ready, 2)
            before = own.n
            own.per = 2 + 2 * 8 + 3 * 8 + 1
            with dve.Fori(0, TURNS) as it:
                own.base, own.n = it * own.per + before, 0
                for half in range(2):
                    dve.wait_ge(proj_out, it * USES + 2 + 2 * half + 2)
                    rope(dve, own, raw[:, 2 * half], raw[:, 2 * half + 1], cos[:], sin[:],
                         rot[:, 2 * half], rot[:, 2 * half + 1], tmp).then_inc(rot_ready, 1)
                    dve.wait_ge(rot_ready, it * 2 + half + 2)

                def maxima(u):
                    hl, qb = units[u]
                    L = (qb + 1) * P
                    dve.wait_ge(score_done, it * 8 + u + 1)
                    diag = ps[u % 2][:, :, qb * P:L]
                    own.link(dve.tensor_tensor(diag, diag, masks[:, 1].unsqueeze(1).broadcast_to([P, 2, P]),
                                               ALU.add))
                    own.link(dve.tensor_reduce(nmax[:, u % 2], ps[u % 2][:, :, 0:L], AX.X, ALU.max,
                                               negate=True))
                    dve.tensor_scalar(nmax[:, u % 2], nmax[:, u % 2], SCALE, None, ALU.mult
                                      ).then_inc(nmax_ready, 1)

                maxima(0)
                for u, (hl, qb) in enumerate(units):
                    L = (qb + 1) * P
                    b = u % 2
                    if u + 1 < 8:
                        maxima(u + 1)
                    dve.wait_ge(exp_done, it * 16 + 2 * u + 6)
                    own.link(dve.reciprocal(rinv[:, b], rsum[:, b]))
                    own.link(dve.tensor_tensor(rinv[:, b, 1:2], rinv[:, b, 1:2], neg_lam[:], ALU.mult))
                    if u >= 2:
                        dve.wait_ge(at_done, it * 8 + u - 1)
                    own.link(dve.tensor_scalar(E[:, b, 0, 0:L], E[:, b, 0, 0:L], rinv[:, b, 0:1], None,
                                               ALU.mult))
                    dve.scalar_tensor_tensor(out=A[:, b, 0:L], in0=E[:, b, 1, 0:L], scalar=rinv[:, b, 1:2],
                                             in1=E[:, b, 0, 0:L], op0=ALU.mult, op1=ALU.add
                                             ).then_inc(a_ready, 1)
                dve.wait_ge(o_out, it * 8 + 9)
                dve.tensor_scalar(ss[:], ss[:], 1.0 / P, EPS, ALU.mult, ALU.add).then_inc(ms_ready, 1)
                dve.wait_ge(rms_ready, it + 1)
                own.link(dve.reciprocal(rstd[:], rms[:]))
                for u in range(8):
                    dve.scalar_tensor_tensor(out=o[:, u], in0=o[:, u], scalar=rstd[:, u:u + 1], in1=g_row[:],
                                             op0=ALU.mult, op1=ALU.mult).then_inc(on_ready, 1)
                own.turned()


def window_attention(nc, xT, w_l, cos_t, sin_t, b_feat, b_v, sinks, masks, ident, oT):
    W = 6 * P + HD
    TURNS = 2
    with ExitStack() as ctx:
        def sb(name, shape, dt=F32):
            return ctx.enter_context(nc.sbuf_tensor("sw_" + name, shape, dt))

        def sem(name):
            return ctx.enter_context(nc.semaphore("sw_" + name))

        w = sb("w", [P, C, W])
        cos, sin = sb("cos", [P, T]), sb("sin", [P, T])
        bias = sb("bias", [P, TURNS, 6])
        bias_v = sb("bias_v", [P, TURNS * HD])
        bv = sb("bv", [P, HD])
        sink_row = sb("sink_row", [P, 16])
        sink = sb("sink", [P, 8])
        raw = sb("raw", [P, 6, T])
        rot = sb("rot", [P, 6, T])
        tmp = sb("tmp", [P, 4, T])
        v = sb("v", [P, NT, HD])
        vb = sb("vb", [P, NT, HD])
        E = sb("E", [P, 2, 4, 256])
        ET = sb("ET", [P, 2, 2, 2, P])
        ETs = sb("ETs", [P, 2, 4, P])
        o = sb("o", [P, NT, 8, HD])
        mx = sb("mx", [P, 2, 4])
        mh = sb("mh", [P, 2, 4])
        nmax = sb("nmax", [P, 2, 4])
        sarg = sb("sarg", [P, 2, 4])
        sexp = sb("sexp", [P, 2, 4])
        rsum = sb("rsum", [P, 2, 4])
        den = sb("den", [P, 2, 4])
        rinv = sb("rinv", [P, 2, 4])
        ps = ctx.enter_context(nc.psum_tensor("sw_ps", [P, 4, 512], F32))
        pp = [ctx.enter_context(nc.psum_tensor(f"sw_pp{n}", [P, 512], F32)) for n in range(2)]
        pt = ctx.enter_context(nc.psum_tensor("sw_pt", [P, 512], F32))
        po = ctx.enter_context(nc.psum_tensor("sw_po", [P, 512], F32))

        consts_loaded = sem("consts_loaded")
        w_loaded, w_used = sem("w_loaded"), sem("w_used")
        proj_done, proj_out = sem("proj_done"), sem("proj_out")
        rot_ready, v_ready = sem("rot_ready"), sem("v_ready")
        score_done, nmax_ready, exp_done = sem("score_done"), sem("nmax_ready"), sem("exp_done")
        at_done, at_out = sem("at_done"), sem("at_out")
        pv_done, on_ready = sem("pv_done"), sem("on_ready")
        dve_step = sem("dve_step")
        block = ctx.enter_context(nc.Block())
        units = [(four, qb) for four in range(2) for qb in range(NT)]
        USES = 12

        @block.sync
        def _(sp):
            sp.dma_start(cos[:], cos_t).then_inc(consts_loaded, 16)
            sp.dma_start(sin[:], sin_t).then_inc(consts_loaded, 16)
            sp.dma_start(bias[:], b_feat).then_inc(consts_loaded, 16)
            sp.dma_start(bias_v[:], b_v.partition_broadcast(P)).then_inc(consts_loaded, 16)
            sp.dma_start(sink_row[:], sinks.partition_broadcast(P)).then_inc(consts_loaded, 16)
            with sp.Fori(0, TURNS) as it:
                sp.wait_ge(w_used, it + 1)
                sp.dma_start(w[:], w_l[it]).then_inc(w_loaded, 16)

        @block.tensor
        def _(pe):
            pe.sem_inc(w_used, 1)
            with pe.Fori(0, TURNS) as it:
                def bank(n):
                    pe.wait_ge(proj_out, it * USES + n + 1)
                    return pp[n % 2]

                pe.wait_ge(w_loaded, it * 16 + 16)
                for n in range(6):
                    dst = bank(n)
                    for c in range(C):
                        last = pe.matmul(dst[:], w[:, c, n * P:(n + 1) * P], xT[:, c, :],
                                         start=(c == 0), stop=(c == C - 1))
                    last.then_inc(proj_done, 1)
                for n in range(6, 8):
                    dst = bank(n)
                    for half in range(2):
                        tt = 2 * (n - 6) + half
                        for c in range(C):
                            last = pe.matmul(dst[:, half * HD:(half + 1) * HD],
                                             xT[:, c, tt * P:(tt + 1) * P], w[:, c, 6 * P:],
                                             start=(c == 0), stop=(c == C - 1))
                    last.then_inc(proj_done, 1)
                pe.wait_ge(proj_done, it * USES + 8)
                pe.sem_inc(w_used, 1)

                def scores(u):
                    four, qb = units[u]
                    k0 = max(0, qb - 1) * P
                    L = (qb + 1) * P - k0
                    if u == 0:
                        pe.wait_ge(rot_ready, it * 3 + 4)
                    pe.wait_ge(exp_done, it * 40 + 5 * u + 5)
                    for m in range(4):
                        for half in range(2):
                            last = pe.matmul(ps[:, m, 0:L],
                                             rot[32 * m:32 * m + 32, 2 * four + half, qb * P:(qb + 1) * P],
                                             rot[32 * m:32 * m + 32, 4 + half, k0:k0 + L],
                                             start=(half == 0), stop=(half == 1))
                    last.then_inc(score_done, 1)

                scores(0)
                for u, (four, qb) in enumerate(units):
                    nb = min(2, qb + 1)
                    kb0 = max(0, qb - 1)
                    if u + 1 < 8:
                        scores(u + 1)
                    pe.wait_ge(exp_done, it * 40 + 5 * u + 10)
                    for r in range(2):
                        pe.wait_ge(at_out, it * 16 + 2 * u + r + 1)
                        for m in range(2):
                            for kb in range(nb):
                                last = pe.transpose(pt[:, (2 * m + kb) * P:(2 * m + kb + 1) * P],
                                                    E[:, u % 2, 2 * r + m, kb * P:(kb + 1) * P], ident[:])
                        last.then_inc(at_done, 1)
                    if u == 0:
                        pe.wait_ge(v_ready, it + 1)
                    pe.wait_ge(at_out, it * 16 + 2 * u + 3)
                    pe.wait_ge(on_ready, it * 8 + u + 1)
                    for m in range(4):
                        for kb in range(nb):
                            blk = ET[:, u % 2, m % 2, kb] if m < 2 else ETs[:, u % 2, 2 * (m % 2) + kb]
                            last = pe.matmul(po[:, m * HD:(m + 1) * HD], blk, vb[:, kb0 + kb],
                                             start=(kb == 0), stop=(kb == nb - 1))
                    last.then_inc(pv_done, 1)
                for cc in range(4):
                    dst = bank(8 + cc)
                    pe.wait_ge(on_ready, it * 8 + 9)
                    for qb in range(NT):
                        last = pe.transpose(dst[:, qb * P:(qb + 1) * P],
                                            o[:, qb, 2 * cc:2 * cc + 2].rearrange("p a b -> p (a b)"), ident[:])
                    last.then_inc(proj_done, 1)

        @block.scalar
        def _(act):
            act.sem_inc(proj_out, 2)
            act.sem_inc(exp_done, 5)
            act.sem_inc(at_out, 1)
            act.wait_ge(consts_loaded, 80)
            with act.Fori(0, TURNS) as it:
                for n in range(8):
                    act.wait_ge(proj_done, it * USES + n + 1)
                    if n == 0:
                        act.wait_ge(rot_ready, it * 3 + 1)
                    if n < 6:
                        act.activation(raw[:, n], pp[n % 2][:], ACT.Identity, bias=bias[:, it, n:n + 1]
                                       ).then_inc(proj_out, 1)
                    else:
                        act.activation(v[:, 2 * (n - 6):2 * (n - 6) + 2].rearrange("p a b -> p (a b)"),
                                       pp[n % 2][:, 0:2 * HD], ACT.Copy).then_inc(proj_out, 1)

                def exps(u):
                    L = min(2, units[u][1] + 1) * P
                    act.wait_ge(nmax_ready, it * 8 + u + 1)
                    if u >= 2:
                        act.wait_ge(at_done, it * 16 + 2 * u - 2)
                    for m in range(4):
                        act.activation(E[:, u % 2, m, 0:L], ps[:, m, 0:L], ACT.Exp,
                                       bias=nmax[:, u % 2, m:m + 1], scale=SCALE,
                                       accum_out=rsum[:, u % 2, m:m + 1]).then_inc(exp_done, 1)
                    act.activation(sexp[:, u % 2], sarg[:, u % 2], ACT.Exp).then_inc(exp_done, 1)

                exps(0)
                for u, (four, qb) in enumerate(units):
                    nb = min(2, qb + 1)
                    if u + 1 < 8:
                        exps(u + 1)
                    for r in range(2):
                        act.wait_ge(at_done, it * 16 + 2 * u + r + 1)
                        src = pt[:].rearrange("p (m k n) -> p m k n", m=2, k=2)[:, :, 0:nb]
                        if r == 0:
                            dst = ET[:, u % 2, :, 0:nb]
                        else:
                            dst = ETs[:, u % 2].rearrange("p (m k) n -> p m k n", m=2)[:, :, 0:nb]
                        act.activation(dst, src, ACT.Copy).then_inc(at_out, 1)
                for cc in range(4):
                    act.wait_ge(proj_done, it * USES + 9 + cc)
                    act.activation(oT[:, it * 4 + cc, :], pp[cc % 2][:], ACT.Copy).then_inc(proj_out, 1)

        @block.vector
        def _(dve):
            own = Chain(dve, dve_step, per=1 + 3 + 8 * 3 + 8 * 2)
            dve.wait_ge(consts_loaded, 80)
            dve.sem_inc(rot_ready, 1)
            dve.sem_inc(on_ready, 1)
            with dve.Fori(0, TURNS) as it:
                own.turn(it)
                dve.tensor_copy(bv[:], bias_v[:, bass.ds(it * HD, HD)])
                own.link(dve.tensor_copy(sink[:], sink_row[:, bass.ds(it * 8, 8)]))
                for part in (0, 1, 2):
                    dve.wait_ge(proj_out, it * USES + 2 + 2 * part + 2)
                    rope(dve, own, raw[:, 2 * part], raw[:, 2 * part + 1], cos[:], sin[:],
                         rot[:, 2 * part], rot[:, 2 * part + 1], tmp).then_inc(rot_ready, 1)
                    dve.wait_ge(rot_ready, it * 3 + part + 2)
                dve.wait_ge(proj_out, it * USES + 10)
                dve.tensor_tensor(vb[:], v[:], bv[:].unsqueeze(1).broadcast_to([P, NT, HD]), ALU.add
                                  ).then_inc(v_ready, 1)

                def maxima(u):
                    four, qb = units[u]
                    b = u % 2
                    L = min(2, qb + 1) * P
                    dve.wait_ge(score_done, it * 8 + u + 1)
                    mask = masks[:].rearrange("p a b -> p (a b)")[:, 2 * P - L:]
                    own.link(dve.tensor_tensor(ps[:, :, 0:L], ps[:, :, 0:L],
                                               mask.unsqueeze(1).broadcast_to([P, 4, L]), ALU.add))
                    own.link(dve.tensor_reduce(mx[:, b], ps[:, :, 0:L], AX.X, ALU.max))
                    own.link(dve.scalar_tensor_tensor(out=mh[:, b], in0=mx[:, b], scalar=SCALE,
                                                      in1=sink[:, 4 * four:4 * four + 4], op0=ALU.mult,
                                                      op1=ALU.max))
                    dve.tensor_scalar(nmax[:, b], mh[:, b], -1.0, None, ALU.mult)
                    dve.tensor_tensor(sarg[:, b], sink[:, 4 * four:4 * four + 4], mh[:, b], ALU.subtract
                                      ).then_inc(nmax_ready, 1)

                maxima(0)
                for u, (four, qb) in enumerate(units):
                    b = u % 2
                    if u + 1 < 8:
                        maxima(u + 1)
                    dve.wait_ge(exp_done, it * 40 + 5 * u + 10)
                    own.link(dve.tensor_tensor(den[:, b], rsum[:, b], sexp[:, b], ALU.add))
                    own.link(dve.reciprocal(rinv[:, b], den[:, b]))
                    dve.wait_ge(pv_done, it * 8 + u + 1)
                    dve.tensor_tensor(o[:, qb, 4 * four:4 * four + 4],
                                      po[:, 0:4 * HD].rearrange("p (m e) -> p m e", m=4),
                                      rinv[:, b].unsqueeze(2).broadcast_to([P, 4, HD]), ALU.mult
                                      ).then_inc(on_ready, 1)
                own.turned()


def norm_tile(dve, own, act_sqrt, r, stats, mv, var, std, rstd, g_row, b_row, out):
    for half in range(2):
        ins = dve.bn_stats(stats[:, half], r[:, half * 512:(half + 1) * 512])
        own.link(ins)
    own.link(dve.bn_aggr(mv, stats))
    act_sqrt(dve.tensor_scalar(var, mv[:, 1:2], EPS, None, ALU.add))
    own.link(dve.reciprocal(rstd, std))
    own.link(dve.tensor_scalar(r, r, mv[:, 0:1], rstd, ALU.subtract, ALU.mult))
    own.link(dve.tensor_tensor(r, r, g_row, ALU.mult))
    return dve.tensor_tensor(out, r, b_row, ALU.add)


def add_and_norm(nc, tag, xres, xT, ident, g, b, *, oT=None, w_o=None, b_o=None, acc=None, out=None):
    with ExitStack() as ctx:
        def sb(name, shape, dt=F32):
            return ctx.enter_context(nc.sbuf_tensor(name + tag, shape, dt))

        def sem(name):
            return ctx.enter_context(nc.semaphore(name + tag))

        g_row, b_row = sb("g_row", [P, D]), sb("b_row", [P, D])
        bo_row = sb("bo_row", [P, D]) if b_o is not None else None
        wo = sb("wo", [P, C, D]) if w_o is not None else None
        r = sb("r", [P, 2, D])
        stats = sb("stats", [P, 2, 6])
        mv = sb("mv", [P, 2])
        var, std, rstd = sb("var", [P, 1]), sb("std", [P, 1]), sb("rstd", [P, 1])
        banks = [ctx.enter_context(nc.psum_tensor(f"bank{n}{tag}", [P, 512], F32)) for n in range(8)]
        w_loaded, rows_loaded, stored = sem("w_loaded"), sem("rows_loaded"), sem("stored")
        mix_done, mix_used, var_ready, std_ready = sem("mix_done"), sem("mix_used"), sem("var_ready"), sem("std_ready")
        x_ready, xt_done, xt_out, dve_step = sem("x_ready"), sem("xt_done"), sem("xt_out"), sem("dve_step")
        block = ctx.enter_context(nc.Block())

        @block.sync
        def _(sp):
            if w_o is not None:
                sp.dma_start(wo[:], w_o.rearrange("(c p) n -> p c n", p=P)).then_inc(w_loaded, 16)
            sp.dma_start(g_row[:], g.partition_broadcast(P)).then_inc(rows_loaded, 16)
            sp.dma_start(b_row[:], b.partition_broadcast(P)).then_inc(rows_loaded, 16)
            if b_o is not None:
                sp.dma_start(bo_row[:], b_o.partition_broadcast(P)).then_inc(rows_loaded, 16)
            if out is not None:
                for tt in range(NT):
                    sp.wait_ge(x_ready, tt + 1)
                    sp.dma_start(out[tt * P:(tt + 1) * P, :], xres[:, tt]).then_inc(stored, 16)
                sp.wait_ge(stored, 16 * NT)

        @block.tensor
        def _(pe):
            if w_o is not None:
                pe.wait_ge(w_loaded, 16)
                for tt in range(NT):
                    for dh in range(2):
                        for c in range(C):
                            last = pe.matmul(banks[2 * tt + dh][:], oT[:, c, tt * P:(tt + 1) * P],
                                             wo[:, c, dh * 512:(dh + 1) * 512], start=(c == 0),
                                             stop=(c == C - 1))
                        last.then_inc(mix_done, 1)
            if out is None:
                for tt in range(NT):
                    pe.wait_ge(x_ready, tt + 1)
                    for half in range(2):
                        for c in range(4):
                            last = pe.transpose(banks[2 * tt + half][:, c * P:(c + 1) * P],
                                                xres[:, tt, (4 * half + c) * P:(4 * half + c + 1) * P],
                                                ident[:])
                        last.then_inc(xt_done, 1)

        @block.scalar
        def _(act):
            for tt in range(NT):
                act.wait_ge(var_ready, tt + 1)
                act.activation(std[:], var[:], ACT.Sqrt).then_inc(std_ready, 1)
            if out is None:
                for n in range(2 * NT):
                    tt, half = n // 2, n % 2
                    act.wait_ge(xt_done, n + 1)
                    act.activation(xT[:, 4 * half:4 * half + 4, tt * P:(tt + 1) * P],
                                   banks[n][:].rearrange("p (c t) -> p c t", c=4), ACT.Copy).then_inc(xt_out, 1)

        @block.vector
        def _(dve):
            own = Chain(dve, dve_step)
            dve.wait_ge(rows_loaded, 32 if b_o is None else 48)
            for tt in range(NT):
                row = r[:, tt % 2]
                if w_o is not None:
                    for dh in range(2):
                        half = slice(dh * 512, (dh + 1) * 512)
                        dve.wait_ge(mix_done, 2 * tt + dh + 1)
                        own.link(dve.scalar_tensor_tensor(out=row[:, half], in0=xres[:, tt, half],
                                                          scalar=ALPHA, in1=banks[2 * tt + dh][:],
                                                          op0=ALU.mult, op1=ALU.add))
                    if b_o is not None:
                        own.link(dve.tensor_tensor(row, row, bo_row[:], ALU.add))
                else:
                    own.link(dve.scalar_tensor_tensor(out=row, in0=xres[:, tt], scalar=ALPHA,
                                                      in1=acc[:, tt], op0=ALU.mult, op1=ALU.add))

                def act_sqrt(var_ins):
                    var_ins.then_inc(var_ready, 1)
                    dve.wait_ge(std_ready, tt + 1)

                norm_tile(dve, own, act_sqrt, row, stats[:], mv[:], var[:], std[:], rstd[:], g_row[:],
                          b_row[:], xres[:, tt]).then_inc(x_ready, 1)


def route(nc, tag, xT, ident, iota_rank, wq_l, keys_l, eiT, ejT, gateT):
    with ExitStack() as ctx:
        def sb(name, shape, dt=F32):
            return ctx.enter_context(nc.sbuf_tensor(name + tag, shape, dt))

        def sem(name):
            return ctx.enter_context(nc.semaphore(name + tag))

        TURNS = PH // 2
        wq = sb("wq", [P, 2, C, P])
        keys = sb("keys", [P, 2, NK])
        qT = sb("qT", [P, 2, T])
        sc = sb("sc", [P, 2, 2, NT, NK])
        came = sb("came", [P, 1])
        rest = sb("rest", [P, 2, NK])
        top = sb("top", [P, 2, NT, 2, K])
        idx = sb("idx", [P, 2, NT, 2, K], U32)
        cand = sb("cand", [P, 2, K, K])
        crest = sb("crest", [P, K * K])
        tops = sb("tops", [P, 2, NT, K])
        poss = sb("poss", [P, 2, NT, K], U32)
        i1 = sb("i1", [P, NT, PH, K])
        i2 = sb("i2", [P, NT, PH, K])
        ts = sb("ts", [P, NT, PH, K])
        pos = sb("pos", [P, NT, PH, K], U32)
        half_u = sb("half_u", [P, PH * K], U32)
        rank = sb("rank", [P, PH, K])
        eq = sb("eq", [P, PH, K, K])
        hit = sb("hit", [P, PH, K, K])
        eij = sb("eij", [P, 2, PH, K])
        gex = sb("gex", [P, PH, K])
        gsum = sb("gsum", [P, PH])
        ginv = sb("ginv", [P, PH])
        pq = [ctx.enter_context(nc.psum_tensor(f"pq{n}{tag}", [P, 512], F32)) for n in range(2)]
        psc = [ctx.enter_context(nc.psum_tensor(f"psc{n}{tag}", [P, 512], F32)) for n in range(4)]
        ptr = ctx.enter_context(nc.psum_tensor("ptr" + tag, [P, 512], F32))
        w_loaded = [sem(f"w_loaded{n}") for n in range(2)]
        q_done, q_out = sem("q_done"), sem("q_out")
        sc_done, sc_out = sem("sc_done"), sem("sc_out")
        top_done, dve_step = sem("top_done"), sem("dve_step")
        gex_in, gex_out = sem("gex_in"), sem("gex_out")
        tr_ready, tr_done, tr_out = sem("tr_ready"), sem("tr_done"), sem("tr_out")
        block = ctx.enter_context(nc.Block())

        @block.sync
        def _(sp):
            with sp.Fori(0, TURNS) as it:
                for b in range(2):
                    sp.wait_ge(sc_done, it * 4 + 2 * b + 2)
                    sp.dma_start(wq[:, b], wq_l[it * 2 + b]).then_inc(w_loaded[b], 16)
                    sp.dma_start(keys[:, b], keys_l[it * 2 + b]).then_inc(w_loaded[b], 16)

        @block.tensor
        def _(pe):
            pe.sem_inc(sc_done, 4)
            with pe.Fori(0, TURNS) as it:
                for b in range(2):
                    pe.wait_ge(w_loaded[b], it * 32 + 32)
                    pe.wait_ge(q_out, it * 2 + b + 1)
                    for c in range(C):
                        last = pe.matmul(pq[b][:], wq[:, b, c], xT[:, c, :], start=(c == 0),
                                         stop=(c == C - 1))
                    last.then_inc(q_done, 1)
                    pe.wait_ge(q_out, it * 2 + b + 3)
                    pe.wait_ge(sc_out, it * 4 + 2 * b + 2)
                    for half in range(2):
                        rows = slice(half * 64, half * 64 + 64)
                        for tt in range(NT):
                            last = pe.matmul(psc[2 * b + half][:, tt * NK:(tt + 1) * NK],
                                             qT[rows, b, tt * P:(tt + 1) * P], keys[rows, b],
                                             start=True, stop=True)
                        last.then_inc(sc_done, 1)
            for tt in range(NT):
                pe.wait_ge(tr_ready, tt + 1)
                if tt:
                    pe.wait_ge(tr_out, 3 * tt)
                for n, src in enumerate((eij[:, 0], eij[:, 1], gex[:])):
                    last = pe.transpose(ptr[:, n * P:(n + 1) * P], src.rearrange("p a b -> p (a b)"), ident[:])
                last.then_inc(tr_done, 1)

        @block.scalar
        def _(act):
            act.sem_inc(q_out, 2)
            act.sem_inc(sc_out, 4)
            with act.Fori(0, TURNS) as it:
                for b in range(2):
                    act.wait_ge(q_done, it * 2 + b + 1)
                    act.wait_ge(sc_done, it * 4 + 2 * b + 4 - 2)
                    act.activation(qT[:, b], pq[b][:], ACT.Copy).then_inc(q_out, 1)
                    act.wait_ge(top_done, it * 2 + b + 1)
                    for half in range(2):
                        act.wait_ge(sc_done, it * 4 + 2 * b + half + 5)
                        act.activation(sc[:, b, half].rearrange("p a b -> p (a b)"), psc[2 * b + half][:],
                                       ACT.Copy).then_inc(sc_out, 1)
            for tt in range(NT):
                act.wait_ge(gex_in, tt + 1)
                act.activation(gex[:], gex[:], ACT.Exp).then_inc(gex_out, 1)
                act.wait_ge(tr_done, tt + 1)
                for n, dst in enumerate((eiT, ejT, gateT)):
                    act.activation(dst[:, tt * P:(tt + 1) * P], ptr[:, n * P:(n + 1) * P], ACT.Copy
                                   ).then_inc(tr_out, 1)

        @block.vector
        def _(dve):
            own = Chain(dve, dve_step)
            dve.sem_inc(top_done, 2)

            def top16(values, out_top, out_idx, scratch):
                own.link(dve.max(out_top[:, 0:8], values))
                dve.max_index(out_idx[:, 0:8], out_top[:, 0:8], values)
                own.link(dve.match_replace(scratch, out_top[:, 0:8], values, -3.0e38))
                own.link(dve.max(out_top[:, 8:16], scratch))
                own.link(dve.max_index(out_idx[:, 8:16], out_top[:, 8:16], scratch))

            with dve.Fori(0, TURNS) as it:
                for b in range(2):
                    dve.sem_clear(dve_step)
                    own.n = 0
                    dve.wait_ge(sc_out, it * 4 + 2 * b + 6)
                    own.link(dve.tensor_copy(came[:], sc[:, b, 1, 0, 0:1]))
                    for tt in range(NT):
                        for half in range(2):
                            top16(sc[:, b, half, tt], top[:, b, tt, half], idx[:, b, tt, half], rest[:, half])
                        own.link(dve.tensor_tensor(
                            cand[:, 0], top[:, b, tt, 0].unsqueeze(2).broadcast_to([P, K, K]),
                            top[:, b, tt, 1].unsqueeze(1).broadcast_to([P, K, K]), ALU.add))
                        top16(cand[:, 0].rearrange("p a b -> p (a b)"), tops[:, b, tt], poss[:, b, tt], crest[:])
                    head = it * 2 + b
                    dve.tensor_copy(i1[:, :, head, :], idx[:, b, :, 0])
                    dve.tensor_copy(i2[:, :, head, :], idx[:, b, :, 1])
                    dve.tensor_copy(ts[:, :, head, :], tops[:, b])
                    dve.tensor_copy(pos[:, :, head, :], poss[:, b]).then_inc(top_done, 1)
            dve.wait_ge(top_done, 2 + PH)
            dve.sem_clear(dve_step)
            own.n = 0
            for tt in range(NT):
                if tt:
                    dve.wait_ge(tr_done, tt)
                for side, (op, arg, ids) in enumerate(((ALU.logical_shift_right, 4, i1),
                                                       (ALU.bitwise_and, K - 1, i2))):
                    own.link(dve.tensor_scalar(half_u[:], pos[:, tt].rearrange("p a b -> p (a b)"), arg, None, op))
                    own.link(dve.tensor_copy(rank[:].rearrange("p a b -> p (a b)"), half_u[:]))
                    own.link(dve.tensor_tensor(
                        eq[:].rearrange("p h k a -> p (h k) a"),
                        rank[:].rearrange("p h k -> p (h k)").unsqueeze(2).broadcast_to([P, PH * K, K]),
                        iota_rank[:].unsqueeze(1).broadcast_to([P, PH * K, K]), ALU.is_equal))
                    own.link(dve.tensor_tensor(hit[:], eq[:], ids[:, tt].unsqueeze(2).broadcast_to([P, PH, K, K]),
                                               ALU.mult))
                    own.link(dve.tensor_reduce(eij[:, side], hit[:], AX.X, ALU.add))
                dve.tensor_tensor(gex[:], ts[:, tt], ts[:, tt, :, 0:1].broadcast_to([P, PH, K]),
                                  ALU.subtract).then_inc(gex_in, 1)
                dve.wait_ge(gex_out, tt + 1)
                own.link(dve.tensor_reduce(gsum[:], gex[:], AX.X, ALU.add))
                own.link(dve.reciprocal(ginv[:], gsum[:]))
                dve.tensor_tensor(gex[:], gex[:], ginv[:].unsqueeze(2).broadcast_to([P, PH, K]), ALU.mult
                                  ).then_inc(tr_ready, 1)


def spread_gates(nc, tag, iota_keys, eiT, ejT, gateT, g_dram):
    SUB = 8
    STEPS = TG // SUB
    TURNS = T // TG // 2
    with ExitStack() as ctx:
        def sb(name, shape, dt=F32):
            return ctx.enter_context(nc.sbuf_tensor(name + tag, shape, dt))

        def sem(name):
            return ctx.enter_context(nc.semaphore(name + tag))

        left = sb("left", [P, 2, SUB, NK])
        right = sb("right", [P, 2, SUB, NK])
        stage = sb("stage", [P, 2, NK, TG])
        banks = [ctx.enter_context(nc.psum_tensor(f"gbank{n}{tag}", [P, 4, NK], F32)) for n in range(4)]
        left_ready, right_ready = sem("left_ready"), sem("right_ready")
        g_done, g_out = sem("g_done"), sem("g_out")
        g_stored = [sem(f"g_stored{n}") for n in range(2)]
        block = ctx.enter_context(nc.Block())
        N = 2 * STEPS

        @block.sync
        def _(sp):
            for b in range(2):
                sp.sem_inc(g_stored[b], 16)
            with sp.Fori(0, TURNS) as it:
                for b in range(2):
                    sp.wait_ge(g_out, it * 2 * N + (b + 1) * N + 4)
                    sp.dma_start(g_dram[it * 2 + b], stage[:, b]).then_inc(g_stored[b], 16)
            for b in range(2):
                sp.wait_ge(g_stored[b], 16 * (TURNS + 1))

        @block.vector
        def _(dve):
            with dve.Fori(0, TURNS) as it:
                for s in range(N):
                    t0 = it * (2 * TG) + s * SUB
                    iota = iota_keys[:].unsqueeze(1).broadcast_to([P, SUB, NK])
                    dve.wait_ge(g_done, it * N + s + 1)
                    dve.tensor_tensor(left[:, s % 2], iota,
                                      eiT[:, bass.ds(t0, SUB)].unsqueeze(2).broadcast_to([P, SUB, NK]),
                                      ALU.is_equal).then_inc(left_ready, 1)
                    for n in range(SUB):
                        ins = dve.tensor_scalar(right[:, s % 2, n], iota_keys[:], ejT[:, bass.ds(t0 + n, 1)],
                                                gateT[:, bass.ds(t0 + n, 1)], ALU.is_equal, ALU.mult)
                    ins.then_inc(right_ready, 1)

        @block.tensor
        def _(pe):
            pe.sem_inc(g_done, 2)
            with pe.Fori(0, TURNS) as it:
                for s in range(N):
                    pe.wait_ge(left_ready, it * N + s + 1)
                    pe.wait_ge(right_ready, it * N + s + 1)
                    pe.wait_ge(g_out, it * 2 * N + 2 * s + 2)
                    for n in range(SUB):
                        last = pe.matmul(banks[2 * (s % 2) + n // 4][:, n % 4], left[:, s % 2, n],
                                         right[:, s % 2, n], start=True, stop=True)
                    last.then_inc(g_done, 1)

        @block.scalar
        def _(act):
            act.sem_inc(g_out, 4)
            with act.Fori(0, TURNS) as it:
                for s in range(N):
                    b = s // STEPS
                    act.wait_ge(g_done, it * N + s + 3)
                    if s % STEPS == 0:
                        act.wait_ge(g_stored[b], it * 16 + 16)
                    for q in range(2):
                        t0 = (s % STEPS) * SUB + 4 * q
                        act.activation(stage[:, b, :, t0:t0 + 4], banks[2 * (s % 2) + q][:].rearrange("p t j -> p j t"),
                                       ACT.Copy).then_inc(g_out, 1)


def clear_semaphores(nc):
    free = sorted(nc.free_semaphores)
    assert free == list(range(free[0], free[-1] + 1))
    with nc.Block() as block:
        @block.gpsimd
        def _(pool):
            pool.sem_clear(range(free[0], free[-1] + 1))


def trunk(nc, a, out):
    g_dram = nc.dram_tensor("g_dram", [T // TG, P, NK, TG], F32, kind="Internal").ap()
    with ExitStack() as ctx:
        def sb(name, shape, dt=F32):
            return ctx.enter_context(nc.sbuf_tensor(name, shape, dt))

        xres = sb("xres", [P, NT, D])
        xT = sb("xT", [P, C, T])
        ident, masks, iota_keys, iota_rank = constants(nc, ctx)
        load_tokens(nc, a["x"], a["x_t"], xres, xT)
        for layer in range(DEPTH):
            tag = f"_{layer}"
            if layer:
                clear_semaphores(nc)
            with nc.sbuf_tensor("oT" + tag, [P, C, T], F32) as oT:
                if layer % 2 == 0:
                    diff_attention(nc, xT, a["da_w"], a["cos_t"], a["sin_t"], a["da_lambda"], a["da_subln_g"],
                                   masks, ident, oT)
                    w_o, b_o = a["da_w_o"], None
                else:
                    window_attention(nc, xT, a["sw_w"], a["cos_t"], a["sin_t"], a["sw_b"], a["sw_bv"],
                                     a["sw_sinks"], masks, ident, oT)
                    w_o, b_o = a["sw_w_o"], a["sw_b_o"]
                add_and_norm(nc, "_m" + tag, xres, xT, ident, a["ln1_g"][layer], a["ln1_b"][layer], oT=oT,
                             w_o=w_o, b_o=b_o)
            with ExitStack() as routed:
                eiT, ejT, gateT = (routed.enter_context(nc.sbuf_tensor(n + tag, [P, T], F32))
                                   for n in ("eiT", "ejT", "gateT"))
                route(nc, tag, xT, ident, iota_rank, a["pk_wq"][layer], a["pk_keys"][layer], eiT, ejT, gateT)
                spread_gates(nc, tag, iota_keys, eiT, ejT, gateT, g_dram)
            with nc.sbuf_tensor("acc" + tag, [P, NT, D], F32) as acc:
                dense(nc, xT, a["pk_u"][layer], a["pk_v"][layer], g_dram, acc, tag)
                last = layer == DEPTH - 1
                add_and_norm(nc, "_p" + tag, xres, xT, ident, a["ln2_g"][layer], a["ln2_b"][layer], acc=acc,
                             out=out if last else None)


def lay_out(np, x, da_w_qkv, da_lambda, da_subln_g, da_w_o, sw_w_qkv, sw_b_qkv, sw_sinks, sw_w_o, sw_b_o,
            pk_w_query, pk_sub_keys, pk_u, pk_v, ln1_g, ln1_b, ln2_g, ln2_b):
    def tiled(w):
        return w.reshape(*w.shape[:-2], C, P, w.shape[-1]).swapaxes(-3, -2)

    a = {"x": x[0], "x_t": tiled(x[0].T)}
    inv = (1.0 / (10000.0 ** (np.arange(0, HD, 2, dtype=np.float32) / np.float32(HD)))).astype(np.float32)
    ang = np.arange(T, dtype=np.float32)[:, None] * inv[None, :]
    a["cos_t"] = np.tile(np.cos(ang).T, (4, 1)).astype(np.float32)
    a["sin_t"] = np.tile(np.sin(ang).T, (4, 1)).astype(np.float32)

    w = da_w_qkv[0]
    turns = []
    for it in range(4):
        cols = []
        for part in range(2):
            for half in range(2):
                cols += [part * D + (4 * it + m) * HD + half * 32 + r for m in range(4) for r in range(32)]
        cols += list(range(2 * D + it * 2 * P, 2 * D + (it + 1) * 2 * P))
        turns.append(tiled(w[:, cols]))
    a["da_w"] = np.stack(turns)
    a["da_lambda"] = da_lambda[0]
    a["da_subln_g"] = da_subln_g[0]
    a["da_w_o"] = da_w_o[0]

    w, b = sw_w_qkv[0], sw_b_qkv[0]
    turns, bias = [], []
    for it in range(2):
        cols = []
        for four in range(2):
            for half in range(2):
                cols += [(8 * it + 4 * four + m) * HD + half * 32 + r for m in range(4) for r in range(32)]
        for half in range(2):
            cols += [16 * HD + it * HD + half * 32 + r for m in range(4) for r in range(32)]
        vcols = list(range(18 * HD + it * HD, 18 * HD + (it + 1) * HD))
        turns.append(tiled(w[:, cols + vcols]))
        bias.append(b[cols].reshape(6, P).T)
    a["sw_w"] = np.stack(turns)
    a["sw_b"] = np.stack(bias, axis=1)
    a["sw_bv"] = b[18 * HD:]
    a["sw_sinks"] = sw_sinks[0]
    a["sw_w_o"] = sw_w_o[0]
    a["sw_b_o"] = sw_b_o[0]

    a["pk_wq"] = tiled(pk_w_query).reshape(DEPTH, P, C, PH, P).transpose(0, 3, 1, 2, 4)
    a["pk_keys"] = pk_sub_keys.transpose(0, 1, 2, 4, 3).reshape(DEPTH, PH, P, NK)
    a["pk_u"] = pk_u.reshape(DEPTH, P, GROUPS, JG, C, P).transpose(0, 2, 5, 3, 4, 1).reshape(
        DEPTH, GROUPS, P, JG, C * P)
    a["pk_v"] = pk_v.reshape(DEPTH, P, GROUPS, JG, D).transpose(0, 2, 1, 3, 4)
    a["ln1_g"], a["ln1_b"], a["ln2_g"], a["ln2_b"] = ln1_g, ln1_b, ln2_g, ln2_b
    return a


def kernel(**inputs):
    import concourse.bacc as bacc
    import numpy as np
    from concourse.bass_utils import run_bass_kernel_spmd

    nc = bacc.Bacc("TRN2", target_bir_lowering=False, num_devices=1)
    laid = lay_out(np, **{k: np.asarray(v) for k, v in inputs.items()})
    arrays, aps = {}, {}
    for name, v in laid.items():
        v = np.ascontiguousarray(v)
        arrays[f"in_{name}"] = v
        aps[name] = nc.dram_tensor(f"in_{name}", v.shape, mybir.dt.from_np(v.dtype), kind="ExternalInput").ap()
    out = nc.dram_tensor("out", [T, D], F32, kind="ExternalOutput").ap()
    trunk(nc, aps, out)
    r = run_bass_kernel_spmd(nc, [arrays], core_ids=[0])
    return r.results[0]["out"].reshape(1, T, D)
```

```python
import math
from contextlib import ExitStack

import concourse.bass as bass
from concourse import mybir

ALU = mybir.AluOpType
ACT = mybir.ActivationFunctionType
AX = mybir.AxisListType
F32 = mybir.dt.float32
F32R = mybir.dt.float32r
U32 = mybir.dt.uint32

P = 128
T = 512
NT = T // P
D = 1024
C = D // P
DEPTH = 2
ALPHA = (2 * DEPTH) ** 0.25
EPS = 1e-5
HD = 64
SCALE = HD ** -0.5
NEG = -1e30
LAMBDA_INIT = 0.8 - 0.6 * math.exp(0.0)

PH = 8
NK = 128
K = 16
TG = 64
JG = 2
GROUPS = NK // JG


def dense(nc, xh, xl, u_l, v_l, g_dram, acc, tag):
    with ExitStack() as ctx:
        def sb(name, shape, dt):
            return ctx.enter_context(nc.sbuf_tensor(name + tag, shape, dt))

        def sem(name):
            return ctx.enter_context(nc.semaphore(name + tag))

        ur = sb("ur", [P, 2, JG, C * P], F32)
        uh = sb("uh", [P, JG, C, P], F32R)
        ul = sb("ul", [P, JG, C, P], F32R)
        vr = sb("vr", [P, 2, JG, D], F32)
        vh = sb("vh", [P, 2, JG, D], F32R)
        vl = sb("vl", [P, 2, JG, D], F32R)
        gt = sb("gt", [P, 2, T // TG, JG, TG], F32)
        act_h = sb("act_h", [P, 2, T], F32)
        wf = sb("wf", [P, 2, T], F32)
        wh = sb("wh", [P, 2, JG, T], F32R)
        wl = sb("wl", [P, 2, JG, T], F32R)
        ph = [ctx.enter_context(nc.psum_tensor(f"ph{n}{tag}", [P, T], F32)) for n in range(2)]
        pv = [ctx.enter_context(nc.psum_tensor(f"pv{n}{tag}", [P, T], F32)) for n in range(4)]

        u_loaded = [sem(f"u_loaded{n}") for n in range(2)]
        v_loaded = [sem(f"v_loaded{n}") for n in range(2)]
        g_loaded = [sem(f"g_loaded{n}") for n in range(2)]
        uh_ready = sem("uh_ready")
        ul_ready = sem("ul_ready")
        vh_ready = sem("vh_ready")
        vl_ready = sem("vl_ready")
        h_done = sem("h_done")
        gelu_done = sem("gelu_done")
        wf_ready = sem("wf_ready")
        wh_ready = sem("wh_ready")
        wl_ready = sem("wl_ready")
        v_done = sem("v_done")
        acc_done = sem("acc_done")
        acc_zero = sem("acc_zero")
        block = ctx.enter_context(nc.Block())

        def pairs(eng, step, first, last):
            for g in range(2):
                step(g, g % 2, g + 1 < GROUPS)
            with eng.Fori(1, GROUPS // 2 - 1) as i:
                for b in range(2):
                    step(i * 2 + b, b, True)
            for g in range(GROUPS - 2, GROUPS):
                step(g, g % 2, g + 1 < GROUPS)

        @block.sync
        def _(sp):
            def load(g, b, more):
                peeled = isinstance(g, int) and g < 2
                if not peeled:
                    sp.wait_ge(ul_ready, (g - 1) * JG)
                    sp.wait_ge(uh_ready, (g - 1) * JG)
                sp.dma_start(ur[:, b], u_l[g]).then_inc(u_loaded[b], 16)
                if not peeled:
                    sp.wait_ge(wf_ready, (g - 1) * JG)
                sp.dma_start(gt[:, b], g_dram[:, :, bass.ds(g * JG, JG), :].rearrange("g i j t -> i g j t")
                             ).then_inc(g_loaded[b], 16)
                if not peeled:
                    sp.wait_ge(vl_ready, (g - 1) * JG)
                    sp.wait_ge(vh_ready, (g - 1) * JG)
                sp.dma_start(vr[:, b], v_l[g]).then_inc(v_loaded[b], 16)
            pairs(sp, load, None, None)

        def count16(g, b):
            if isinstance(g, int):
                return 16 * (g // 2 + 1)
            return (g - b) * 8 + 16

        @block.tensor
        def _(pe):
            def hidden(g, b):
                for jj in range(JG):
                    pe.wait_ge(uh_ready, g * JG + jj + 1)
                    pe.wait_ge(ul_ready, g * JG + jj + 1)
                    if not (isinstance(g, int) and g == 0):
                        pe.wait_ge(gelu_done, g * JG + jj - 1)
                    for c in range(C):
                        pe.matmul(ph[jj][:], uh[:, jj, c, :], xh[:, c, :], start=(c == 0), stop=False)
                        pe.matmul(ph[jj][:], uh[:, jj, c, :], xl[:, c, :], start=False, stop=False)
                        last = pe.matmul(ph[jj][:], ul[:, jj, c, :], xh[:, c, :], start=False,
                                         stop=(c == C - 1))
                    last.then_inc(h_done, 1)

            def output(g, b):
                pe.wait_ge(vh_ready, (g + 1) * JG)
                pe.wait_ge(vl_ready, (g + 1) * JG)
                pe.wait_ge(wh_ready, (g + 1) * JG)
                pe.wait_ge(wl_ready, (g + 1) * JG)
                for n in range(2 * NT):
                    tt, dh = n // 2, n % 2
                    if not (isinstance(g, int) and g == 0 and n < 4):
                        pe.wait_ge(acc_done, g * 8 + n - 3)
                    for jj in range(JG):
                        w_hi = wh[:, b, jj, tt * P:(tt + 1) * P]
                        w_lo = wl[:, b, jj, tt * P:(tt + 1) * P]
                        v_hi = vh[:, b, jj, dh * 512:(dh + 1) * 512]
                        v_lo = vl[:, b, jj, dh * 512:(dh + 1) * 512]
                        pe.matmul(pv[n % 4][:], w_hi, v_hi, start=(jj == 0), stop=False)
                        pe.matmul(pv[n % 4][:], w_hi, v_lo, start=False, stop=False)
                        last = pe.matmul(pv[n % 4][:], w_lo, v_hi, start=False, stop=(jj == JG - 1))
                    last.then_inc(v_done, 1)

            hidden(0, 0)
            hidden(1, 1)
            output(0, 0)
            with pe.Fori(1, GROUPS // 2) as i:
                hidden(i * 2, 0)
                output(i * 2 - 1, 1)
                hidden(i * 2 + 1, 1)
                output(i * 2, 0)
            output(GROUPS - 1, 1)

        @block.scalar
        def _(act):
            def split_u(g, b, jj):
                act.wait_ge(u_loaded[b], count16(g, b))
                if not (isinstance(g, int) and g == 0):
                    act.wait_ge(h_done, (g - 1) * JG + jj + 1)
                act.activation(uh[:, jj].rearrange("p c n -> p (c n)"), ur[:, b, jj], ACT.Copy
                               ).then_inc(uh_ready, 1)

            for jj in range(JG):
                split_u(0, 0, jj)

            def step(g, b, more):
                for jj in range(JG):
                    if jj == 0:
                        act.wait_ge(v_loaded[b], count16(g, b))
                        if not (isinstance(g, int) and g < 2):
                            act.wait_ge(v_done, (g - 1) * 8)
                    act.activation(vh[:, b, jj], vr[:, b, jj], ACT.Copy).then_inc(vh_ready, 1)
                    act.wait_ge(h_done, g * JG + jj + 1)
                    if not (isinstance(g, int) and g == 0):
                        act.wait_ge(wf_ready, g * JG + jj - 1)
                    act.activation(act_h[:, jj], ph[jj][:], ACT.Gelu).then_inc(gelu_done, 1)
                    if more:
                        split_u(g + 1, 1 - b, jj)
                    act.wait_ge(wf_ready, g * JG + jj + 1)
                    act.activation(wh[:, b, jj], wf[:, jj], ACT.Copy).then_inc(wh_ready, 1)
            pairs(act, step, None, None)

        @block.vector
        def _(dve):
            dve.memset(acc[:], 0.0).then_inc(acc_zero, 1)
            dve.wait_ge(acc_zero, 1)

            def split_u(g, b, jj):
                dve.wait_ge(uh_ready, g * JG + jj + 1)
                if not (isinstance(g, int) and g == 0):
                    dve.wait_ge(h_done, (g - 1) * JG + jj + 1)
                dve.tensor_tensor(ul[:, jj].rearrange("p c n -> p (c n)"), ur[:, b, jj],
                                  uh[:, jj].rearrange("p c n -> p (c n)").bitcast(F32),
                                  ALU.subtract).then_inc(ul_ready, 1)

            for jj in range(JG):
                split_u(0, 0, jj)

            def add_sums(g):
                for n in range(2 * NT):
                    tt, dh = n // 2, n % 2
                    part = acc[:, tt, dh * 512:(dh + 1) * 512]
                    dve.wait_ge(v_done, g * 8 + n + 1)
                    if not (isinstance(g, int) and g == 0):
                        dve.wait_ge(acc_done, g * 8 + n - 7)
                    dve.tensor_tensor(part, pv[n % 4][:], part, ALU.add).then_inc(acc_done, 1)

            def step(g, b, more):
                for jj in range(JG):
                    dve.wait_ge(vh_ready, g * JG + jj + 1)
                    dve.tensor_tensor(vl[:, b, jj], vr[:, b, jj], vh[:, b, jj].bitcast(F32),
                                      ALU.subtract).then_inc(vl_ready, 1)
                    dve.wait_ge(gelu_done, g * JG + jj + 1)
                    if jj == 0:
                        dve.wait_ge(g_loaded[b], count16(g, b))
                    if not (isinstance(g, int) and g == 0):
                        dve.wait_ge(wh_ready, g * JG + jj - 1)
                        dve.wait_ge(wl_ready, g * JG + jj - 1)
                    dve.tensor_tensor(wf[:, jj].rearrange("p (g t) -> p g t", t=TG),
                                      act_h[:, jj].rearrange("p (g t) -> p g t", t=TG),
                                      gt[:, b, :, jj, :], ALU.mult).then_inc(wf_ready, 1)
                    if more:
                        split_u(g + 1, 1 - b, jj)
                    dve.wait_ge(wh_ready, g * JG + jj + 1)
                    dve.tensor_tensor(wl[:, b, jj], wf[:, jj], wh[:, b, jj].bitcast(F32),
                                      ALU.subtract).then_inc(wl_ready, 1)
                if not (isinstance(g, int) and g == 0):
                    add_sums(g - 1)
            pairs(dve, step, None, None)
            add_sums(GROUPS - 1)


def constants(nc, ctx):
    def sb(name, shape):
        return ctx.enter_context(nc.sbuf_tensor(name, shape, F32))

    ident = sb("ident", [P, P])
    masks = sb("masks", [P, 2, P])
    iota_keys = sb("iota_keys", [P, NK])
    iota_rank = sb("iota_rank", [P, K])
    with ExitStack() as inner:
        cleared = inner.enter_context(nc.semaphore("cleared"))
        block = inner.enter_context(nc.Block())

        @block.gpsimd
        def _(pool):
            pool.memset(ident[:], 0.0).then_inc(cleared, 1)
            pool.memset(masks[:], 0.0).then_inc(cleared, 1)
            pool.iota(iota_keys[:], pattern=[[1, NK]], base=0, channel_multiplier=0,
                      allow_small_or_imprecise_dtypes=True).then_inc(cleared, 1)
            pool.iota(iota_rank[:], pattern=[[1, K]], base=0, channel_multiplier=0,
                      allow_small_or_imprecise_dtypes=True).then_inc(cleared, 1)
            pool.wait_ge(cleared, 4)
            pool.affine_select(out=ident[:], in_=ident[:], compare_op=ALU.not_equal, fill=1.0, base=0,
                               pattern=[[-1, P]], channel_multiplier=1).then_inc(cleared, 1)
            pool.affine_select(out=masks[:, 0], in_=masks[:, 0], compare_op=ALU.is_ge, fill=NEG, base=-1,
                               pattern=[[1, P]], channel_multiplier=-1).then_inc(cleared, 1)
            pool.affine_select(out=masks[:, 1], in_=masks[:, 1], compare_op=ALU.is_ge, fill=NEG, base=0,
                               pattern=[[-1, P]], channel_multiplier=1).then_inc(cleared, 1)
            pool.wait_ge(cleared, 7)
    return ident, masks, iota_keys, iota_rank


def load_tokens(nc, x, x_t, xres, xh, xl):
    with ExitStack() as ctx:
        raw = ctx.enter_context(nc.sbuf_tensor("x_raw", [P, C, T], F32))
        xt_loaded, x_loaded = ctx.enter_context(nc.semaphore("xt_loaded")), ctx.enter_context(nc.semaphore("x_loaded"))
        xh_ready, xl_ready = ctx.enter_context(nc.semaphore("xh_ready")), ctx.enter_context(nc.semaphore("xl_ready"))
        block = ctx.enter_context(nc.Block())

        @block.sync
        def _(sp):
            sp.dma_start(raw[:], x_t).then_inc(xt_loaded, 16)
            sp.dma_start(xres[:], x.rearrange("(n p) d -> p n d", p=P)).then_inc(x_loaded, 16)
            sp.wait_ge(x_loaded, 16)

        @block.scalar
        def _(act):
            act.wait_ge(xt_loaded, 16)
            for c in range(C):
                act.activation(xh[:, c], raw[:, c], ACT.Copy).then_inc(xh_ready, 1)

        @block.vector
        def _(dve):
            for c in range(C):
                dve.wait_ge(xh_ready, c + 1)
                dve.tensor_tensor(xl[:, c], raw[:, c], xh[:, c].bitcast(F32), ALU.subtract).then_inc(xl_ready, 1)
            dve.wait_ge(xl_ready, C)


class Chain:

    def __init__(self, eng, s, per=0):
        self.eng, self.s, self.n, self.base, self.per = eng, s, 0, 0, per

    def mark(self, ins):
        self.n += 1
        ins.then_inc(self.s, 1)
        return self.n

    def wait(self, n):
        self.eng.wait_ge(self.s, self.base + n)

    def link(self, ins):
        self.wait(self.mark(ins))

    def turn(self, i):
        self.base, self.n = i * self.per, 0

    def turned(self):
        assert self.n == self.per, self.n


def rope(dve, dve_own, a, b, cos, sin, out_a, out_b, tmp):
    dve.tensor_tensor(tmp[:, 0], b, sin, ALU.mult)
    dve.tensor_tensor(tmp[:, 1], a, sin, ALU.mult)
    dve.tensor_tensor(tmp[:, 2], b, cos, ALU.mult)
    dve_own.link(dve.tensor_tensor(tmp[:, 3], a, cos, ALU.mult))
    dve.tensor_tensor(out_a, tmp[:, 3], tmp[:, 0], ALU.subtract)
    return dve.tensor_tensor(out_b, tmp[:, 2], tmp[:, 1], ALU.add)


def diff_attention(nc, xh, xl, w_l, cos_t, sin_t, lam, subln, masks, ident, oh, ol):
    TURNS = 4
    CHUNKS = 6
    RING = 3
    PROJ_AT = {1: 2, 3: 3, 5: 4, 6: 5}
    SPLIT_AT = {0: (2,), 2: (3,), 4: (4, 5)}
    SPLIT_ON = {5: 0, 7: 1}
    with ExitStack() as ctx:
        def sb(name, shape, dt=F32):
            return ctx.enter_context(nc.sbuf_tensor("da_" + name, shape, dt))

        def sem(name):
            return ctx.enter_context(nc.semaphore("da_" + name))

        w = sb("w", [P, RING, C, P])
        wh = sb("wh", [P, C, CHUNKS * P], F32R)
        wl = sb("wl", [P, C, CHUNKS * P], F32R)
        cos, sin = sb("cos", [P, T]), sb("sin", [P, T])
        raw = sb("raw", [P, 4, T])
        rot = sb("rot", [P, 4, T])
        v_next = sb("v_next", [P, NT, 2 * P])
        v = sb("v", [P, NT, 2 * P])
        E = sb("E", [P, 2, 2, T])
        A = sb("A", [P, 2, T])
        AT = sb("AT", [P, 2, NT, P])
        o = sb("o", [P, 8, P])
        sq = sb("sq", [P, P])
        ss = sb("ss", [P, 8])
        rms = sb("rms", [P, 8])
        rstd = sb("rstd", [P, 8])
        nmax = sb("nmax", [P, 2, 2])
        rsum = sb("rsum", [P, 2, 2])
        rinv = sb("rinv", [P, 2, 2])
        lam_row = sb("lam_row", [P, 4, HD])
        lam_prod = sb("lam_prod", [P, 2, HD])
        lam_sum = sb("lam_sum", [P, 2])
        lam_exp = sb("lam_exp", [P, 2])
        neg_lam = sb("neg_lam", [P, 1])
        g_row = sb("g_row", [P, P])
        ps = [ctx.enter_context(nc.psum_tensor(f"da_ps{n}", [P, 2, 512], F32)) for n in range(2)]
        pp = [ctx.enter_context(nc.psum_tensor(f"da_pp{n}", [P, 512], F32)) for n in range(2)]
        pt = ctx.enter_context(nc.psum_tensor("da_pt", [P, 512], F32))
        po = ctx.enter_context(nc.psum_tensor("da_po", [P, 512], F32))

        consts_loaded = sem("consts_loaded")
        w_loaded = [sem(f"w_loaded{n}") for n in range(RING)]
        wh_ready, wl_ready = sem("wh_ready"), sem("wl_ready")
        proj_done, ot_done, oh_ready = sem("proj_done"), sem("ot_done"), sem("oh_ready")
        bank_free = [sem(f"bank_free{n}") for n in range(2)]
        rot_ready, v_ready = sem("rot_ready"), sem("v_ready")
        score_done, nmax_ready, exp_done = sem("score_done"), sem("nmax_ready"), sem("exp_done")
        a_ready, at_done, at_out = sem("a_ready"), sem("at_done"), sem("at_out")
        pv_done, o_out = sem("pv_done"), sem("o_out")
        ms_ready, rms_ready, on_ready = sem("ms_ready"), sem("rms_ready"), sem("on_ready")
        lam_ready, lam_exped, dve_step = sem("lam_ready"), sem("lam_exped"), sem("dve_step")
        block = ctx.enter_context(nc.Block())
        units = [(hl, qb) for hl in range(2) for qb in range(NT)]

        def turns(eng, turn):
            with eng.Fori(0, TURNS - 2) as it:
                turn(it, True, True)
            turn(TURNS - 2, True, False)
            turn(TURNS - 1, False, False)

        @block.sync
        def _(sp):
            def load(t, n):
                if isinstance(t, int) and t == 0:
                    if n >= RING:
                        sp.wait_ge(wl_ready, n - RING + 1)
                else:
                    sp.wait_ge(wl_ready, t * CHUNKS + n - RING + 1)
                sp.dma_start(w[:, n % RING], w_l[t, n]).then_inc(w_loaded[n % RING], 16)

            for n in range(CHUNKS):
                load(0, n)
            sp.dma_start(cos[:], cos_t).then_inc(consts_loaded, 16)
            sp.dma_start(sin[:], sin_t).then_inc(consts_loaded, 16)
            sp.dma_start(lam_row[:], lam.partition_broadcast(P)).then_inc(consts_loaded, 16)
            sp.dma_start(g_row[:], subln.partition_broadcast(P)).then_inc(consts_loaded, 16)
            with sp.Fori(1, TURNS) as t:
                for n in range(CHUNKS):
                    load(t, n)

        @block.gpsimd
        def _(pool):
            def split(t, n):
                pool.wait_ge(wh_ready, t * CHUNKS + n + 1)
                if not (isinstance(t, int) and t == 0):
                    pool.wait_ge(proj_done, (t - 1) * CHUNKS + (n + 1 if n < 4 else 6))
                cols = slice(n * P, (n + 1) * P)
                pool.tensor_tensor(wl[:, :, cols], w[:, n % RING], wh[:, :, cols].bitcast(F32), ALU.subtract
                                   ).then_inc(wl_ready, 1)

            def turn(it, more, more2):
                for b in range(2):
                    pool.wait_ge(bank_free[b], it * 4 + 3)
                if not (isinstance(it, int) and it == 0):
                    pool.wait_ge(pv_done, it * 8)
                pool.tensor_copy(v[:], v_next[:]).then_inc(v_ready, 1)
                for u in range(8):
                    for n in SPLIT_AT.get(u, ()) if more else ():
                        split(it + 1, n)
                    if u in SPLIT_ON and more2:
                        split(it + 2, SPLIT_ON[u])

            for n in range(CHUNKS):
                split(0, n)
            for n in range(2):
                split(1, n)
            turn(0, True, True)
            with pool.Fori(1, TURNS - 2) as it:
                turn(it, True, True)
            turn(TURNS - 2, True, False)
            turn(TURNS - 1, False, False)

        @block.tensor
        def _(pe):
            def project(t, n, prior):
                dst = pp[n % 2]
                if not (isinstance(prior, int) and prior == 0):
                    pe.wait_ge(bank_free[n % 2], prior)
                pe.wait_ge(wl_ready, t * CHUNKS + (n + 1 if n < 4 else 6))
                if n < 4:
                    cols = slice(n * P, (n + 1) * P)
                    for c in range(C):
                        pe.matmul(dst[:], wh[:, c, cols], xh[:, c, :], start=(c == 0), stop=False)
                        pe.matmul(dst[:], wh[:, c, cols], xl[:, c, :], start=False, stop=False)
                        last = pe.matmul(dst[:], wl[:, c, cols], xh[:, c, :], start=False, stop=(c == C - 1))
                else:
                    for half in range(2):
                        tok = slice((2 * (n - 4) + half) * P, (2 * (n - 4) + half + 1) * P)
                        part = dst[:, half * 2 * P:(half + 1) * 2 * P]
                        for c in range(C):
                            pe.matmul(part, xh[:, c, tok], wh[:, c, 4 * P:], start=(c == 0), stop=False)
                            pe.matmul(part, xh[:, c, tok], wl[:, c, 4 * P:], start=False, stop=False)
                            last = pe.matmul(part, xl[:, c, tok], wh[:, c, 4 * P:], start=False,
                                             stop=(c == C - 1))
                last.then_inc(proj_done, 1)

            def turn(it, more, more2):
                def scores(u):
                    hl, qb = units[u]
                    L = (qb + 1) * P
                    if u == 0:
                        pe.wait_ge(rot_ready, it * 2 + 2)
                    pe.wait_ge(exp_done, it * 16 + 2 * u + 2)
                    for p in range(2):
                        m = 2 * hl + p
                        for half in range(2):
                            last = pe.matmul(ps[u % 2][:, p, 0:L],
                                             rot[32 * m:32 * m + 32, half, qb * P:(qb + 1) * P],
                                             rot[32 * m:32 * m + 32, 2 + half, 0:L],
                                             start=(half == 0), stop=(half == 1))
                    last.then_inc(score_done, 1)

                if more:
                    project(it + 1, 0, it * 4 + 4)
                    project(it + 1, 1, it * 4 + 4)
                scores(0)
                for u, (hl, qb) in enumerate(units):
                    if u + 1 < 8:
                        scores(u + 1)
                    pe.wait_ge(a_ready, it * 8 + u + 3)
                    pe.wait_ge(at_out, it * 8 + u + 1)
                    for kb in range(qb + 1):
                        last = pe.transpose(pt[:, kb * P:(kb + 1) * P], A[:, u % 2, kb * P:(kb + 1) * P],
                                            ident[:])
                    last.then_inc(at_done, 1)
                    if more and u in PROJ_AT:
                        n = PROJ_AT[u]
                        project(it + 1, n, it * 4 + 4 + n // 2)
                    if u == 0:
                        pe.wait_ge(v_ready, it + 1)
                    pe.wait_ge(at_out, it * 8 + u + 2)
                    pe.wait_ge(o_out, it * 8 + u + 1)
                    for kb in range(qb + 1):
                        last = pe.matmul(po[:, 0:P], AT[:, u % 2, kb], v[:, kb, hl * P:(hl + 1) * P],
                                         start=(kb == 0), stop=(kb == qb))
                    last.then_inc(pv_done, 1)
                for hl in range(2):
                    pe.wait_ge(bank_free[hl], it * 4 + (7 if more else 4))
                    pe.wait_ge(on_ready, it * 8 + 4 * hl + 4)
                    for qb in range(NT):
                        last = pe.transpose(pp[hl][:, qb * P:(qb + 1) * P], o[:, 4 * hl + qb], ident[:])
                    last.then_inc(ot_done, 1)

            for n in range(CHUNKS):
                project(0, n, n // 2)
            turns(pe, turn)

        @block.scalar
        def _(act):
            def split(t, n):
                if isinstance(t, int):
                    act.wait_ge(w_loaded[n % RING], 16 * (2 * t + n // RING + 1))
                else:
                    act.wait_ge(w_loaded[n % RING], t * 32 + 16 * (n // RING + 1))
                if not (isinstance(t, int) and t == 0):
                    act.wait_ge(proj_done, (t - 1) * CHUNKS + (n + 1 if n < 4 else 6))
                act.activation(wh[:, :, n * P:(n + 1) * P], w[:, n % RING], ACT.Copy).then_inc(wh_ready, 1)

            def take(t, n):
                act.wait_ge(proj_done, t * CHUNKS + n + 1)
                dst = raw[:, n] if n < 4 else v_next[:, 2 * (n - 4):2 * (n - 4) + 2].rearrange("p a b -> p (a b)")
                act.activation(dst, pp[n % 2][:], ACT.Copy).then_inc(bank_free[n % 2], 1)

            def turn(it, more, more2):
                def exps(u):
                    L = (units[u][1] + 1) * P
                    act.wait_ge(nmax_ready, it * 8 + u + 1)
                    act.wait_ge(a_ready, it * 8 + u + 1)
                    for p in range(2):
                        act.activation(E[:, u % 2, p, 0:L], ps[u % 2][:, p, 0:L], ACT.Exp,
                                       bias=nmax[:, u % 2, p:p + 1], scale=SCALE,
                                       accum_out=rsum[:, u % 2, p:p + 1]).then_inc(exp_done, 1)

                if more:
                    act.wait_ge(rot_ready, it * 2 + 2)
                    take(it + 1, 0)
                    take(it + 1, 1)
                exps(0)
                for u, (hl, qb) in enumerate(units):
                    if u + 1 < 8:
                        exps(u + 1)
                    act.wait_ge(at_done, it * 8 + u + 1)
                    act.activation(AT[:, u % 2, 0:qb + 1].rearrange("p a b -> p (a b)"), pt[:, 0:(qb + 1) * P],
                                   ACT.Copy).then_inc(at_out, 1)
                    for n in SPLIT_AT.get(u, ()) if more else ():
                        split(it + 1, n)
                    if u in SPLIT_ON and more2:
                        split(it + 2, SPLIT_ON[u])
                    if more and u in PROJ_AT:
                        n = PROJ_AT[u]
                        if n == 4:
                            act.wait_ge(v_ready, it + 1)
                        take(it + 1, n)
                    act.wait_ge(pv_done, it * 8 + u + 1)
                    act.activation(sq[:], po[:, 0:P], ACT.Square, accum_out=ss[:, u:u + 1])
                    act.activation(o[:, u], po[:, 0:P], ACT.Copy).then_inc(o_out, 1)
                act.wait_ge(ms_ready, it + 1)
                act.activation(rms[:], ss[:], ACT.Sqrt).then_inc(rms_ready, 1)
                for hl in range(2):
                    act.wait_ge(ot_done, it * 2 + 1 + hl)
                    act.activation(oh[:, it * 2 + hl, :], pp[hl][:], ACT.Copy).then_inc(oh_ready, 1)

            for n in range(CHUNKS):
                split(0, n)
                if n:
                    take(0, n - 1)
            take(0, CHUNKS - 1)
            for n in range(2):
                split(1, n)
                act.sem_inc(bank_free[n], 1)
            act.wait_ge(lam_ready, 1)
            act.activation(lam_exp[:], lam_sum[:], ACT.Exp).then_inc(lam_exped, 1)
            act.sem_inc(exp_done, 4)
            act.sem_inc(at_out, 1)
            act.sem_inc(o_out, 1)
            turns(act, turn)

        @block.vector
        def _(dve):
            own = Chain(dve, dve_step)
            dve.wait_ge(consts_loaded, 64)
            own.link(dve.tensor_tensor(lam_prod[:], lam_row[:, 0:4:2], lam_row[:, 1:4:2], ALU.mult))
            dve.tensor_reduce(lam_sum[:], lam_prod[:], AX.X, ALU.add).then_inc(lam_ready, 1)
            dve.wait_ge(lam_exped, 1)
            own.link(dve.tensor_tensor(neg_lam[:], lam_exp[:, 1:2], lam_exp[:, 0:1], ALU.subtract))
            own.link(dve.tensor_scalar(neg_lam[:], neg_lam[:], -LAMBDA_INIT, None, ALU.add))
            own.link(dve.tensor_scalar(g_row[:], g_row[:], 1.0 - LAMBDA_INIT, None, ALU.mult))
            dve.sem_inc(a_ready, 2)
            before = own.n
            own.per = 2 + 2 * 8 + 3 * 8 + 1

            def turn(it, more, more2):
                own.base, own.n = it * own.per + before, 0
                tmp = E[:].rearrange("p a b t -> p (a b) t")
                for half in range(2):
                    for b in range(2):
                        dve.wait_ge(bank_free[b], it * 4 + half + 1)
                    rope(dve, own, raw[:, 2 * half], raw[:, 2 * half + 1], cos[:], sin[:],
                         rot[:, 2 * half], rot[:, 2 * half + 1], tmp).then_inc(rot_ready, 1)
                    dve.wait_ge(rot_ready, it * 2 + half + 1)

                def maxima(u):
                    hl, qb = units[u]
                    L = (qb + 1) * P
                    dve.wait_ge(score_done, it * 8 + u + 1)
                    diag = ps[u % 2][:, :, qb * P:L]
                    own.link(dve.tensor_tensor(diag, diag, masks[:, 1].unsqueeze(1).broadcast_to([P, 2, P]),
                                               ALU.add))
                    own.link(dve.tensor_reduce(nmax[:, u % 2], ps[u % 2][:, :, 0:L], AX.X, ALU.max,
                                               negate=True))
                    dve.tensor_scalar(nmax[:, u % 2], nmax[:, u % 2], SCALE, None, ALU.mult
                                      ).then_inc(nmax_ready, 1)

                maxima(0)
                for u, (hl, qb) in enumerate(units):
                    L = (qb + 1) * P
                    b = u % 2
                    if u + 1 < 8:
                        maxima(u + 1)
                    dve.wait_ge(exp_done, it * 16 + 2 * u + 6)
                    own.link(dve.reciprocal(rinv[:, b], rsum[:, b]))
                    own.link(dve.tensor_tensor(rinv[:, b, 1:2], rinv[:, b, 1:2], neg_lam[:], ALU.mult))
                    if u >= 2:
                        dve.wait_ge(at_done, it * 8 + u - 1)
                    own.link(dve.tensor_scalar(E[:, b, 0, 0:L], E[:, b, 0, 0:L], rinv[:, b, 0:1], None,
                                               ALU.mult))
                    dve.scalar_tensor_tensor(out=A[:, b, 0:L], in0=E[:, b, 1, 0:L], scalar=rinv[:, b, 1:2],
                                             in1=E[:, b, 0, 0:L], op0=ALU.mult, op1=ALU.add
                                             ).then_inc(a_ready, 1)
                dve.wait_ge(o_out, it * 8 + 9)
                dve.tensor_scalar(ss[:], ss[:], 1.0 / P, EPS, ALU.mult, ALU.add).then_inc(ms_ready, 1)
                dve.wait_ge(rms_ready, it + 1)
                own.link(dve.reciprocal(rstd[:], rms[:]))
                for u in range(8):
                    dve.scalar_tensor_tensor(out=o[:, u], in0=o[:, u], scalar=rstd[:, u:u + 1], in1=g_row[:],
                                             op0=ALU.mult, op1=ALU.mult).then_inc(on_ready, 1)
                for hl in range(2):
                    dve.wait_ge(oh_ready, it * 2 + 1 + hl)
                    dve.tensor_tensor(ol[:, it * 2 + hl, :], pp[hl][:], oh[:, it * 2 + hl, :].bitcast(F32),
                                      ALU.subtract).then_inc(bank_free[hl], 1)
                own.turned()

            turns(dve, turn)


def window_attention(nc, xh, xl, w_l, cos_t, sin_t, b_feat, b_v, sinks, masks, ident, oh, ol):
    FOURS = 4
    CHUNKS = 5 + 2 * FOURS
    BLOCKS = [(f, qb) for f in range(FOURS) for qb in range(NT)]
    with ExitStack() as ctx:
        def sb(name, shape, dt=F32):
            return ctx.enter_context(nc.sbuf_tensor("sw_" + name, shape, dt))

        def sem(name):
            return ctx.enter_context(nc.semaphore("sw_" + name))

        w = sb("w", [P, 2, C, P])
        wh, wl = sb("wh", [P, 2, C, P], F32R), sb("wl", [P, 2, C, P], F32R)
        cos, sin = sb("cos", [P, T]), sb("sin", [P, T])
        bias = sb("bias", [P, CHUNKS])
        bv = sb("bv", [P, P])
        sink = sb("sink", [P, 16])
        raw = sb("raw", [P, 2, T])
        rot_k = sb("rot_k", [P, 2, 2, T])
        rot_q = sb("rot_q", [P, 2, 2, T])
        tmp = sb("tmp", [P, 4, T])
        v = sb("v", [P, NT, P])
        vb = sb("vb", [P, NT, P])
        E = sb("E", [P, 2, 4, 256])
        ET = sb("ET", [P, 2, 4, 2, P])
        o = sb("o", [P, 2, NT, 4, HD])
        mx, mh, nmax, sarg = (sb(n, [P, 2, 4]) for n in ("mx", "mh", "nmax", "sarg"))
        sexp, rsum, den, rinv = (sb(n, [P, 2, 4]) for n in ("sexp", "rsum", "den", "rinv"))
        ps = ctx.enter_context(nc.psum_tensor("sw_ps", [P, 4, 512], F32))
        pp = [ctx.enter_context(nc.psum_tensor(f"sw_pp{n}", [P, 512], F32)) for n in range(2)]
        pt = ctx.enter_context(nc.psum_tensor("sw_pt", [P, 512], F32))
        po = ctx.enter_context(nc.psum_tensor("sw_po", [P, 512], F32))

        consts_loaded = sem("consts_loaded")
        w_loaded = [sem(f"w_loaded{n}") for n in range(2)]
        wh_ready, wl_ready, proj_done = sem("wh_ready"), sem("wl_ready"), sem("proj_done")
        bank_free = [sem(f"bank_free{n}") for n in range(2)]
        raw_ready, rot_ready, v_out, v_ready = sem("raw_ready"), sem("rot_ready"), sem("v_out"), sem("v_ready")
        score_done, nmax_ready, exp_done = sem("score_done"), sem("nmax_ready"), sem("exp_done")
        at_done, at_out = sem("at_done"), sem("at_out")
        pv_done, on_ready = sem("pv_done"), sem("on_ready")
        ot_done, oh_ready, dve_step = sem("ot_done"), sem("oh_ready"), sem("dve_step")
        block = ctx.enter_context(nc.Block())

        uses = [("w", n) for n in range(7)]
        for f in range(1, FOURS + 1):
            if f < FOURS:
                uses += [("w", 5 + 2 * f), ("w", 6 + 2 * f)]
            if f > 1:
                uses += [("o", 2 * (f - 2)), ("o", 2 * (f - 2) + 1)]
        uses += [("o", 2 * (FOURS - 1)), ("o", 2 * (FOURS - 1) + 1)]
        place = {use: n for n, use in enumerate(uses)}

        def ahead(u):
            f, qb = BLOCKS[u]
            return [5 + 2 * (f + 1) + qb] if qb < 2 and f + 1 < FOURS else []

        @block.sync
        def _(sp):
            for n in range(CHUNKS):
                if n >= 2:
                    sp.wait_ge(wl_ready, n - 1)
                sp.dma_start(w[:, n % 2], w_l[n]).then_inc(w_loaded[n % 2], 16)
                if n == 1:
                    sp.dma_start(bias[:], b_feat).then_inc(consts_loaded, 16)
                    sp.dma_start(cos[:], cos_t).then_inc(consts_loaded, 16)
                    sp.dma_start(sin[:], sin_t).then_inc(consts_loaded, 16)
                    sp.dma_start(bv[:], b_v.partition_broadcast(P)).then_inc(consts_loaded, 16)
                    sp.dma_start(sink[:], sinks.partition_broadcast(P)).then_inc(consts_loaded, 16)

        @block.gpsimd
        def _(pool):
            for n in range(CHUNKS):
                pool.wait_ge(wh_ready, n + 1)
                if n >= 2:
                    pool.wait_ge(proj_done, n - 1)
                pool.tensor_tensor(wl[:, n % 2], w[:, n % 2], wh[:, n % 2].bitcast(F32), ALU.subtract
                                   ).then_inc(wl_ready, 1)

        @block.tensor
        def _(pe):
            def bank(use):
                n = place[use]
                if n >= 2:
                    pe.wait_ge(bank_free[n % 2], n // 2)
                return pp[n % 2]

            def project(n):
                dst = bank(("w", n))
                pe.wait_ge(wl_ready, n + 1)
                if n != 4:
                    for c in range(C):
                        pe.matmul(dst[:], wh[:, n % 2, c], xh[:, c, :], start=(c == 0), stop=False)
                        pe.matmul(dst[:], wh[:, n % 2, c], xl[:, c, :], start=False, stop=False)
                        last = pe.matmul(dst[:], wl[:, n % 2, c], xh[:, c, :], start=False, stop=(c == C - 1))
                else:
                    for tt in range(NT):
                        tok = slice(tt * P, (tt + 1) * P)
                        for c in range(C):
                            pe.matmul(dst[:, tok], xh[:, c, tok], wh[:, 0, c], start=(c == 0), stop=False)
                            pe.matmul(dst[:, tok], xh[:, c, tok], wl[:, 0, c], start=False, stop=False)
                            last = pe.matmul(dst[:, tok], xl[:, c, tok], wh[:, 0, c], start=False,
                                             stop=(c == C - 1))
                last.then_inc(proj_done, 1)

            def scores(u):
                f, qb = BLOCKS[u]
                k0 = max(0, qb - 1) * P
                L = (qb + 1) * P - k0
                if qb == 0:
                    pe.wait_ge(rot_ready, 3 + f)
                if u:
                    pe.wait_ge(exp_done, 5 * u)
                for m in range(4):
                    rows = slice(32 * m, 32 * m + 32)
                    for half in range(2):
                        last = pe.matmul(ps[:, m, 0:L], rot_q[rows, f % 2, half, qb * P:(qb + 1) * P],
                                         rot_k[rows, f // 2, half, k0:k0 + L],
                                         start=(half == 0), stop=(half == 1))
                last.then_inc(score_done, 1)

            def turn_output(f):
                for cc in range(2):
                    dst = bank(("o", 2 * f + cc))
                    pe.wait_ge(on_ready, 4 * f + 4)
                    for qb in range(NT):
                        last = pe.transpose(dst[:, qb * P:(qb + 1) * P],
                                            o[:, f % 2, qb, 2 * cc:2 * cc + 2].rearrange("p a b -> p (a b)"),
                                            ident[:])
                    last.then_inc(ot_done, 1)

            for n in range(7):
                project(n)
            scores(0)
            for u, (f, qb) in enumerate(BLOCKS):
                nb = min(2, qb + 1)
                kb0 = max(0, qb - 1)
                pe.wait_ge(exp_done, 5 * u + 5)
                for r in range(2):
                    if u or r:
                        pe.wait_ge(at_out, 2 * u + r)
                    for m in range(2):
                        for kb in range(nb):
                            last = pe.transpose(pt[:, (2 * m + kb) * P:(2 * m + kb + 1) * P],
                                                E[:, u % 2, 2 * r + m, kb * P:(kb + 1) * P], ident[:])
                    last.then_inc(at_done, 1)
                    if r == 0 and u + 1 < len(BLOCKS):
                        scores(u + 1)
                for n in ahead(u):
                    project(n)
                if qb == 1 and f:
                    turn_output(f - 1)
                if u == 0:
                    pe.wait_ge(v_ready, 1)
                pe.wait_ge(at_out, 2 * u + 2)
                if u:
                    pe.wait_ge(on_ready, u)
                for m in range(4):
                    for kb in range(nb):
                        last = pe.matmul(po[:, m * HD:(m + 1) * HD], ET[:, u % 2, m, kb],
                                         vb[:, kb0 + kb, (f // 2) * HD:(f // 2 + 1) * HD],
                                         start=(kb == 0), stop=(kb == nb - 1))
                last.then_inc(pv_done, 1)
            turn_output(FOURS - 1)

        @block.scalar
        def _(act):
            def split(n):
                act.wait_ge(w_loaded[n % 2], 16 * (n // 2 + 1))
                if n >= 2:
                    act.wait_ge(proj_done, n - 1)
                act.activation(wh[:, n % 2], w[:, n % 2], ACT.Copy).then_inc(wh_ready, 1)

            def take(n):
                act.wait_ge(proj_done, n + 1)
                free = bank_free[place[("w", n)] % 2]
                if n == 4:
                    act.activation(v[:].rearrange("p a b -> p (a b)"), pp[0][:], ACT.Copy).then_inc(free, 1)
                    return
                pair, half = (n // 2, n % 2) if n < 4 else ((n - 5) // 2 + 2, (n - 5) % 2)
                if pair and half == 0:
                    act.wait_ge(rot_ready, pair)
                act.activation(raw[:, half], pp[place[("w", n)] % 2][:], ACT.Identity,
                               bias=bias[:, n:n + 1]).then_inc(free, 1)

            def exps(u):
                L = min(2, BLOCKS[u][1] + 1) * P
                act.wait_ge(nmax_ready, u + 1)
                if u >= 2:
                    act.wait_ge(at_done, 2 * u - 2)
                for m in range(4):
                    act.activation(E[:, u % 2, m, 0:L], ps[:, m, 0:L], ACT.Exp,
                                   bias=nmax[:, u % 2, m:m + 1], scale=SCALE,
                                   accum_out=rsum[:, u % 2, m:m + 1]).then_inc(exp_done, 1)
                act.activation(sexp[:, u % 2], sarg[:, u % 2], ACT.Exp).then_inc(exp_done, 1)

            act.wait_ge(consts_loaded, 80)
            for n in range(7):
                split(n)
                if n:
                    take(n - 1)
            take(6)
            split(7)
            split(8)
            exps(0)
            for u, (f, qb) in enumerate(BLOCKS):
                nb = min(2, qb + 1)
                for r in range(2):
                    act.wait_ge(at_done, 2 * u + r + 1)
                    act.activation(ET[:, u % 2, 2 * r:2 * r + 2, 0:nb],
                                   pt[:].rearrange("p (m k n) -> p m k n", m=2, k=2)[:, :, 0:nb], ACT.Copy
                                   ).then_inc(at_out, 1)
                if u + 1 < len(BLOCKS):
                    exps(u + 1)
                for n in ahead(u):
                    take(n)
                    if n + 2 < CHUNKS:
                        split(n + 2)
                if qb == 1 and f or u == len(BLOCKS) - 1:
                    g = f - 1 if qb == 1 else f
                    for cc in range(2):
                        act.wait_ge(ot_done, 2 * g + cc + 1)
                        act.activation(oh[:, 2 * g + cc, :], pp[place[("o", 2 * g + cc)] % 2][:], ACT.Copy
                                       ).then_inc(oh_ready, 1)

        @block.vector
        def _(dve):
            own = Chain(dve, dve_step)
            dve.wait_ge(consts_loaded, 80)

            def rotate(pair):
                first = 2 * pair if pair < 2 else 5 + 2 * (pair - 2)
                for half in range(2):
                    n = place[("w", first + half)]
                    dve.wait_ge(bank_free[n % 2], n // 2 + 1)
                out = rot_k[:, pair] if pair < 2 else rot_q[:, pair % 2]
                if pair >= 4:
                    dve.wait_ge(score_done, 4 * (pair - 3))
                rope(dve, own, raw[:, 0], raw[:, 1], cos[:], sin[:], out[:, 0], out[:, 1], tmp
                     ).then_inc(rot_ready, 1)
                dve.wait_ge(rot_ready, pair + 1)

            def maxima(u):
                f, qb = BLOCKS[u]
                b = u % 2
                L = min(2, qb + 1) * P
                dve.wait_ge(score_done, u + 1)
                mask = masks[:].rearrange("p a b -> p (a b)")[:, 2 * P - L:]
                own.link(dve.tensor_tensor(ps[:, :, 0:L], ps[:, :, 0:L],
                                           mask.unsqueeze(1).broadcast_to([P, 4, L]), ALU.add))
                own.link(dve.tensor_reduce(mx[:, b], ps[:, :, 0:L], AX.X, ALU.max))
                own.link(dve.scalar_tensor_tensor(out=mh[:, b], in0=mx[:, b], scalar=SCALE,
                                                  in1=sink[:, 4 * f:4 * f + 4], op0=ALU.mult, op1=ALU.max))
                dve.tensor_scalar(nmax[:, b], mh[:, b], -1.0, None, ALU.mult)
                dve.tensor_tensor(sarg[:, b], sink[:, 4 * f:4 * f + 4], mh[:, b], ALU.subtract
                                  ).then_inc(nmax_ready, 1)

            rotate(0)
            rotate(1)
            dve.wait_ge(bank_free[0], 3)
            dve.tensor_tensor(vb[:], v[:], bv[:].unsqueeze(1).broadcast_to([P, NT, P]), ALU.add
                              ).then_inc(v_ready, 1)
            rotate(2)
            maxima(0)
            for u, (f, qb) in enumerate(BLOCKS):
                b = u % 2
                if u + 1 < len(BLOCKS):
                    maxima(u + 1)
                dve.wait_ge(exp_done, 5 * u + 5)
                own.link(dve.tensor_tensor(den[:, b], rsum[:, b], sexp[:, b], ALU.add))
                own.link(dve.reciprocal(rinv[:, b], den[:, b]))
                dve.wait_ge(pv_done, u + 1)
                if qb == 0 and f >= 2:
                    dve.wait_ge(ot_done, 2 * (f - 1))
                dve.tensor_tensor(o[:, f % 2, qb], po[:, 0:4 * HD].rearrange("p (m e) -> p m e", m=4),
                                  rinv[:, b].unsqueeze(2).broadcast_to([P, 4, HD]), ALU.mult
                                  ).then_inc(on_ready, 1)
                if qb == 1 and f or u == len(BLOCKS) - 1:
                    g = f - 1 if qb == 1 else f
                    for cc in range(2):
                        n = place[("o", 2 * g + cc)]
                        dve.wait_ge(oh_ready, 2 * g + cc + 1)
                        dve.tensor_tensor(ol[:, 2 * g + cc, :], pp[n % 2][:], oh[:, 2 * g + cc, :].bitcast(F32),
                                          ALU.subtract).then_inc(bank_free[n % 2], 1)
                if qb == 1 and f + 1 < FOURS:
                    rotate(f + 3)


def norm_tile(dve, own, act_sqrt, r, stats, mv, var, std, rstd, g_row, b_row, out):
    for half in range(2):
        ins = dve.bn_stats(stats[:, half], r[:, half * 512:(half + 1) * 512])
        own.link(ins)
    own.link(dve.bn_aggr(mv, stats))
    act_sqrt(dve.tensor_scalar(var, mv[:, 1:2], EPS, None, ALU.add))
    own.link(dve.reciprocal(rstd, std))
    own.link(dve.tensor_scalar(r, r, mv[:, 0:1], rstd, ALU.subtract, ALU.mult))
    own.link(dve.tensor_tensor(r, r, g_row, ALU.mult))
    return dve.tensor_tensor(out, r, b_row, ALU.add)


def add_and_norm(nc, tag, xres, xh, xl, ident, g, b, *, oh=None, ol=None, w_o=None, b_o=None, acc=None, out=None):
    with ExitStack() as ctx:
        def sb(name, shape, dt=F32):
            return ctx.enter_context(nc.sbuf_tensor(name + tag, shape, dt))

        def sem(name):
            return ctx.enter_context(nc.semaphore(name + tag))

        g_row, b_row = sb("g_row", [P, D]), sb("b_row", [P, D])
        bo_row = sb("bo_row", [P, D]) if b_o is not None else None
        if w_o is not None:
            wo = sb("wo", [P, 4, D])
            wh, wl = sb("wh", [P, 2, D], F32R), sb("wl", [P, 2, D], F32R)
        r = sb("r", [P, 2, D])
        stats = sb("stats", [P, 2, 6])
        mv = sb("mv", [P, 2])
        var, std, rstd = sb("var", [P, 1]), sb("std", [P, 1]), sb("rstd", [P, 1])
        banks = [ctx.enter_context(nc.psum_tensor(f"bank{n}{tag}", [P, 512], F32)) for n in range(8)]
        w_loaded = [sem(f"w_loaded{n}") for n in range(4)]
        wh_ready, wl_ready, w_used = sem("wh_ready"), sem("wl_ready"), sem("w_used")
        rows_loaded, stored, xl_ready = sem("rows_loaded"), sem("stored"), sem("xl_ready")
        mix_done, mix_used, var_ready, std_ready = sem("mix_done"), sem("mix_used"), sem("var_ready"), sem("std_ready")
        x_ready, xt_done, xt_out, dve_step = sem("x_ready"), sem("xt_done"), sem("xt_out"), sem("dve_step")
        block = ctx.enter_context(nc.Block())

        @block.sync
        def _(sp):
            if w_o is not None:
                for c in range(C):
                    if c >= 4:
                        sp.wait_ge(wl_ready, c - 3)
                    sp.dma_start(wo[:, c % 4], w_o[c * P:(c + 1) * P, :]).then_inc(w_loaded[c % 4], 16)
            sp.dma_start(g_row[:], g.partition_broadcast(P)).then_inc(rows_loaded, 16)
            sp.dma_start(b_row[:], b.partition_broadcast(P)).then_inc(rows_loaded, 16)
            if b_o is not None:
                sp.dma_start(bo_row[:], b_o.partition_broadcast(P)).then_inc(rows_loaded, 16)
            if out is not None:
                for tt in range(NT):
                    sp.wait_ge(x_ready, tt + 1)
                    sp.dma_start(out[tt * P:(tt + 1) * P, :], xres[:, tt]).then_inc(stored, 16)
                sp.wait_ge(stored, 16 * NT)

        @block.tensor
        def _(pe):
            if w_o is not None:
                for c in range(C):
                    pe.wait_ge(wl_ready, c + 1)
                    for n in range(2 * NT):
                        tok = slice(n // 2 * P, (n // 2 + 1) * P)
                        half = slice(n % 2 * 512, (n % 2 + 1) * 512)
                        pe.matmul(banks[n][:], oh[:, c, tok], wh[:, c % 2, half], start=(c == 0), stop=False)
                        pe.matmul(banks[n][:], oh[:, c, tok], wl[:, c % 2, half], start=False, stop=False)
                        last = pe.matmul(banks[n][:], ol[:, c, tok], wh[:, c % 2, half], start=False,
                                         stop=(c == C - 1))
                        if c == C - 1:
                            last.then_inc(mix_done, 1)
                    if c < C - 1:
                        last.then_inc(w_used, 1)
            if out is None:
                for tt in range(NT):
                    pe.wait_ge(x_ready, tt + 1)
                    for half in range(2):
                        for c in range(4):
                            last = pe.transpose(banks[2 * tt + half][:, c * P:(c + 1) * P],
                                                xres[:, tt, (4 * half + c) * P:(4 * half + c + 1) * P],
                                                ident[:])
                        last.then_inc(xt_done, 1)

        @block.gpsimd
        def _(pool):
            if w_o is not None:
                for c in range(C):
                    pool.wait_ge(wh_ready, c + 1)
                    if c >= 2:
                        pool.wait_ge(w_used, c - 1)
                    pool.tensor_tensor(wl[:, c % 2], wo[:, c % 4], wh[:, c % 2].bitcast(F32), ALU.subtract
                                       ).then_inc(wl_ready, 1)

        @block.scalar
        def _(act):
            if w_o is not None:
                for c in range(C):
                    act.wait_ge(w_loaded[c % 4], 16 * (c // 4 + 1))
                    if c >= 2:
                        act.wait_ge(w_used, c - 1)
                    act.activation(wh[:, c % 2], wo[:, c % 4], ACT.Copy).then_inc(wh_ready, 1)
            for tt in range(NT):
                act.wait_ge(var_ready, tt + 1)
                act.activation(std[:], var[:], ACT.Sqrt).then_inc(std_ready, 1)
            if out is None:
                for n in range(2 * NT):
                    tt, half = n // 2, n % 2
                    act.wait_ge(xt_done, n + 1)
                    act.activation(xh[:, 4 * half:4 * half + 4, tt * P:(tt + 1) * P],
                                   banks[n][:].rearrange("p (c t) -> p c t", c=4), ACT.Copy).then_inc(xt_out, 1)

        @block.vector
        def _(dve):
            own = Chain(dve, dve_step)
            dve.wait_ge(rows_loaded, 32 if b_o is None else 48)
            for tt in range(NT):
                row = r[:, tt % 2]
                if w_o is not None:
                    for dh in range(2):
                        half = slice(dh * 512, (dh + 1) * 512)
                        dve.wait_ge(mix_done, 2 * tt + dh + 1)
                        own.link(dve.scalar_tensor_tensor(out=row[:, half], in0=xres[:, tt, half],
                                                          scalar=ALPHA, in1=banks[2 * tt + dh][:],
                                                          op0=ALU.mult, op1=ALU.add))
                    if b_o is not None:
                        own.link(dve.tensor_tensor(row, row, bo_row[:], ALU.add))
                else:
                    own.link(dve.scalar_tensor_tensor(out=row, in0=xres[:, tt], scalar=ALPHA,
                                                      in1=acc[:, tt], op0=ALU.mult, op1=ALU.add))

                def act_sqrt(var_ins):
                    var_ins.then_inc(var_ready, 1)
                    dve.wait_ge(std_ready, tt + 1)

                norm_tile(dve, own, act_sqrt, row, stats[:], mv[:], var[:], std[:], rstd[:], g_row[:],
                          b_row[:], xres[:, tt]).then_inc(x_ready, 1)
            if out is None:
                for n in range(2 * NT):
                    chunks, tok = slice(4 * (n % 2), 4 * (n % 2) + 4), slice(n // 2 * P, (n // 2 + 1) * P)
                    dve.wait_ge(xt_out, n + 1)
                    dve.tensor_tensor(xl[:, chunks, tok], banks[n][:].rearrange("p (c t) -> p c t", c=4),
                                      xh[:, chunks, tok].bitcast(F32), ALU.subtract).then_inc(xl_ready, 1)
                dve.wait_ge(xl_ready, 2 * NT)


def route(nc, tag, xh, xl, ident, iota_rank, wq_l, keys_l, eiT, ejT, gateT):
    with ExitStack() as ctx:
        def sb(name, shape, dt=F32):
            return ctx.enter_context(nc.sbuf_tensor(name + tag, shape, dt))

        def sem(name):
            return ctx.enter_context(nc.semaphore(name + tag))

        TURNS = PH // 2
        wq = sb("wq", [P, 2, C, P])
        wh, wl = sb("wqh", [P, 2, C, P], F32R), sb("wql", [P, 2, C, P], F32R)
        keys = sb("keys", [P, 2, NK])
        qT = sb("qT", [P, 2, T])
        sc = sb("sc", [P, 2, 2, NT, NK])
        came = sb("came", [P, 1])
        rest = sb("rest", [P, 2, NT, NK])
        top = sb("top", [P, 2, NT, 2, K])
        idx = sb("idx", [P, 2, NT, 2, K], U32)
        cand = sb("cand", [P, NT, K, K])
        crest = sb("crest", [P, NT, K * K])
        tops = sb("tops", [P, 2, NT, K])
        poss = sb("poss", [P, 2, NT, K], U32)
        i1 = sb("i1", [P, NT, PH, K])
        i2 = sb("i2", [P, NT, PH, K])
        ts = sb("ts", [P, NT, PH, K])
        pos = sb("pos", [P, NT, PH, K], U32)
        half_u = sb("half_u", [P, PH * K], U32)
        rank = sb("rank", [P, PH, K])
        eq = sb("eq", [P, PH, K, K])
        hit = sb("hit", [P, PH, K, K])
        eij = sb("eij", [P, 2, PH, K])
        gex = sb("gex", [P, PH, K])
        gsum = sb("gsum", [P, PH])
        ginv = sb("ginv", [P, PH])
        pq = [ctx.enter_context(nc.psum_tensor(f"pq{n}{tag}", [P, 512], F32)) for n in range(2)]
        psc = [ctx.enter_context(nc.psum_tensor(f"psc{n}{tag}", [P, 512], F32)) for n in range(4)]
        ptr = ctx.enter_context(nc.psum_tensor("ptr" + tag, [P, 512], F32))
        w_loaded = [sem(f"w_loaded{n}") for n in range(2)]
        wh_ready, wl_ready = sem("wqh_ready"), sem("wql_ready")
        q_done, q_out = sem("q_done"), sem("q_out")
        sc_done, sc_out = sem("sc_done"), sem("sc_out")
        top_done, dve_step = sem("top_done"), sem("dve_step")
        gex_in, gex_out = sem("gex_in"), sem("gex_out")
        tr_ready, tr_done, tr_out = sem("tr_ready"), sem("tr_done"), sem("tr_out")
        block = ctx.enter_context(nc.Block())

        @block.sync
        def _(sp):
            with sp.Fori(0, TURNS) as it:
                for b in range(2):
                    sp.wait_ge(sc_done, it * 4 + 2 * b + 2)
                    sp.dma_start(wq[:, b], wq_l[it * 2 + b]).then_inc(w_loaded[b], 16)
                    sp.dma_start(keys[:, b], keys_l[it * 2 + b]).then_inc(w_loaded[b], 16)

        @block.tensor
        def _(pe):
            pe.sem_inc(sc_done, 4)
            with pe.Fori(0, TURNS) as it:
                for b in range(2):
                    pe.wait_ge(w_loaded[b], it * 32 + 32)
                    pe.wait_ge(q_out, it * 2 + b + 1)
                    pe.wait_ge(wl_ready, it * 2 + b + 1)
                    for c in range(C):
                        pe.matmul(pq[b][:], wh[:, b, c], xh[:, c, :], start=(c == 0), stop=False)
                        pe.matmul(pq[b][:], wh[:, b, c], xl[:, c, :], start=False, stop=False)
                        last = pe.matmul(pq[b][:], wl[:, b, c], xh[:, c, :], start=False, stop=(c == C - 1))
                    last.then_inc(q_done, 1)
                    pe.wait_ge(q_out, it * 2 + b + 3)
                    pe.wait_ge(sc_out, it * 4 + 2 * b + 2)
                    for half in range(2):
                        rows = slice(half * 64, half * 64 + 64)
                        for tt in range(NT):
                            last = pe.matmul(psc[2 * b + half][:, tt * NK:(tt + 1) * NK],
                                             qT[rows, b, tt * P:(tt + 1) * P], keys[rows, b],
                                             start=True, stop=True)
                        last.then_inc(sc_done, 1)
            for tt in range(NT):
                pe.wait_ge(tr_ready, tt + 1)
                if tt:
                    pe.wait_ge(tr_out, 3 * tt)
                for n, src in enumerate((eij[:, 0], eij[:, 1], gex[:])):
                    last = pe.transpose(ptr[:, n * P:(n + 1) * P], src.rearrange("p a b -> p (a b)"), ident[:])
                last.then_inc(tr_done, 1)

        @block.gpsimd
        def _(pool):
            pool.sem_inc(q_done, 2)
            with pool.Fori(0, TURNS) as it:
                for b in range(2):
                    pool.wait_ge(wh_ready, it * 2 + b + 1)
                    pool.wait_ge(q_done, it * 2 + b + 1)
                    pool.tensor_tensor(wl[:, b], wq[:, b], wh[:, b].bitcast(F32), ALU.subtract
                                       ).then_inc(wl_ready, 1)

        @block.scalar
        def _(act):
            act.sem_inc(q_out, 2)
            act.sem_inc(sc_out, 4)

            def split(head, b):
                act.wait_ge(w_loaded[b], (head - b) * 16 + 32)
                act.wait_ge(q_done, head + 1)
                act.activation(wh[:, b], wq[:, b], ACT.Copy).then_inc(wh_ready, 1)

            with act.Fori(0, TURNS) as it:
                for b in range(2):
                    split(it * 2 + b, b)
                    act.wait_ge(q_done, it * 2 + b + 3)
                    act.wait_ge(sc_done, it * 4 + 2 * b + 4 - 2)
                    act.activation(qT[:, b], pq[b][:], ACT.Copy).then_inc(q_out, 1)
                    act.wait_ge(top_done, it * 2 + b + 1)
                    for half in range(2):
                        act.wait_ge(sc_done, it * 4 + 2 * b + half + 5)
                        act.activation(sc[:, b, half].rearrange("p a b -> p (a b)"), psc[2 * b + half][:],
                                       ACT.Copy).then_inc(sc_out, 1)
            for tt in range(NT):
                act.wait_ge(gex_in, tt + 1)
                act.activation(gex[:], gex[:], ACT.Exp).then_inc(gex_out, 1)
                act.wait_ge(tr_done, tt + 1)
                for n, dst in enumerate((eiT, ejT, gateT)):
                    act.activation(dst[:, tt * P:(tt + 1) * P], ptr[:, n * P:(n + 1) * P], ACT.Copy
                                   ).then_inc(tr_out, 1)

        @block.vector
        def _(dve):
            own = Chain(dve, dve_step)
            dve.sem_inc(top_done, 2)

            def top16(lists):
                seen = [own.mark(dve.max(out_top[:, 0:8], values)) for values, out_top, _, _ in lists]
                gone = []
                for n, (values, out_top, out_idx, scratch) in zip(seen, lists):
                    own.wait(n)
                    dve.max_index(out_idx[:, 0:8], out_top[:, 0:8], values)
                    gone.append(own.mark(dve.match_replace(scratch, out_top[:, 0:8], values, -3.0e38)))
                seen = []
                for n, (_, out_top, _, scratch) in zip(gone, lists):
                    own.wait(n)
                    seen.append(own.mark(dve.max(out_top[:, 8:16], scratch)))
                for n, (_, out_top, out_idx, scratch) in zip(seen, lists):
                    own.wait(n)
                    last = own.mark(dve.max_index(out_idx[:, 8:16], out_top[:, 8:16], scratch))
                return last

            with dve.Fori(0, TURNS) as it:
                for b in range(2):
                    dve.sem_clear(dve_step)
                    own.n = 0
                    dve.wait_ge(sc_out, it * 4 + 2 * b + 6)
                    own.link(dve.tensor_copy(came[:], sc[:, b, 1, 0, 0:1]))
                    last = top16([(sc[:, b, half, tt], top[:, b, tt, half], idx[:, b, tt, half], rest[:, half, tt])
                                  for tt in range(NT) for half in range(2)])
                    own.wait(last)
                    for tt in range(NT):
                        last = own.mark(dve.tensor_tensor(
                            cand[:, tt], top[:, b, tt, 0].unsqueeze(2).broadcast_to([P, K, K]),
                            top[:, b, tt, 1].unsqueeze(1).broadcast_to([P, K, K]), ALU.add))
                    own.wait(last)
                    own.wait(top16([(cand[:, tt].rearrange("p a b -> p (a b)"), tops[:, b, tt], poss[:, b, tt],
                                     crest[:, tt]) for tt in range(NT)]))
                    head = it * 2 + b
                    dve.tensor_copy(i1[:, :, head, :], idx[:, b, :, 0])
                    dve.tensor_copy(i2[:, :, head, :], idx[:, b, :, 1])
                    dve.tensor_copy(ts[:, :, head, :], tops[:, b])
                    dve.tensor_copy(pos[:, :, head, :], poss[:, b]).then_inc(top_done, 1)
            dve.wait_ge(top_done, 2 + PH)
            dve.sem_clear(dve_step)
            own.n = 0
            for tt in range(NT):
                if tt:
                    dve.wait_ge(tr_done, tt)
                for side, (op, arg, ids) in enumerate(((ALU.logical_shift_right, 4, i1),
                                                       (ALU.bitwise_and, K - 1, i2))):
                    own.link(dve.tensor_scalar(half_u[:], pos[:, tt].rearrange("p a b -> p (a b)"), arg, None, op))
                    own.link(dve.tensor_copy(rank[:].rearrange("p a b -> p (a b)"), half_u[:]))
                    own.link(dve.tensor_tensor(
                        eq[:].rearrange("p h k a -> p (h k) a"),
                        rank[:].rearrange("p h k -> p (h k)").unsqueeze(2).broadcast_to([P, PH * K, K]),
                        iota_rank[:].unsqueeze(1).broadcast_to([P, PH * K, K]), ALU.is_equal))
                    own.link(dve.tensor_tensor(hit[:], eq[:], ids[:, tt].unsqueeze(2).broadcast_to([P, PH, K, K]),
                                               ALU.mult))
                    own.link(dve.tensor_reduce(eij[:, side], hit[:], AX.X, ALU.add))
                dve.tensor_tensor(gex[:], ts[:, tt], ts[:, tt, :, 0:1].broadcast_to([P, PH, K]),
                                  ALU.subtract).then_inc(gex_in, 1)
                dve.wait_ge(gex_out, tt + 1)
                own.link(dve.tensor_reduce(gsum[:], gex[:], AX.X, ALU.add))
                own.link(dve.reciprocal(ginv[:], gsum[:]))
                dve.tensor_tensor(gex[:], gex[:], ginv[:].unsqueeze(2).broadcast_to([P, PH, K]), ALU.mult
                                  ).then_inc(tr_ready, 1)


def spread_gates(nc, tag, iota_keys, eiT, ejT, gateT, g_dram):
    SUB = 8
    STEPS = TG // SUB
    TURNS = T // TG // 2
    with ExitStack() as ctx:
        def sb(name, shape, dt=F32):
            return ctx.enter_context(nc.sbuf_tensor(name + tag, shape, dt))

        def sem(name):
            return ctx.enter_context(nc.semaphore(name + tag))

        left = sb("left", [P, 2, SUB, NK])
        right = sb("right", [P, 2, SUB, NK])
        hot = sb("hot", [P, 2, SUB, NK])
        stage = sb("stage", [P, 2, NK, TG])
        banks = [ctx.enter_context(nc.psum_tensor(f"gbank{n}{tag}", [P, 4, NK], F32)) for n in range(4)]
        hot_ready = sem("hot_ready")
        left_ready, right_ready = sem("left_ready"), sem("right_ready")
        g_done, g_out = sem("g_done"), sem("g_out")
        g_stored = [sem(f"g_stored{n}") for n in range(2)]
        block = ctx.enter_context(nc.Block())
        N = 2 * STEPS

        @block.sync
        def _(sp):
            for b in range(2):
                sp.sem_inc(g_stored[b], 16)
            with sp.Fori(0, TURNS) as it:
                for b in range(2):
                    sp.wait_ge(g_out, it * 2 * N + (b + 1) * N + 4)
                    sp.dma_start(g_dram[it * 2 + b], stage[:, b]).then_inc(g_stored[b], 16)
            for b in range(2):
                sp.wait_ge(g_stored[b], 16 * (TURNS + 1))

        def columns(m, t0):
            return m[:, bass.ds(t0, SUB)].unsqueeze(2).broadcast_to([P, SUB, NK])

        @block.gpsimd
        def _(pool):
            with pool.Fori(0, TURNS) as it:
                for s in range(N):
                    pool.wait_ge(hot_ready, it * N + s + 1)
                    pool.wait_ge(g_done, it * N + s + 1)
                    pool.tensor_tensor(right[:, s % 2], hot[:, s % 2], columns(gateT, it * (2 * TG) + s * SUB),
                                       ALU.mult).then_inc(right_ready, 1)

        @block.vector
        def _(dve):
            iota = iota_keys[:].unsqueeze(1).broadcast_to([P, SUB, NK])
            dve.sem_inc(right_ready, 2)
            with dve.Fori(0, TURNS) as it:
                for s in range(N):
                    t0 = it * (2 * TG) + s * SUB
                    dve.wait_ge(right_ready, it * N + s + 1)
                    dve.tensor_tensor(hot[:, s % 2], iota, columns(ejT, t0), ALU.is_equal).then_inc(hot_ready, 1)
                    dve.wait_ge(g_done, it * N + s + 1)
                    dve.tensor_tensor(left[:, s % 2], iota, columns(eiT, t0), ALU.is_equal).then_inc(left_ready, 1)

        @block.tensor
        def _(pe):
            pe.sem_inc(g_done, 2)
            with pe.Fori(0, TURNS) as it:
                for s in range(N):
                    pe.wait_ge(left_ready, it * N + s + 1)
                    pe.wait_ge(right_ready, it * N + s + 3)
                    pe.wait_ge(g_out, it * 2 * N + 2 * s + 2)
                    for n in range(SUB):
                        last = pe.matmul(banks[2 * (s % 2) + n // 4][:, n % 4], left[:, s % 2, n],
                                         right[:, s % 2, n], start=True, stop=True)
                    last.then_inc(g_done, 1)

        @block.scalar
        def _(act):
            act.sem_inc(g_out, 4)
            with act.Fori(0, TURNS) as it:
                for s in range(N):
                    b = s // STEPS
                    act.wait_ge(g_done, it * N + s + 3)
                    if s % STEPS == 0:
                        act.wait_ge(g_stored[b], it * 16 + 16)
                    for q in range(2):
                        t0 = (s % STEPS) * SUB + 4 * q
                        act.activation(stage[:, b, :, t0:t0 + 4], banks[2 * (s % 2) + q][:].rearrange("p t j -> p j t"),
                                       ACT.Copy).then_inc(g_out, 1)


def clear_semaphores(nc):
    free = sorted(nc.free_semaphores)
    assert free == list(range(free[0], free[-1] + 1))
    with nc.Block() as block:
        @block.gpsimd
        def _(pool):
            pool.sem_clear(range(free[0], free[-1] + 1))


def trunk(nc, a, out):
    g_dram = nc.dram_tensor("g_dram", [T // TG, P, NK, TG], F32, kind="Internal").ap()
    with ExitStack() as ctx:
        def sb(name, shape, dt=F32):
            return ctx.enter_context(nc.sbuf_tensor(name, shape, dt))

        xres = sb("xres", [P, NT, D])
        xh, xl = sb("xh", [P, C, T], F32R), sb("xl", [P, C, T], F32R)
        ident, masks, iota_keys, iota_rank = constants(nc, ctx)
        load_tokens(nc, a["x"], a["x_t"], xres, xh, xl)
        for layer in range(DEPTH):
            tag = f"_{layer}"
            if layer:
                clear_semaphores(nc)
            with nc.sbuf_tensor("oh" + tag, [P, C, T], F32R) as oh, nc.sbuf_tensor("ol" + tag, [P, C, T], F32R) as ol:
                if layer % 2 == 0:
                    diff_attention(nc, xh, xl, a["da_w"], a["cos_t"], a["sin_t"], a["da_lambda"], a["da_subln_g"],
                                   masks, ident, oh, ol)
                    w_o, b_o = a["da_w_o"], None
                else:
                    window_attention(nc, xh, xl, a["sw_w"], a["cos_t"], a["sin_t"], a["sw_b"], a["sw_bv"],
                                     a["sw_sinks"], masks, ident, oh, ol)
                    w_o, b_o = a["sw_w_o"], a["sw_b_o"]
                add_and_norm(nc, "_m" + tag, xres, xh, xl, ident, a["ln1_g"][layer], a["ln1_b"][layer], oh=oh, ol=ol,
                             w_o=w_o, b_o=b_o)
            with ExitStack() as routed:
                eiT, ejT, gateT = (routed.enter_context(nc.sbuf_tensor(n + tag, [P, T], F32))
                                   for n in ("eiT", "ejT", "gateT"))
                route(nc, tag, xh, xl, ident, iota_rank, a["pk_wq"][layer], a["pk_keys"][layer], eiT, ejT, gateT)
                spread_gates(nc, tag, iota_keys, eiT, ejT, gateT, g_dram)
            with nc.sbuf_tensor("acc" + tag, [P, NT, D], F32) as acc:
                dense(nc, xh, xl, a["pk_u"][layer], a["pk_v"][layer], g_dram, acc, tag)
                last = layer == DEPTH - 1
                add_and_norm(nc, "_p" + tag, xres, xh, xl, ident, a["ln2_g"][layer], a["ln2_b"][layer], acc=acc,
                             out=out if last else None)


def lay_out(np, x, da_w_qkv, da_lambda, da_subln_g, da_w_o, sw_w_qkv, sw_b_qkv, sw_sinks, sw_w_o, sw_b_o,
            pk_w_query, pk_sub_keys, pk_u, pk_v, ln1_g, ln1_b, ln2_g, ln2_b):
    def tiled(w):
        return w.reshape(*w.shape[:-2], C, P, w.shape[-1]).swapaxes(-3, -2)

    a = {"x": x[0], "x_t": tiled(x[0].T)}
    inv = (1.0 / (10000.0 ** (np.arange(0, HD, 2, dtype=np.float32) / np.float32(HD)))).astype(np.float32)
    ang = np.arange(T, dtype=np.float32)[:, None] * inv[None, :]
    a["cos_t"] = np.tile(np.cos(ang).T, (4, 1)).astype(np.float32)
    a["sin_t"] = np.tile(np.sin(ang).T, (4, 1)).astype(np.float32)

    cols = []
    for it in range(4):
        for part in range(2):
            for half in range(2):
                cols += [part * D + (4 * it + m) * HD + half * 32 + r for m in range(4) for r in range(32)]
        cols += list(range(2 * D + it * 2 * P, 2 * D + (it + 1) * 2 * P))
    a["da_w"] = tiled(da_w_qkv[0][:, cols]).reshape(P, C, 4, 6, P).transpose(2, 3, 0, 1, 4)
    a["da_lambda"] = da_lambda[0]
    a["da_subln_g"] = da_subln_g[0]
    a["da_w_o"] = da_w_o[0]

    w, b = sw_w_qkv[0], sw_b_qkv[0]
    cols = []
    for kv in range(2):
        for half in range(2):
            cols += [(16 + kv) * HD + half * 32 + r for m in range(4) for r in range(32)]
    cols += list(range(18 * HD, 20 * HD))
    for four in range(4):
        for half in range(2):
            cols += [(4 * four + m) * HD + half * 32 + r for m in range(4) for r in range(32)]
    a["sw_w"] = tiled(w[:, cols]).reshape(P, C, 13, P).transpose(2, 0, 1, 3)
    a["sw_b"] = b[cols].reshape(13, P).T
    a["sw_bv"] = b[18 * HD:]
    a["sw_sinks"] = sw_sinks[0]
    a["sw_w_o"] = sw_w_o[0]
    a["sw_b_o"] = sw_b_o[0]

    a["pk_wq"] = tiled(pk_w_query).reshape(DEPTH, P, C, PH, P).transpose(0, 3, 1, 2, 4)
    a["pk_keys"] = pk_sub_keys.transpose(0, 1, 2, 4, 3).reshape(DEPTH, PH, P, NK)
    a["pk_u"] = pk_u.reshape(DEPTH, P, GROUPS, JG, C, P).transpose(0, 2, 5, 3, 4, 1).reshape(
        DEPTH, GROUPS, P, JG, C * P)
    a["pk_v"] = pk_v.reshape(DEPTH, P, GROUPS, JG, D).transpose(0, 2, 1, 3, 4)
    a["ln1_g"], a["ln1_b"], a["ln2_g"], a["ln2_b"] = ln1_g, ln1_b, ln2_g, ln2_b
    return a


def kernel(**inputs):
    import concourse.bacc as bacc
    import numpy as np
    from concourse.bass_utils import run_bass_kernel_spmd

    nc = bacc.Bacc("TRN2", target_bir_lowering=False, num_devices=1)
    laid = lay_out(np, **{k: np.asarray(v) for k, v in inputs.items()})
    arrays, aps = {}, {}
    for name, v in laid.items():
        v = np.ascontiguousarray(v)
        arrays[f"in_{name}"] = v
        aps[name] = nc.dram_tensor(f"in_{name}", v.shape, mybir.dt.from_np(v.dtype), kind="ExternalInput").ap()
    out = nc.dram_tensor("out", [T, D], F32, kind="ExternalOutput").ap()
    trunk(nc, aps, out)
    r = run_bass_kernel_spmd(nc, [arrays], core_ids=[0])
    return r.results[0]["out"].reshape(1, T, D)
```

```python
import math
from contextlib import ExitStack

import concourse.bass as bass
from concourse import mybir

ALU = mybir.AluOpType
ACT = mybir.ActivationFunctionType
AX = mybir.AxisListType
F32 = mybir.dt.float32
F32R = mybir.dt.float32r
U32 = mybir.dt.uint32

P = 128
T = 512
NT = T // P
D = 1024
C = D // P
DEPTH = 2
ALPHA = (2 * DEPTH) ** 0.25
EPS = 1e-5
HD = 64
SCALE = HD ** -0.5
NEG = -1e30
LAMBDA_INIT = 0.8 - 0.6 * math.exp(0.0)

PH = 8
NK = 128
K = 16
TG = 32
G_STORED = 16 * (T // TG // 2 + 1)
JG = 2
ROUTED = 28
EARLY = 32
GROUPS = (NK - EARLY) // JG
assert EARLY % (2 * JG) == 0 and GROUPS % 2 == 0 and PH % 2 == 0


def early_columns(nc, first_h, early_h, v_l, g_dram, g_stored, acc, tag):
    STEPS = EARLY // JG
    with ExitStack() as ctx:
        def sb(name, shape, dt):
            return ctx.enter_context(nc.sbuf_tensor("early_" + name + tag, shape, dt))

        def sem(name):
            return ctx.enter_context(nc.semaphore("ec_" + name + tag))

        vr = sb("vr", [P, 2, JG, D], F32)
        gt = sb("gt", [P, 2, T // TG, JG, TG], F32)
        wf = sb("wf", [P, 2, T], F32)
        wh = sb("wh", [P, 2, JG, T], F32R)
        wl = sb("wl", [P, 2, JG, T], F32R)
        vh = sb("vh", [P, 2, JG, D], F32R)
        vl = sb("vl", [P, 2, JG, D], F32R)
        sums = [ctx.enter_context(nc.psum_tensor(f"early_sum{n}{tag}", [P, 512], F32)) for n in range(2 * NT)]
        v_loaded = [sem(f"v_loaded{n}") for n in range(2)]
        g_loaded = [sem(f"g_loaded{n}") for n in range(2)]
        vh_ready, vl_ready = sem("vh_ready"), sem("vl_ready")
        wf_ready, wh_ready, wl_ready = sem("wf_ready"), sem("wh_ready"), sem("wl_ready")
        col_done, all_done, acc_out = sem("col_done"), sem("all_done"), sem("acc_out")
        block = ctx.enter_context(nc.Block())

        def pairs(eng, step):
            for g in range(PH // JG):
                step(g, g % 2)
            with eng.Fori(PH // JG // 2, STEPS // 2 - 1) as i:
                for b in range(2):
                    step(i * 2 + b, b)
            for g in range(STEPS - 2, STEPS):
                step(g, g % 2)

        def first(g):
            return isinstance(g, int) and g < 2

        @block.sync
        def _(sp):
            def load(g, b):
                if not first(g):
                    sp.wait_ge(vl_ready, (g - 1) * JG)
                    sp.wait_ge(vh_ready, (g - 1) * JG)
                sp.dma_start(vr[:, b], v_l[g]).then_inc(v_loaded[b], 16)
                if isinstance(g, int) and g == 0:
                    for stored in g_stored:
                        sp.wait_ge(stored, G_STORED)
                if not first(g):
                    sp.wait_ge(wf_ready, (g - 1) * JG)
                sp.dma_start(gt[:, b], g_dram[:, :, bass.ds(g * JG, JG), :].rearrange("g i j t -> i g j t")
                             ).then_inc(g_loaded[b], 16)
            pairs(sp, load)

        @block.tensor
        def _(pe):
            def output(g, b):
                for jj in range(JG):
                    pe.wait_ge(vh_ready, g * JG + jj + 1)
                    pe.wait_ge(vl_ready, g * JG + jj + 1)
                    pe.wait_ge(wh_ready, g * JG + jj + 1)
                    pe.wait_ge(wl_ready, g * JG + jj + 1)
                    begins = isinstance(g, int) and g == 0 and jj == 0
                    ends = isinstance(g, int) and g == STEPS - 1 and jj == JG - 1
                    for n in range(2 * NT):
                        tt, dh = n // 2, n % 2
                        w_hi = wh[:, b, jj, tt * P:(tt + 1) * P]
                        w_lo = wl[:, b, jj, tt * P:(tt + 1) * P]
                        v_hi = vh[:, b, jj, dh * 512:(dh + 1) * 512]
                        v_lo = vl[:, b, jj, dh * 512:(dh + 1) * 512]
                        pe.matmul(sums[n][:], w_hi, v_hi, start=begins, stop=False)
                        pe.matmul(sums[n][:], w_hi, v_lo, start=False, stop=False)
                        last = pe.matmul(sums[n][:], w_lo, v_hi, start=False, stop=ends)
                        if ends:
                            last.then_inc(all_done, 1)
                    if not ends:
                        last.then_inc(col_done, 1)
            pairs(pe, output)

        @block.gpsimd
        def _(pool):
            def split_v(g, b):
                for jj in range(JG):
                    pool.wait_ge(vh_ready, g * JG + jj + 1)
                    if not first(g):
                        pool.wait_ge(col_done, (g - 2) * JG + jj + 1)
                    pool.tensor_tensor(vl[:, b, jj], vr[:, b, jj], vh[:, b, jj].bitcast(F32), ALU.subtract
                                       ).then_inc(vl_ready, 1)
            pairs(pool, split_v)

        @block.scalar
        def _(act):
            def step(g, b):
                for jj in range(JG):
                    if jj == 0:
                        act.wait_ge(v_loaded[b], 16 * (g // 2 + 1) if isinstance(g, int) else (g - b) * 8 + 16)
                    if not first(g):
                        act.wait_ge(col_done, (g - 2) * JG + jj + 1)
                    act.activation(vh[:, b, jj], vr[:, b, jj], ACT.Copy).then_inc(vh_ready, 1)
                    act.wait_ge(wf_ready, g * JG + jj + 1)
                    act.activation(wh[:, b, jj], wf[:, jj], ACT.Copy).then_inc(wh_ready, 1)
            pairs(act, step)

        @block.vector
        def _(dve):
            def step(g, b):
                for jj in range(JG):
                    if jj == 0:
                        dve.wait_ge(g_loaded[b], 16 * (g // 2 + 1) if isinstance(g, int) else (g - b) * 8 + 16)
                    if not (isinstance(g, int) and g == 0):
                        dve.wait_ge(wh_ready, g * JG + jj - 1)
                        dve.wait_ge(wl_ready, g * JG + jj - 1)
                    src, col = (first_h, g * JG + jj) if isinstance(g, int) and g < PH // JG else (
                        early_h, g * JG + jj - PH)
                    dve.tensor_tensor(wf[:, jj].rearrange("p (g t) -> p g t", t=TG),
                                      src[:, bass.ds(col, 1)].rearrange("p a (g t) -> p (a g) t", t=TG),
                                      gt[:, b, :, jj, :], ALU.mult).then_inc(wf_ready, 1)
                    dve.wait_ge(wh_ready, g * JG + jj + 1)
                    if not first(g):
                        dve.wait_ge(col_done, (g - 2) * JG + jj + 1)
                    dve.tensor_tensor(wl[:, b, jj], wf[:, jj], wh[:, b, jj].bitcast(F32),
                                      ALU.subtract).then_inc(wl_ready, 1)
            pairs(dve, step)
            for n in range(2 * NT):
                dve.wait_ge(all_done, n + 1)
                dve.tensor_copy(acc[:, n // 2, n % 2 * 512:(n % 2 + 1) * 512], sums[n][:]).then_inc(acc_out, 1)


def dense(nc, xh, xl, u_l, v_l, g_dram, acc, tag):
    with ExitStack() as ctx:
        def sb(name, shape, dt):
            return ctx.enter_context(nc.sbuf_tensor(name + tag, shape, dt))

        def sem(name):
            return ctx.enter_context(nc.semaphore(name + tag))

        ur = sb("ur", [P, 2, JG, C * P], F32)
        uh = sb("uh", [P, JG, C, P], F32R)
        ul = sb("ul", [P, JG, C, P], F32R)
        vr = sb("vr", [P, 2, JG, D], F32)
        vh = sb("vh", [P, 2, JG, D], F32R)
        vl = sb("vl", [P, 2, JG, D], F32R)
        gt = sb("gt", [P, 2, T // TG, JG, TG], F32)
        act_h = sb("act_h", [P, 2, T], F32)
        wf = sb("wf", [P, 2, T], F32)
        wh = sb("wh", [P, 2, JG, T], F32R)
        wl = sb("wl", [P, 2, JG, T], F32R)
        ph = [ctx.enter_context(nc.psum_tensor(f"ph{n}{tag}", [P, T], F32)) for n in range(2)]
        pv = [ctx.enter_context(nc.psum_tensor(f"pv{n}{tag}", [P, T], F32)) for n in range(4)]

        u_loaded = [sem(f"u_loaded{n}") for n in range(2)]
        v_loaded = [sem(f"v_loaded{n}") for n in range(2)]
        g_loaded = [sem(f"g_loaded{n}") for n in range(2)]
        uh_ready = sem("uh_ready")
        ul_ready = sem("ul_ready")
        vh_ready = sem("vh_ready")
        vl_ready = sem("vl_ready")
        h_done = sem("h_done")
        gelu_done = sem("gelu_done")
        wf_ready = sem("wf_ready")
        wh_ready = sem("wh_ready")
        wl_ready = sem("wl_ready")
        v_done = sem("v_done")
        acc_done = sem("acc_done")
        block = ctx.enter_context(nc.Block())

        def pairs(eng, step, first, last):
            for g in range(2):
                step(g, g % 2, g + 1 < GROUPS)
            with eng.Fori(1, GROUPS // 2 - 1) as i:
                for b in range(2):
                    step(i * 2 + b, b, True)
            for g in range(GROUPS - 2, GROUPS):
                step(g, g % 2, g + 1 < GROUPS)

        @block.sync
        def _(sp):
            def load(g, b, more):
                peeled = isinstance(g, int) and g < 2
                if not peeled:
                    sp.wait_ge(ul_ready, (g - 1) * JG)
                    sp.wait_ge(uh_ready, (g - 1) * JG)
                sp.dma_start(ur[:, b], u_l[g]).then_inc(u_loaded[b], 16)
                if not peeled:
                    sp.wait_ge(wf_ready, (g - 1) * JG)
                sp.dma_start(gt[:, b], g_dram[:, :, bass.ds(g * JG, JG), :].rearrange("g i j t -> i g j t")
                             ).then_inc(g_loaded[b], 16)
                if not peeled:
                    sp.wait_ge(vl_ready, (g - 1) * JG)
                    sp.wait_ge(vh_ready, (g - 1) * JG)
                sp.dma_start(vr[:, b], v_l[g]).then_inc(v_loaded[b], 16)
            pairs(sp, load, None, None)

        def count16(g, b):
            if isinstance(g, int):
                return 16 * (g // 2 + 1)
            return (g - b) * 8 + 16

        @block.tensor
        def _(pe):
            def hidden(g, b):
                for jj in range(JG):
                    pe.wait_ge(uh_ready, g * JG + jj + 1)
                    pe.wait_ge(ul_ready, g * JG + jj + 1)
                    if not (isinstance(g, int) and g == 0):
                        pe.wait_ge(gelu_done, g * JG + jj - 1)
                    for c in range(C):
                        pe.matmul(ph[jj][:], uh[:, jj, c, :], xh[:, c, :], start=(c == 0), stop=False)
                        pe.matmul(ph[jj][:], uh[:, jj, c, :], xl[:, c, :], start=False, stop=False)
                        last = pe.matmul(ph[jj][:], ul[:, jj, c, :], xh[:, c, :], start=False,
                                         stop=(c == C - 1))
                    last.then_inc(h_done, 1)

            def output(g, b):
                pe.wait_ge(vh_ready, (g + 1) * JG)
                pe.wait_ge(vl_ready, (g + 1) * JG)
                pe.wait_ge(wh_ready, (g + 1) * JG)
                pe.wait_ge(wl_ready, (g + 1) * JG)
                for n in range(2 * NT):
                    tt, dh = n // 2, n % 2
                    if not (isinstance(g, int) and g == 0 and n < 4):
                        pe.wait_ge(acc_done, g * 8 + n - 3)
                    for jj in range(JG):
                        w_hi = wh[:, b, jj, tt * P:(tt + 1) * P]
                        w_lo = wl[:, b, jj, tt * P:(tt + 1) * P]
                        v_hi = vh[:, b, jj, dh * 512:(dh + 1) * 512]
                        v_lo = vl[:, b, jj, dh * 512:(dh + 1) * 512]
                        pe.matmul(pv[n % 4][:], w_hi, v_hi, start=(jj == 0), stop=False)
                        pe.matmul(pv[n % 4][:], w_hi, v_lo, start=False, stop=False)
                        last = pe.matmul(pv[n % 4][:], w_lo, v_hi, start=False, stop=(jj == JG - 1))
                    last.then_inc(v_done, 1)

            hidden(0, 0)
            hidden(1, 1)
            output(0, 0)
            with pe.Fori(1, GROUPS // 2) as i:
                hidden(i * 2, 0)
                output(i * 2 - 1, 1)
                hidden(i * 2 + 1, 1)
                output(i * 2, 0)
            output(GROUPS - 1, 1)

        @block.scalar
        def _(act):
            def split_u(g, b, jj):
                act.wait_ge(u_loaded[b], count16(g, b))
                if not (isinstance(g, int) and g == 0):
                    act.wait_ge(h_done, (g - 1) * JG + jj + 1)
                act.activation(uh[:, jj].rearrange("p c n -> p (c n)"), ur[:, b, jj], ACT.Copy
                               ).then_inc(uh_ready, 1)

            for jj in range(JG):
                split_u(0, 0, jj)

            def step(g, b, more):
                for jj in range(JG):
                    if jj == 0:
                        act.wait_ge(v_loaded[b], count16(g, b))
                        if not (isinstance(g, int) and g < 2):
                            act.wait_ge(v_done, (g - 1) * 8)
                    act.activation(vh[:, b, jj], vr[:, b, jj], ACT.Copy).then_inc(vh_ready, 1)
                    act.wait_ge(h_done, g * JG + jj + 1)
                    if not (isinstance(g, int) and g == 0):
                        act.wait_ge(wf_ready, g * JG + jj - 1)
                    act.activation(act_h[:, jj], ph[jj][:], ACT.Gelu).then_inc(gelu_done, 1)
                    if more:
                        split_u(g + 1, 1 - b, jj)
                    act.wait_ge(wf_ready, g * JG + jj + 1)
                    act.activation(wh[:, b, jj], wf[:, jj], ACT.Copy).then_inc(wh_ready, 1)
            pairs(act, step, None, None)

        @block.vector
        def _(dve):
            def split_u(g, b, jj):
                dve.wait_ge(uh_ready, g * JG + jj + 1)
                if not (isinstance(g, int) and g == 0):
                    dve.wait_ge(h_done, (g - 1) * JG + jj + 1)
                dve.tensor_tensor(ul[:, jj].rearrange("p c n -> p (c n)"), ur[:, b, jj],
                                  uh[:, jj].rearrange("p c n -> p (c n)").bitcast(F32),
                                  ALU.subtract).then_inc(ul_ready, 1)

            for jj in range(JG):
                split_u(0, 0, jj)

            def add_sums(g):
                for n in range(2 * NT):
                    tt, dh = n // 2, n % 2
                    part = acc[:, tt, dh * 512:(dh + 1) * 512]
                    dve.wait_ge(v_done, g * 8 + n + 1)
                    if not (isinstance(g, int) and g == 0):
                        dve.wait_ge(acc_done, g * 8 + n - 7)
                    dve.tensor_tensor(part, pv[n % 4][:], part, ALU.add).then_inc(acc_done, 1)

            def step(g, b, more):
                for jj in range(JG):
                    dve.wait_ge(vh_ready, g * JG + jj + 1)
                    dve.tensor_tensor(vl[:, b, jj], vr[:, b, jj], vh[:, b, jj].bitcast(F32),
                                      ALU.subtract).then_inc(vl_ready, 1)
                    dve.wait_ge(gelu_done, g * JG + jj + 1)
                    if jj == 0:
                        dve.wait_ge(g_loaded[b], count16(g, b))
                    if not (isinstance(g, int) and g == 0):
                        dve.wait_ge(wh_ready, g * JG + jj - 1)
                        dve.wait_ge(wl_ready, g * JG + jj - 1)
                    dve.tensor_tensor(wf[:, jj].rearrange("p (g t) -> p g t", t=TG),
                                      act_h[:, jj].rearrange("p (g t) -> p g t", t=TG),
                                      gt[:, b, :, jj, :], ALU.mult).then_inc(wf_ready, 1)
                    if more:
                        split_u(g + 1, 1 - b, jj)
                    dve.wait_ge(wh_ready, g * JG + jj + 1)
                    dve.tensor_tensor(wl[:, b, jj], wf[:, jj], wh[:, b, jj].bitcast(F32),
                                      ALU.subtract).then_inc(wl_ready, 1)
                if not (isinstance(g, int) and g == 0):
                    add_sums(g - 1)
            pairs(dve, step, None, None)
            add_sums(GROUPS - 1)


def constants(nc, ctx):
    def sb(name, shape):
        return ctx.enter_context(nc.sbuf_tensor(name, shape, F32))

    ident = sb("ident", [P, P])
    masks = sb("masks", [P, 2, P])
    iota_keys = sb("iota_keys", [P, NK])
    iota_rank = sb("iota_rank", [P, K])
    with ExitStack() as inner:
        cleared = inner.enter_context(nc.semaphore("cleared"))
        block = inner.enter_context(nc.Block())

        @block.gpsimd
        def _(pool):
            pool.memset(ident[:], 0.0).then_inc(cleared, 1)
            pool.memset(masks[:], 0.0).then_inc(cleared, 1)
            pool.iota(iota_keys[:], pattern=[[1, NK]], base=0, channel_multiplier=0,
                      allow_small_or_imprecise_dtypes=True).then_inc(cleared, 1)
            pool.iota(iota_rank[:], pattern=[[1, K]], base=0, channel_multiplier=0,
                      allow_small_or_imprecise_dtypes=True).then_inc(cleared, 1)
            pool.wait_ge(cleared, 4)
            pool.affine_select(out=ident[:], in_=ident[:], compare_op=ALU.not_equal, fill=1.0, base=0,
                               pattern=[[-1, P]], channel_multiplier=1).then_inc(cleared, 1)
            pool.affine_select(out=masks[:, 0], in_=masks[:, 0], compare_op=ALU.is_ge, fill=NEG, base=-1,
                               pattern=[[1, P]], channel_multiplier=-1).then_inc(cleared, 1)
            pool.affine_select(out=masks[:, 1], in_=masks[:, 1], compare_op=ALU.is_ge, fill=NEG, base=0,
                               pattern=[[-1, P]], channel_multiplier=1).then_inc(cleared, 1)
            pool.wait_ge(cleared, 7)
    return ident, masks, iota_keys, iota_rank


class Chain:

    def __init__(self, eng, s, per=0):
        self.eng, self.s, self.n, self.base, self.per = eng, s, 0, 0, per

    def mark(self, ins):
        self.n += 1
        ins.then_inc(self.s, 1)
        return self.n

    def wait(self, n):
        self.eng.wait_ge(self.s, self.base + n)

    def link(self, ins):
        self.wait(self.mark(ins))

    def turn(self, i):
        self.base, self.n = i * self.per, 0

    def turned(self):
        assert self.n == self.per, self.n


def sin_products(dve, x, sin, crossed):
    for q in range(4):
        src, dst = slice(32 * q, 32 * q + 32), slice(32 * (q ^ 1), 32 * (q ^ 1) + 32)
        last = dve.tensor_tensor(crossed[dst], x[src], sin[src], ALU.mult)
    return last


def diff_attention(nc, x, x_t, xres, xh, xl, w_l, cos_t, sin_t, lam, subln, masks, ident, oh, ol):
    TURNS = 4
    CHUNKS = 6
    RING = 3
    PROJ_AT = {1: 2, 2: 3, 4: 4, 6: 5}
    SPLIT_AT = {0: (2, 3), 2: (4, 5)}
    SPLIT_ON = {5: 0, 6: 1}
    SIN_AT = {1: 0, 2: 1, 3: 2, 5: 3}
    with ExitStack() as ctx:
        def sb(name, shape, dt=F32):
            return ctx.enter_context(nc.sbuf_tensor("da_" + name, shape, dt))

        def sem(name):
            return ctx.enter_context(nc.semaphore("da_" + name))

        w = sb("w", [P, RING, C, P])
        wh = sb("wh", [P, C, CHUNKS * P], F32R)
        wl = sb("wl", [P, C, CHUNKS * P], F32R)
        cos, sin = sb("cos", [P, T]), sb("sin", [P, T])
        raw = sb("raw", [P, 4, T])
        crossed = sb("crossed", [P, 4, T])
        rot = sb("rot", [P, 4, T])
        v_next = sb("v_next", [P, NT, 2 * P])
        v = sb("v", [P, NT, 2 * P])
        E = sb("E", [P, 2, 2, T])
        A = sb("A", [P, 2, T])
        AT = sb("AT", [P, 2, NT, P])
        o = sb("o", [P, 8, P])
        sq = sb("sq", [P, P])
        ss = sb("ss", [P, 8])
        rms = sb("rms", [P, 8])
        rstd = sb("rstd", [P, 8])
        nmax = sb("nmax", [P, 2, 2])
        rsum = sb("rsum", [P, 2, 2])
        rinv = sb("rinv", [P, 2, 2])
        lam_row = sb("lam_row", [P, 4, HD])
        lam_prod = sb("lam_prod", [P, 2, HD])
        lam_sum = sb("lam_sum", [P, 2])
        lam_exp = sb("lam_exp", [P, 2])
        neg_lam = sb("neg_lam", [P, 1])
        g_row = sb("g_row", [P, P])
        ps = [ctx.enter_context(nc.psum_tensor(f"da_ps{n}", [P, 2, 512], F32)) for n in range(2)]
        pp = [ctx.enter_context(nc.psum_tensor(f"da_pp{n}", [P, 512], F32)) for n in range(2)]
        pt = ctx.enter_context(nc.psum_tensor("da_pt", [P, 512], F32))
        po = ctx.enter_context(nc.psum_tensor("da_po", [P, 512], F32))

        consts_loaded = sem("consts_loaded")
        xt_loaded = [sem(f"xt_loaded{n}") for n in range(2)]
        x_loaded, xh_ready, xl_ready = sem("x_loaded"), sem("xh_ready"), sem("xl_ready")
        w_loaded = [sem(f"w_loaded{n}") for n in range(RING)]
        wh_ready, wl_ready = sem("wh_ready"), sem("wl_ready")
        proj_done, ot_done = sem("proj_done"), sem("ot_done")
        oh_ready, ol_ready = sem("oh_ready"), sem("ol_ready")
        bank_free = [sem(f"bank_free{n}") for n in range(2)]
        rot_ready, v_ready = sem("rot_ready"), sem("v_ready")
        score_done, nmax_ready, exp_done = sem("score_done"), sem("nmax_ready"), sem("exp_done")
        a_ready, at_done, at_out = sem("a_ready"), sem("at_done"), sem("at_out")
        pv_done, o_out = sem("pv_done"), sem("o_out")
        ms_ready, rms_ready, on_ready = sem("ms_ready"), sem("rms_ready"), sem("on_ready")
        lam_ready, lam_exped, dve_step = sem("lam_ready"), sem("lam_exped"), sem("dve_step")
        block = ctx.enter_context(nc.Block())
        units = [(hl, qb) for hl in range(2) for qb in range(NT)]

        def turns(eng, turn):
            with eng.Fori(0, TURNS - 2) as it:
                turn(it, True, True)
            turn(TURNS - 2, True, False)
            turn(TURNS - 1, False, False)

        @block.sync
        def _(sp):
            def load(t, n):
                if isinstance(t, int) and t == 0:
                    if n >= RING:
                        sp.wait_ge(wl_ready, n - RING + 1)
                else:
                    sp.wait_ge(wl_ready, t * CHUNKS + n - RING + 1)
                sp.dma_start(w[:, n % RING], w_l[t, n]).then_inc(w_loaded[n % RING], 16)

            load(0, 0)
            sp.dma_start(raw[:], x_t[:, 0:4]).then_inc(xt_loaded[0], 16)
            sp.dma_start(rot[:], x_t[:, 4:8]).then_inc(xt_loaded[1], 16)
            for n in range(1, CHUNKS):
                load(0, n)
            sp.dma_start(cos[:], cos_t).then_inc(consts_loaded, 16)
            sp.dma_start(sin[:], sin_t).then_inc(consts_loaded, 16)
            sp.dma_start(lam_row[:], lam.partition_broadcast(P)).then_inc(consts_loaded, 16)
            sp.dma_start(g_row[:], subln.partition_broadcast(P)).then_inc(consts_loaded, 16)
            sp.dma_start(xres[:], x.rearrange("(n p) d -> p n d", p=P)).then_inc(x_loaded, 16)
            with sp.Fori(1, TURNS) as t:
                for n in range(CHUNKS):
                    load(t, n)
            sp.wait_ge(x_loaded, 16)

        @block.gpsimd
        def _(pool):
            def split(t, n):
                pool.wait_ge(wh_ready, t * CHUNKS + n + 1)
                if not (isinstance(t, int) and t == 0):
                    pool.wait_ge(proj_done, (t - 1) * CHUNKS + (n + 1 if n < 4 else 6))
                cols = slice(n * P, (n + 1) * P)
                pool.tensor_tensor(wl[:, :, cols], w[:, n % RING], wh[:, :, cols].bitcast(F32), ALU.subtract
                                   ).then_inc(wl_ready, 1)

            def turn(it, more, more2):
                for b in range(2):
                    pool.wait_ge(bank_free[b], it * 3 + 3)
                if not (isinstance(it, int) and it == 0):
                    pool.wait_ge(pv_done, it * 8)
                pool.tensor_copy(v[:], v_next[:]).then_inc(v_ready, 1)
                for u in range(8):
                    for n in SPLIT_AT.get(u, ()) if more else ():
                        split(it + 1, n)
                    if u in SPLIT_ON and more2:
                        split(it + 2, SPLIT_ON[u])

            for n in range(CHUNKS):
                split(0, n)
            for n in range(2):
                split(1, n)
            turn(0, True, True)
            with pool.Fori(1, TURNS - 2) as it:
                turn(it, True, True)
            turn(TURNS - 2, True, False)
            turn(TURNS - 1, False, False)

        @block.tensor
        def _(pe):
            def project(t, n):
                dst = pp[n % 2]
                if not (isinstance(t, int) and t == 0 and n < 2):
                    pe.wait_ge(bank_free[n % 2], t * 3 + n // 2)
                pe.wait_ge(wl_ready, t * CHUNKS + (n + 1 if n < 4 else 6))
                if n < 4:
                    cols = slice(n * P, (n + 1) * P)
                    for c in range(C):
                        pe.matmul(dst[:], wh[:, c, cols], xh[:, c, :], start=(c == 0), stop=False)
                        pe.matmul(dst[:], wh[:, c, cols], xl[:, c, :], start=False, stop=False)
                        last = pe.matmul(dst[:], wl[:, c, cols], xh[:, c, :], start=False, stop=(c == C - 1))
                else:
                    for half in range(2):
                        tok = slice((2 * (n - 4) + half) * P, (2 * (n - 4) + half + 1) * P)
                        part = dst[:, half * 2 * P:(half + 1) * 2 * P]
                        for c in range(C):
                            pe.matmul(part, xh[:, c, tok], wh[:, c, 4 * P:], start=(c == 0), stop=False)
                            pe.matmul(part, xh[:, c, tok], wl[:, c, 4 * P:], start=False, stop=False)
                            last = pe.matmul(part, xl[:, c, tok], wh[:, c, 4 * P:], start=False,
                                             stop=(c == C - 1))
                last.then_inc(proj_done, 1)

            def turn(it, more, more2):
                def scores(u):
                    hl, qb = units[u]
                    L = (qb + 1) * P
                    if u == 0:
                        pe.wait_ge(rot_ready, it * 4 + 4)
                    pe.wait_ge(exp_done, it * 16 + 2 * u + 2)
                    for p in range(2):
                        rows = slice(HD * p, HD * (p + 1))
                        last = pe.matmul(ps[u % 2][:, p, 0:L], rot[rows, hl, qb * P:(qb + 1) * P],
                                         rot[rows, 2 + hl, 0:L], start=True, stop=True)
                    last.then_inc(score_done, 1)

                scores(0)
                scores(1)
                for u, (hl, qb) in enumerate(units):
                    if u == 0:
                        pe.wait_ge(ol_ready, it * 2 + 2)
                    pe.wait_ge(a_ready, it * 8 + u + 3)
                    pe.wait_ge(at_out, it * 8 + u + 1)
                    for kb in range(qb + 1):
                        last = pe.transpose(pt[:, kb * P:(kb + 1) * P], A[:, u % 2, kb * P:(kb + 1) * P],
                                            ident[:])
                    last.then_inc(at_done, 1)
                    if u + 2 < 8:
                        scores(u + 2)
                    if more and u in PROJ_AT:
                        project(it + 1, PROJ_AT[u])
                    if u == 0:
                        pe.wait_ge(v_ready, it + 1)
                    pe.wait_ge(at_out, it * 8 + u + 2)
                    pe.wait_ge(o_out, it * 8 + u + 1)
                    for kb in range(qb + 1):
                        last = pe.matmul(po[:, 0:P], AT[:, u % 2, kb], v[:, kb, hl * P:(hl + 1) * P],
                                         start=(kb == 0), stop=(kb == qb))
                    last.then_inc(pv_done, 1)
                if more2:
                    project(it + 2, 0)
                for hl in range(2):
                    pe.wait_ge(on_ready, it * 8 + 4 * hl + 4)
                    for qb in range(NT):
                        last = pe.transpose((pt, po)[hl][:, qb * P:(qb + 1) * P], o[:, 4 * hl + qb], ident[:])
                    last.then_inc(ot_done, 1)
                if more2:
                    project(it + 2, 1)

            pe.wait_ge(xl_ready, C)
            for n in range(CHUNKS):
                project(0, n)
            for n in range(2):
                project(1, n)
            turns(pe, turn)

        @block.scalar
        def _(act):
            def split(t, n):
                if isinstance(t, int):
                    act.wait_ge(w_loaded[n % RING], 16 * (2 * t + n // RING + 1))
                else:
                    act.wait_ge(w_loaded[n % RING], t * 32 + 16 * (n // RING + 1))
                if not (isinstance(t, int) and t == 0):
                    act.wait_ge(proj_done, (t - 1) * CHUNKS + (n + 1 if n < 4 else 6))
                act.activation(wh[:, :, n * P:(n + 1) * P], w[:, n % RING], ACT.Copy).then_inc(wh_ready, 1)

            def take(t, n):
                act.wait_ge(proj_done, t * CHUNKS + n + 1)
                dst = raw[:, n] if n < 4 else v_next[:, 2 * (n - 4):2 * (n - 4) + 2].rearrange("p a b -> p (a b)")
                act.activation(dst, pp[n % 2][:], ACT.Copy).then_inc(bank_free[n % 2], 1)

            def turn(it, more, more2):
                def exps(u):
                    L = (units[u][1] + 1) * P
                    act.wait_ge(nmax_ready, it * 8 + u + 1)
                    act.wait_ge(a_ready, it * 8 + u + 1)
                    for p in range(2):
                        act.activation(E[:, u % 2, p, 0:L], ps[u % 2][:, p, 0:L], ACT.Exp,
                                       bias=nmax[:, u % 2, p:p + 1], scale=SCALE,
                                       accum_out=rsum[:, u % 2, p:p + 1]).then_inc(exp_done, 1)

                if more:
                    act.wait_ge(rot_ready, it * 4 + 4)
                    take(it + 1, 0)
                    take(it + 1, 1)
                exps(0)
                for u, (hl, qb) in enumerate(units):
                    act.wait_ge(at_done, it * 8 + u + 1)
                    act.activation(AT[:, u % 2, 0:qb + 1].rearrange("p a b -> p (a b)"), pt[:, 0:(qb + 1) * P],
                                   ACT.Copy).then_inc(at_out, 1)
                    if u + 1 < 8:
                        exps(u + 1)
                    for n in SPLIT_AT.get(u, ()) if more else ():
                        split(it + 1, n)
                    if u in SPLIT_ON and more2:
                        split(it + 2, SPLIT_ON[u])
                    if more and u in PROJ_AT:
                        n = PROJ_AT[u]
                        if n == 4:
                            act.wait_ge(v_ready, it + 1)
                        take(it + 1, n)
                    act.wait_ge(pv_done, it * 8 + u + 1)
                    act.activation(sq[:], po[:, 0:P], ACT.Square, accum_out=ss[:, u:u + 1])
                    act.activation(o[:, u], po[:, 0:P], ACT.Copy).then_inc(o_out, 1)
                act.wait_ge(ms_ready, it + 1)
                act.activation(rms[:], ss[:], ACT.Sqrt).then_inc(rms_ready, 1)
                for hl in range(2):
                    act.wait_ge(ot_done, it * 2 + 1 + hl)
                    act.activation(oh[:, it * 2 + hl, :], (pt, po)[hl][:], ACT.Copy).then_inc(oh_ready, 1)

            for n in range(CHUNKS):
                split(0, n)
                if n == 0:
                    for c in range(C):
                        act.wait_ge(xt_loaded[c // 4], 16)
                        act.activation(xh[:, c], (raw, rot)[c // 4][:, c % 4], ACT.Copy).then_inc(xh_ready, 1)
                    act.wait_ge(xl_ready, C)
                else:
                    take(0, n - 1)
            take(0, CHUNKS - 1)
            for n in range(2):
                split(1, n)
            act.wait_ge(lam_ready, 1)
            act.activation(lam_exp[:], lam_sum[:], ACT.Exp).then_inc(lam_exped, 1)
            act.sem_inc(exp_done, 4)
            act.sem_inc(at_out, 1)
            act.sem_inc(o_out, 1)
            turns(act, turn)

        @block.vector
        def _(dve):
            own = Chain(dve, dve_step)
            for c in range(C):
                dve.wait_ge(xh_ready, c + 1)
                dve.tensor_tensor(xl[:, c], (raw, rot)[c // 4][:, c % 4], xh[:, c].bitcast(F32), ALU.subtract
                                  ).then_inc(xl_ready, 1)
            dve.wait_ge(xl_ready, C)
            dve.wait_ge(consts_loaded, 64)
            own.link(dve.tensor_tensor(lam_prod[:], lam_row[:, 0:4:2], lam_row[:, 1:4:2], ALU.mult))
            dve.tensor_reduce(lam_sum[:], lam_prod[:], AX.X, ALU.add).then_inc(lam_ready, 1)
            dve.wait_ge(lam_exped, 1)
            own.link(dve.tensor_tensor(neg_lam[:], lam_exp[:, 1:2], lam_exp[:, 0:1], ALU.subtract))
            own.link(dve.tensor_scalar(neg_lam[:], neg_lam[:], -LAMBDA_INIT, None, ALU.add))
            own.link(dve.tensor_scalar(g_row[:], g_row[:], 1.0 - LAMBDA_INIT, None, ALU.mult))
            dve.sem_inc(a_ready, 2)
            dve.sem_inc(ol_ready, 2)

            def cross(t, n):
                dve.wait_ge(bank_free[n % 2], t * 3 + n // 2 + 1)
                return sin_products(dve, raw[:, n], sin, crossed[:, n])

            def rotate(t):
                for n in range(4):
                    last = own.mark(dve.tensor_tensor(rot[:, n], raw[:, n], cos[:], ALU.mult))
                own.wait(last)
                for n in range(4):
                    dve.tensor_tensor(rot[:, n], rot[:, n], crossed[:, n], ALU.add).then_inc(rot_ready, 1)

            for n in range(4):
                last = cross(0, n)
            own.link(last)
            rotate(0)
            before = own.n
            own.per = 4 + 4 + 2 * 8 + 3 * 8 + 1

            def turn(it, more, more2):
                own.base, own.n = it * own.per + before, 0

                def maxima(u):
                    hl, qb = units[u]
                    L = (qb + 1) * P
                    dve.wait_ge(score_done, it * 8 + u + 1)
                    diag = ps[u % 2][:, :, qb * P:L]
                    own.link(dve.tensor_tensor(diag, diag, masks[:, 1].unsqueeze(1).broadcast_to([P, 2, P]),
                                               ALU.add))
                    own.link(dve.tensor_reduce(nmax[:, u % 2], ps[u % 2][:, :, 0:L], AX.X, ALU.max,
                                               negate=True))
                    dve.tensor_scalar(nmax[:, u % 2], nmax[:, u % 2], SCALE, None, ALU.mult
                                      ).then_inc(nmax_ready, 1)

                for u, (hl, qb) in enumerate(units):
                    L = (qb + 1) * P
                    b = u % 2
                    maxima(u)
                    dve.wait_ge(exp_done, it * 16 + 2 * u + 6)
                    own.link(dve.reciprocal(rinv[:, b], rsum[:, b]))
                    own.link(dve.tensor_tensor(rinv[:, b, 1:2], rinv[:, b, 1:2], neg_lam[:], ALU.mult))
                    if u >= 2:
                        dve.wait_ge(at_done, it * 8 + u - 1)
                    own.link(dve.tensor_scalar(E[:, b, 0, 0:L], E[:, b, 0, 0:L], rinv[:, b, 0:1], None,
                                               ALU.mult))
                    dve.scalar_tensor_tensor(out=A[:, b, 0:L], in0=E[:, b, 1, 0:L], scalar=rinv[:, b, 1:2],
                                             in1=E[:, b, 0, 0:L], op0=ALU.mult, op1=ALU.add
                                             ).then_inc(a_ready, 1)
                    if more and u in SIN_AT:
                        crossing = own.mark(cross(it + 1, SIN_AT[u]))
                dve.wait_ge(o_out, it * 8 + 9)
                dve.tensor_scalar(ss[:], ss[:], 1.0 / P, EPS, ALU.mult, ALU.add).then_inc(ms_ready, 1)
                dve.wait_ge(rms_ready, it + 1)
                own.link(dve.reciprocal(rstd[:], rms[:]))
                for u in range(8):
                    dve.scalar_tensor_tensor(out=o[:, u], in0=o[:, u], scalar=rstd[:, u:u + 1], in1=g_row[:],
                                             op0=ALU.mult, op1=ALU.mult).then_inc(on_ready, 1)
                if more:
                    own.wait(crossing)
                    rotate(it + 1)
                    own.turned()
                for hl in range(2):
                    dve.wait_ge(oh_ready, it * 2 + 1 + hl)
                    dve.tensor_tensor(ol[:, it * 2 + hl, :], (pt, po)[hl][:], oh[:, it * 2 + hl, :].bitcast(F32),
                                      ALU.subtract).then_inc(ol_ready, 1)

            turns(dve, turn)


def window_attention(nc, xh, xl, w_l, cos_t, sin_t, b_feat, b_v, sinks, masks, ident, oh, ol):
    FOURS = 4
    CHUNKS = 3 + 2 * FOURS
    RING = 4
    BLOCKS = [(f, qb) for f in range(FOURS) for qb in range(NT)]
    with ExitStack() as ctx:
        def sb(name, shape, dt=F32):
            return ctx.enter_context(nc.sbuf_tensor("sw_" + name, shape, dt))

        def sem(name):
            return ctx.enter_context(nc.semaphore("sw_" + name))

        w = sb("w", [P, RING, C, P])
        wh, wl = sb("wh", [P, RING, C, P], F32R), sb("wl", [P, RING, C, P], F32R)
        cos, sin = sb("cos", [P, T]), sb("sin", [P, T])
        bias = sb("bias", [P, CHUNKS])
        bv = sb("bv", [P, P])
        sink = sb("sink", [P, 16])
        raw = sb("raw", [P, 2, T])
        rot_k = sb("rot_k", [P, 2, T])
        rot_q = sb("rot_q", [P, 2, 2, T])
        crossed = sb("crossed", [P, 2, T])
        v = sb("v", [P, NT, P])
        vb = sb("vb", [P, NT, P])
        E = sb("E", [P, 2, 4, 256])
        ET = sb("ET", [P, 2, 4, 2, P])
        o = sb("o", [P, 2, NT, 4, HD])
        mx, mh, nmax, sarg = (sb(n, [P, 2, 4]) for n in ("mx", "mh", "nmax", "sarg"))
        sexp, rsum, den, rinv = (sb(n, [P, 2, 4]) for n in ("sexp", "rsum", "den", "rinv"))
        ps = [ctx.enter_context(nc.psum_tensor(f"sw_ps{n}", [P, 4, 256], F32))[:].rearrange(
            "p (r t) k -> p t r k", r=2) for n in range(2)]
        pp = [ctx.enter_context(nc.psum_tensor(f"sw_pp{n}", [P, 512], F32)) for n in range(2)]
        pt = ctx.enter_context(nc.psum_tensor("sw_pt", [P, 512], F32))
        po = ctx.enter_context(nc.psum_tensor("sw_po", [P, 512], F32))

        consts_loaded = sem("consts_loaded")
        w_loaded = [sem(f"w_loaded{n}") for n in range(RING)]
        wh_ready, wl_ready, proj_done = sem("wh_ready"), sem("wl_ready"), sem("proj_done")
        bank_free = [sem(f"bank_free{n}") for n in range(2)]
        raw_ready, rot_ready, v_out, v_ready = sem("raw_ready"), sem("rot_ready"), sem("v_out"), sem("v_ready")
        score_done, nmax_ready, exp_done = sem("score_done"), sem("nmax_ready"), sem("exp_done")
        at_done, at_out = sem("at_done"), sem("at_out")
        pv_done, on_ready = sem("pv_done"), sem("on_ready")
        ot_done, oh_ready, dve_step = sem("ot_done"), sem("oh_ready"), sem("dve_step")
        block = ctx.enter_context(nc.Block())

        uses = [("w", n) for n in range(7)]
        for f in range(FOURS):
            if f:
                uses += [("o", 2 * (f - 1)), ("o", 2 * (f - 1) + 1)]
            if f + 2 < FOURS:
                uses += [("w", 3 + 2 * (f + 2)), ("w", 4 + 2 * (f + 2))]
        uses += [("o", 2 * (FOURS - 1)), ("o", 2 * (FOURS - 1) + 1)]
        place = {use: n for n, use in enumerate(uses)}

        def ahead(u):
            f, qb = BLOCKS[u]
            return [1 + 2 * (f + 2) + qb] if qb >= 2 and f + 2 < FOURS else []

        @block.sync
        def _(sp):
            for n in range(CHUNKS):
                if n >= RING:
                    sp.wait_ge(wl_ready, n - RING + 1)
                sp.dma_start(w[:, n % RING], w_l[n]).then_inc(w_loaded[n % RING], 16)
                if n == 1:
                    sp.dma_start(bias[:], b_feat).then_inc(consts_loaded, 16)
                    sp.dma_start(cos[:], cos_t).then_inc(consts_loaded, 16)
                    sp.dma_start(sin[:], sin_t).then_inc(consts_loaded, 16)
                    sp.dma_start(bv[:], b_v.partition_broadcast(P)).then_inc(consts_loaded, 16)
                    sp.dma_start(sink[:], sinks.partition_broadcast(P)).then_inc(consts_loaded, 16)

        @block.gpsimd
        def _(pool):
            for n in range(CHUNKS):
                pool.wait_ge(wh_ready, n + 1)
                if n >= RING:
                    pool.wait_ge(proj_done, n - RING + 1)
                pool.tensor_tensor(wl[:, n % RING], w[:, n % RING], wh[:, n % RING].bitcast(F32), ALU.subtract
                                   ).then_inc(wl_ready, 1)

        @block.tensor
        def _(pe):
            def bank(use):
                n = place[use]
                if n >= 2:
                    pe.wait_ge(bank_free[n % 2], n // 2)
                return pp[n % 2]

            def project(n):
                dst = bank(("w", n))
                pe.wait_ge(wl_ready, n + 1)
                if n != 2:
                    for c in range(C):
                        pe.matmul(dst[:], wh[:, n % RING, c], xh[:, c, :], start=(c == 0), stop=False)
                        pe.matmul(dst[:], wh[:, n % RING, c], xl[:, c, :], start=False, stop=False)
                        last = pe.matmul(dst[:], wl[:, n % RING, c], xh[:, c, :], start=False, stop=(c == C - 1))
                else:
                    for tt in range(NT):
                        tok = slice(tt * P, (tt + 1) * P)
                        for c in range(C):
                            pe.matmul(dst[:, tok], xh[:, c, tok], wh[:, n % RING, c], start=(c == 0), stop=False)
                            pe.matmul(dst[:, tok], xh[:, c, tok], wl[:, n % RING, c], start=False, stop=False)
                            last = pe.matmul(dst[:, tok], xl[:, c, tok], wh[:, n % RING, c], start=False,
                                             stop=(c == C - 1))
                last.then_inc(proj_done, 1)

            def scores(u):
                f, qb = BLOCKS[u]
                k0 = max(0, qb - 1) * P
                L = (qb + 1) * P - k0
                if qb == 0:
                    pe.wait_ge(rot_ready, 2 * (f + 2))
                if u >= 2:
                    pe.wait_ge(exp_done, 5 * (u - 1))
                for m in range(4):
                    rows = slice(m % 2 * HD, (m % 2 + 1) * HD)
                    last = pe.matmul(ps[u % 2][:, m // 2, m % 2, 0:L], rot_q[rows, f % 2, m // 2, qb * P:(qb + 1) * P],
                                     rot_k[rows, f // 2, k0:k0 + L], start=True, stop=True)
                last.then_inc(score_done, 1)

            def turn_output(f):
                for cc in range(2):
                    dst = bank(("o", 2 * f + cc))
                    pe.wait_ge(on_ready, 4 * f + 4)
                    for qb in range(NT):
                        last = pe.transpose(dst[:, qb * P:(qb + 1) * P],
                                            o[:, f % 2, qb, 2 * cc:2 * cc + 2].rearrange("p a b -> p (a b)"),
                                            ident[:])
                    last.then_inc(ot_done, 1)

            for n in range(7):
                project(n)
            scores(0)
            scores(1)
            for u, (f, qb) in enumerate(BLOCKS):
                nb = min(2, qb + 1)
                kb0 = max(0, qb - 1)
                for r in range(2):
                    pe.wait_ge(exp_done, 5 * u + 2 * r + 2)
                    if u or r:
                        pe.wait_ge(at_out, 2 * u + r)
                    for m in range(2):
                        for kb in range(nb):
                            last = pe.transpose(pt[:, (2 * m + kb) * P:(2 * m + kb + 1) * P],
                                                E[:, u % 2, 2 * r + m, kb * P:(kb + 1) * P], ident[:])
                    last.then_inc(at_done, 1)
                    if r == 0 and u + 2 < len(BLOCKS):
                        scores(u + 2)
                for n in ahead(u):
                    project(n)
                if qb == 1 and f:
                    turn_output(f - 1)
                if u == 0:
                    pe.wait_ge(v_ready, 1)
                pe.wait_ge(at_out, 2 * u + 2)
                if u:
                    pe.wait_ge(on_ready, u)
                for m in range(4):
                    for kb in range(nb):
                        last = pe.matmul(po[:, m * HD:(m + 1) * HD], ET[:, u % 2, m, kb],
                                         vb[:, kb0 + kb, (f // 2) * HD:(f // 2 + 1) * HD],
                                         start=(kb == 0), stop=(kb == nb - 1))
                last.then_inc(pv_done, 1)
            turn_output(FOURS - 1)

        @block.scalar
        def _(act):
            def split(n):
                act.wait_ge(w_loaded[n % RING], 16 * (n // RING + 1))
                if n >= RING:
                    act.wait_ge(proj_done, n - RING + 1)
                act.activation(wh[:, n % RING], w[:, n % RING], ACT.Copy).then_inc(wh_ready, 1)

            def take(n):
                act.wait_ge(proj_done, n + 1)
                free = bank_free[place[("w", n)] % 2]
                if n == 2:
                    act.activation(v[:].rearrange("p a b -> p (a b)"), pp[0][:], ACT.Copy).then_inc(free, 1)
                    return
                pair, tile = (0, n) if n < 2 else ((n - 3) // 2 + 1, (n - 3) % 2)
                if pair and tile == 0:
                    act.wait_ge(rot_ready, 2 * pair)
                act.activation(raw[:, tile], pp[place[("w", n)] % 2][:], ACT.Identity,
                               bias=bias[:, n:n + 1]).then_inc(free, 1)

            def exps(u):
                L = min(2, BLOCKS[u][1] + 1) * P
                act.wait_ge(nmax_ready, u + 1)
                if u >= 2:
                    act.wait_ge(at_done, 2 * u - 2)
                for m in range(4):
                    act.activation(E[:, u % 2, m, 0:L], ps[u % 2][:, m // 2, m % 2, 0:L], ACT.Exp,
                                   bias=nmax[:, u % 2, m:m + 1], scale=SCALE,
                                   accum_out=rsum[:, u % 2, m:m + 1]).then_inc(exp_done, 1)
                act.activation(sexp[:, u % 2], sarg[:, u % 2], ACT.Exp).then_inc(exp_done, 1)

            for n in range(RING - 1):
                split(n)
            act.wait_ge(consts_loaded, 80)
            for n in range(7):
                split(n + RING - 1)
                take(n)
            exps(0)
            for u, (f, qb) in enumerate(BLOCKS):
                nb = min(2, qb + 1)
                for r in range(2):
                    act.wait_ge(at_done, 2 * u + r + 1)
                    act.activation(ET[:, u % 2, 2 * r:2 * r + 2, 0:nb],
                                   pt[:].rearrange("p (m k n) -> p m k n", m=2, k=2)[:, :, 0:nb], ACT.Copy
                                   ).then_inc(at_out, 1)
                if u + 1 < len(BLOCKS):
                    exps(u + 1)
                for n in ahead(u):
                    take(n)
                    if n + 3 < CHUNKS:
                        split(n + 3)
                if qb == 1 and f or u == len(BLOCKS) - 1:
                    g = f - 1 if qb == 1 else f
                    for cc in range(2):
                        act.wait_ge(ot_done, 2 * g + cc + 1)
                        act.activation(oh[:, 2 * g + cc, :], pp[place[("o", 2 * g + cc)] % 2][:], ACT.Copy
                                       ).then_inc(oh_ready, 1)

        @block.vector
        def _(dve):
            own = Chain(dve, dve_step)
            dve.wait_ge(consts_loaded, 80)

            def cross(pair):
                first = 0 if pair == 0 else 3 + 2 * (pair - 1)
                for tile in range(2):
                    n = place[("w", first + tile)]
                    dve.wait_ge(bank_free[n % 2], n // 2 + 1)
                    sin_products(dve, raw[:, tile], sin, crossed[:, tile])

            def rotate(pair):
                out = rot_k if pair == 0 else rot_q[:, (pair - 1) % 2]
                if pair >= 3:
                    dve.wait_ge(score_done, 4 * (pair - 2))
                for tile in range(2):
                    last = own.mark(dve.tensor_tensor(out[:, tile], raw[:, tile], cos[:], ALU.mult))
                own.wait(last)
                for tile in range(2):
                    last = dve.tensor_tensor(out[:, tile], out[:, tile], crossed[:, tile], ALU.add)
                    last.then_inc(rot_ready, 1)
                dve.wait_ge(rot_ready, 2 * pair + 2)

            def maxima(u):
                f, qb = BLOCKS[u]
                b = u % 2
                L = min(2, qb + 1) * P
                dve.wait_ge(score_done, u + 1)
                mask = masks[:].rearrange("p a b -> p (a b)")[:, 2 * P - L:]
                scores = ps[b][:, :, :, 0:L]
                own.link(dve.tensor_tensor(scores, scores,
                                           mask.unsqueeze(1).unsqueeze(1).broadcast_to([P, 2, 2, L]), ALU.add))
                own.link(dve.tensor_reduce(mx[:, b].rearrange("p (t r) -> p t r", t=2), scores, AX.X, ALU.max))
                own.link(dve.scalar_tensor_tensor(out=mh[:, b], in0=mx[:, b], scalar=SCALE,
                                                  in1=sink[:, 4 * f:4 * f + 4], op0=ALU.mult, op1=ALU.max))
                dve.tensor_scalar(nmax[:, b], mh[:, b], -1.0, None, ALU.mult)
                dve.tensor_tensor(sarg[:, b], sink[:, 4 * f:4 * f + 4], mh[:, b], ALU.subtract
                                  ).then_inc(nmax_ready, 1)

            cross(0)
            rotate(0)
            dve.wait_ge(bank_free[0], 2)
            dve.tensor_tensor(vb[:], v[:], bv[:].unsqueeze(1).broadcast_to([P, NT, P]), ALU.add
                              ).then_inc(v_ready, 1)
            cross(1)
            rotate(1)
            maxima(0)
            for u, (f, qb) in enumerate(BLOCKS):
                b = u % 2
                if u + 1 < len(BLOCKS):
                    maxima(u + 1)
                dve.wait_ge(exp_done, 5 * u + 5)
                own.link(dve.tensor_tensor(den[:, b], rsum[:, b], sexp[:, b], ALU.add))
                own.link(dve.reciprocal(rinv[:, b], den[:, b]))
                if f + 1 < FOURS and qb == 0:
                    cross(f + 2)
                if f + 1 < FOURS and qb == 1:
                    rotate(f + 2)
                dve.wait_ge(pv_done, u + 1)
                if qb == 0 and f >= 2:
                    dve.wait_ge(ot_done, 2 * (f - 1))
                dve.tensor_tensor(o[:, f % 2, qb], po[:, 0:4 * HD].rearrange("p (m e) -> p m e", m=4),
                                  rinv[:, b].unsqueeze(2).broadcast_to([P, 4, HD]), ALU.mult
                                  ).then_inc(on_ready, 1)
                if qb == 1 and f or u == len(BLOCKS) - 1:
                    g = f - 1 if qb == 1 else f
                    for cc in range(2):
                        n = place[("o", 2 * g + cc)]
                        dve.wait_ge(oh_ready, 2 * g + cc + 1)
                        dve.tensor_tensor(ol[:, 2 * g + cc, :], pp[n % 2][:], oh[:, 2 * g + cc, :].bitcast(F32),
                                          ALU.subtract).then_inc(bank_free[n % 2], 1)


def add_and_norm(nc, tag, xres, xh, xl, ident, g, b, *, oh=None, ol=None, w_o=None, b_o=None, acc=None, out=None):
    mix = w_o is not None
    with ExitStack() as ctx:
        def sb(name, shape, dt=F32):
            return ctx.enter_context(nc.sbuf_tensor(name + tag, shape, dt))

        def sem(name):
            return ctx.enter_context(nc.semaphore(name + tag))

        g_row, b_row = sb("g_row", [P, D]), sb("b_row", [P, D])
        bo_row = sb("bo_row", [P, D]) if b_o is not None else None
        if mix:
            wo = sb("wo", [P, 4, D])
            wh, wl = sb("wh", [P, C, D], F32R), sb("wl", [P, C, D], F32R)
        stats = sb("stats", [P, NT, 2, 6])
        mv = sb("mv", [P, NT, 2])
        var, std, rstd, shift = (sb(n, [P, NT]) for n in ("var", "std", "rstd", "shift"))
        banks = [ctx.enter_context(nc.psum_tensor(f"bank{n}{tag}", [P, 512], F32)) for n in range(8)]
        w_loaded = [sem(f"w_loaded{n}") for n in range(4)]
        wh_ready, wl_ready = sem("wh_ready"), sem("wl_ready")
        rows_loaded, stored, xl_ready = sem("rows_loaded"), sem("stored"), sem("xl_ready")
        mix_done, var_ready, std_ready = sem("mix_done"), sem("var_ready"), sem("std_ready")
        scale_ready, normed = sem("scale_ready"), sem("normed")
        x_ready = [sem(f"x_ready{n}") for n in range(2)]
        xt_done, xt_out = sem("xt_done"), sem("xt_out")
        dve_step, pool_step = sem("dve_step"), sem("pool_step")
        block = ctx.enter_context(nc.Block())

        @block.sync
        def _(sp):
            def load_w(c):
                if c >= 4:
                    sp.wait_ge(wl_ready, c - 3)
                sp.dma_start(wo[:, c % 4], w_o[c * P:(c + 1) * P, :]).then_inc(w_loaded[c % 4], 16)

            if mix:
                for c in range(4):
                    load_w(c)
            sp.dma_start(g_row[:], g.partition_broadcast(P)).then_inc(rows_loaded, 16)
            sp.dma_start(b_row[:], b.partition_broadcast(P)).then_inc(rows_loaded, 16)
            if b_o is not None:
                sp.dma_start(bo_row[:], b_o.partition_broadcast(P)).then_inc(rows_loaded, 16)
            if mix:
                for c in range(4, C):
                    load_w(c)
            if out is not None:
                for tt in range(NT):
                    sp.wait_ge(x_ready[tt % 2], tt // 2 + 1)
                    sp.dma_start(out[tt * P:(tt + 1) * P, :], xres[:, tt]).then_inc(stored, 16)
                sp.wait_ge(stored, 16 * NT)

        rows_there = 32 if b_o is None else 48

        def gain_and_bias(eng, own, tt):
            eng.wait_ge(normed, tt + 1)
            own.link(eng.tensor_tensor(xres[:, tt], xres[:, tt], g_row[:], ALU.mult))
            eng.tensor_tensor(xres[:, tt], xres[:, tt], b_row[:], ALU.add).then_inc(x_ready[tt % 2], 1)

        @block.tensor
        def _(pe):
            def product(c, n):
                tok = slice(n // 2 * P, (n // 2 + 1) * P)
                half = slice(n % 2 * 512, (n % 2 + 1) * 512)
                pe.matmul(banks[n][:], oh[:, c, tok], wh[:, c, half], start=(c == 0), stop=False)
                pe.matmul(banks[n][:], oh[:, c, tok], wl[:, c, half], start=False, stop=False)
                last = pe.matmul(banks[n][:], ol[:, c, tok], wh[:, c, half], start=False, stop=(c == C - 1))
                if c == C - 1:
                    last.then_inc(mix_done, 1)

            def transposes(tt):
                if out is not None:
                    return
                pe.wait_ge(x_ready[tt % 2], tt // 2 + 1)
                for half in range(2):
                    for c in range(4):
                        last = pe.transpose(banks[2 * tt + half][:, c * P:(c + 1) * P],
                                            xres[:, tt, (4 * half + c) * P:(4 * half + c + 1) * P], ident[:])
                    last.then_inc(xt_done, 1)

            if mix:
                for c in range(C):
                    pe.wait_ge(wl_ready, c + 1)
                    for n in range(4):
                        product(c, n)
                for n in (4, 5):
                    for c in range(C):
                        product(c, n)
                transposes(0)
                for n in (6, 7):
                    for c in range(C):
                        product(c, n)
            for tt in range(1 if mix else 0, NT):
                transposes(tt)

        @block.gpsimd
        def _(pool):
            if mix:
                for c in range(C):
                    pool.wait_ge(wh_ready, c + 1)
                    pool.tensor_tensor(wl[:, c], wo[:, c % 4], wh[:, c].bitcast(F32), ALU.subtract
                                       ).then_inc(wl_ready, 1)
            own = Chain(pool, pool_step)
            pool.wait_ge(rows_loaded, rows_there)
            for tt in range(0, NT, 2):
                gain_and_bias(pool, own, tt)

        @block.scalar
        def _(act):
            def root(tt):
                act.wait_ge(var_ready, tt + 1)
                act.activation(std[:, tt:tt + 1], var[:, tt:tt + 1], ACT.Sqrt).then_inc(std_ready, 1)

            def norm(tt):
                act.wait_ge(scale_ready, tt + 1)
                act.activation(xres[:, tt], xres[:, tt], ACT.Identity, bias=shift[:, tt:tt + 1],
                               scale=rstd[:, tt:tt + 1]).then_inc(normed, 1)

            def first_part(tt):
                if out is not None:
                    return
                for half in range(2):
                    act.wait_ge(xt_done, 2 * tt + half + 1)
                    act.activation(xh[:, 4 * half:4 * half + 4, tt * P:(tt + 1) * P],
                                   banks[2 * tt + half][:].rearrange("p (c t) -> p c t", c=4), ACT.Copy
                                   ).then_inc(xt_out, 1)

            if mix:
                for c in range(C):
                    act.wait_ge(w_loaded[c % 4], 16 * (c // 4 + 1))
                    act.activation(wh[:, c], wo[:, c % 4], ACT.Copy).then_inc(wh_ready, 1)
            root(0)
            norm(0)
            root(1)
            norm(1)
            if mix:
                root(2)
                norm(2)
                first_part(0)
                root(3)
                norm(3)
            else:
                root(2)
                first_part(0)
                norm(2)
                root(3)
                first_part(1)
                norm(3)
            for tt in range(1 if mix else 2, NT):
                first_part(tt)

        @block.vector
        def _(dve):
            own = Chain(dve, dve_step)
            if b_o is not None:
                dve.wait_ge(rows_loaded, rows_there)
                for tt in range(NT):
                    last = own.mark(dve.scalar_tensor_tensor(out=xres[:, tt], in0=xres[:, tt], scalar=ALPHA,
                                                             in1=bo_row[:], op0=ALU.mult, op1=ALU.add))
                own.wait(last)

            def moments(tt):
                for dh in range(2):
                    half = slice(dh * 512, (dh + 1) * 512)
                    if mix:
                        dve.wait_ge(mix_done, 2 * tt + dh + 1)
                    f = banks[2 * tt + dh][:] if mix else acc[:, tt, half]
                    if b_o is not None:
                        last = own.mark(dve.tensor_tensor(xres[:, tt, half], f, xres[:, tt, half], ALU.add))
                    else:
                        last = own.mark(dve.scalar_tensor_tensor(out=xres[:, tt, half], in0=xres[:, tt, half],
                                                                 scalar=ALPHA, in1=f, op0=ALU.mult, op1=ALU.add))
                own.wait(last)
                for dh in range(2):
                    last = own.mark(dve.bn_stats(stats[:, tt, dh], xres[:, tt, dh * 512:(dh + 1) * 512]))
                own.wait(last)
                own.link(dve.bn_aggr(mv[:, tt], stats[:, tt]))
                dve.tensor_scalar(var[:, tt:tt + 1], mv[:, tt, 1:2], EPS, None, ALU.add).then_inc(var_ready, 1)

            def scale(tt):
                dve.wait_ge(std_ready, tt + 1)
                own.link(dve.reciprocal(rstd[:, tt:tt + 1], std[:, tt:tt + 1]))
                dve.scalar_tensor_tensor(out=shift[:, tt:tt + 1], in0=mv[:, tt, 0:1], scalar=-1.0,
                                         in1=rstd[:, tt:tt + 1], op0=ALU.mult, op1=ALU.mult
                                         ).then_inc(scale_ready, 1)

            def second_part(tt):
                if out is not None:
                    return
                tok = slice(tt * P, (tt + 1) * P)
                for half in range(2):
                    chunks = slice(4 * half, 4 * half + 4)
                    dve.wait_ge(xt_out, 2 * tt + half + 1)
                    dve.tensor_tensor(xl[:, chunks, tok], banks[2 * tt + half][:].rearrange("p (c t) -> p c t", c=4),
                                      xh[:, chunks, tok].bitcast(F32), ALU.subtract).then_inc(xl_ready, 1)

            moments(0)
            if mix:
                scale(0)
                moments(1)
                scale(1)
                dve.wait_ge(rows_loaded, rows_there)
                gain_and_bias(dve, own, 1)
                moments(2)
                scale(2)
                second_part(0)
                moments(3)
                scale(3)
                gain_and_bias(dve, own, 3)
            else:
                moments(1)
                scale(0)
                moments(2)
                scale(1)
                moments(3)
                scale(2)
                dve.wait_ge(rows_loaded, rows_there)
                gain_and_bias(dve, own, 1)
                scale(3)
                second_part(0)
                gain_and_bias(dve, own, 3)
            for tt in range(1, NT):
                second_part(tt)
            if out is None:
                dve.wait_ge(xl_ready, 2 * NT)


def route(nc, tag, xh, xl, ident, iota_rank, wq_l, keys_l, u_l, eiT, ejT, gateT, first_h, early_h):
    with ExitStack() as ctx:
        def sb(name, shape, dt=F32):
            return ctx.enter_context(nc.sbuf_tensor(name + tag, shape, dt))

        def sem(name):
            return ctx.enter_context(nc.semaphore(name + tag))

        TURNS = PH // 2
        wq = sb("wq", [P, 2, C, P])
        wh, wl = sb("wqh", [P, 2, C, P], F32R), sb("wql", [P, 2, C, P], F32R)
        keys = sb("keys", [P, 2, NK])
        qT = sb("qT", [P, 2, T])
        sc = sb("sc", [P, 2, 2, NT, NK])
        came = sb("came", [P, 1])
        rest = sb("rest", [P, 2, NT, NK])
        top = sb("top", [P, 2, NT, 2, K])
        idx = sb("idx", [P, 2, NT, 2, K], U32)
        cand = sb("cand", [P, NT, K, K])
        crest = rest[:].rearrange("p a b n -> p (a b n)").rearrange("p (t n) -> p t n", t=NT)
        tops = sb("tops", [P, 2, NT, K])
        poss = sb("poss", [P, 2, NT, K], U32)
        i1 = sb("i1", [P, NT, PH, K])
        i2 = sb("i2", [P, NT, PH, K])
        ts = sb("ts", [P, NT, PH, K])
        pos = sb("pos", [P, NT, PH, K], U32)
        half_u = sb("half_u", [P, PH * K], U32)
        rank = sb("rank", [P, PH, K])
        eq = sc[:].rearrange("p a b t n -> p (a b t n)").rearrange("p (h k a) -> p h k a", h=PH, k=K)
        eij = sb("eij", [P, 2, 2, PH, K])
        gates = cand[:, 0:2].rearrange("p a b c -> p (a b) c")
        gsum = sb("gsum", [P, NT * PH])
        ginv = sb("ginv", [P, NT * PH])
        pq = [ctx.enter_context(nc.psum_tensor(f"pq{n}{tag}", [P, 512], F32)) for n in range(2)]
        psc = [ctx.enter_context(nc.psum_tensor(f"psc{n}{tag}", [P, 512], F32)) for n in range(4)]
        ptr = psc[0]
        ph = [ctx.enter_context(nc.psum_tensor(f"ph_early{n}{tag}", [P, 512], F32)) for n in range(2)]
        ur = sb("early_u", [P, 2, C * P])
        uh, ul = sb("early_uh", [P, 2, C, P], F32R), sb("early_ul", [P, 2, C, P], F32R)
        u_loaded = [sem(f"early_u_loaded{n}") for n in range(2)]
        uh_ready, ul_ready = sem("early_uh_ready"), sem("early_ul_ready")
        h_done, gelu_done = sem("early_h_done"), sem("early_gelu_done")
        BEFORE = 7
        bounds = [min(PH + BEFORE + 4 * tt, ROUTED) for tt in range(NT + 1)]
        tails = [range(PH, bounds[1])] + [range(bounds[tt], bounds[tt + 1]) for tt in range(1, NT)]
        assert bounds[NT] == ROUTED
        w_loaded = [sem(f"w_loaded{n}") for n in range(2)]
        wh_ready, wl_ready = sem("wqh_ready"), sem("wql_ready")
        q_done, q_out = sem("q_done"), sem("q_out")
        sc_done, sc_out = sem("sc_done"), sem("sc_out")
        top_done, dve_step = sem("top_done"), sem("dve_step")
        exp_in, exp_out = sem("exp_in"), sem("exp_out")
        tr_ready, tr_done, tr_out = sem("tr_ready"), sem("tr_done"), sem("tr_out")
        block = ctx.enter_context(nc.Block())

        @block.sync
        def _(sp):
            with sp.Fori(0, TURNS) as it:
                for b in range(2):
                    sp.wait_ge(sc_done, it * 4 + 2 * b + 2)
                    sp.dma_start(wq[:, b], wq_l[it * 2 + b]).then_inc(w_loaded[b], 16)
                    sp.dma_start(keys[:, b], keys_l[it * 2 + b]).then_inc(w_loaded[b], 16)
                    sp.wait_ge(ul_ready, it * 2 + b + 1)
                    sp.dma_start(ur[:, b], u_l[it, :, b]).then_inc(u_loaded[b], 16)
            for col in range(PH, ROUTED):
                sp.wait_ge(ul_ready, col + 1)
                sp.dma_start(ur[:, col % 2], u_l[col // JG, :, col % JG]).then_inc(u_loaded[col % 2], 16)

        @block.tensor
        def _(pe):
            def hidden(col, b):
                pe.wait_ge(uh_ready, col + 1)
                pe.wait_ge(ul_ready, col + 3)
                pe.wait_ge(gelu_done, col + 1)
                for c in range(C):
                    pe.matmul(ph[b][:], uh[:, b, c], xh[:, c, :], start=(c == 0), stop=False)
                    pe.matmul(ph[b][:], uh[:, b, c], xl[:, c, :], start=False, stop=False)
                    last = pe.matmul(ph[b][:], ul[:, b, c], xh[:, c, :], start=False, stop=(c == C - 1))
                last.then_inc(h_done, 1)

            pe.sem_inc(sc_done, 4)
            pe.sem_inc(h_done, 2)
            with pe.Fori(0, TURNS) as it:
                for b in range(2):
                    pe.wait_ge(w_loaded[b], it * 32 + 32)
                    pe.wait_ge(q_out, it * 2 + b + 1)
                    pe.wait_ge(wl_ready, it * 2 + b + 1)
                    for c in range(C):
                        pe.matmul(pq[b][:], wh[:, b, c], xh[:, c, :], start=(c == 0), stop=False)
                        pe.matmul(pq[b][:], wh[:, b, c], xl[:, c, :], start=False, stop=False)
                        last = pe.matmul(pq[b][:], wl[:, b, c], xh[:, c, :], start=False, stop=(c == C - 1))
                    last.then_inc(q_done, 1)
                    pe.wait_ge(q_out, it * 2 + b + 3)
                    pe.wait_ge(sc_out, it * 4 + 2 * b + 2)
                    for half in range(2):
                        rows = slice(half * 64, half * 64 + 64)
                        for tt in range(NT):
                            last = pe.matmul(psc[2 * b + half][:, tt * NK:(tt + 1) * NK],
                                             qT[rows, b, tt * P:(tt + 1) * P], keys[rows, b],
                                             start=True, stop=True)
                        last.then_inc(sc_done, 1)
                    hidden(it * 2 + b, b)
            for tt in range(NT):
                for col in tails[tt]:
                    hidden(col, col % 2)
                pe.wait_ge(tr_ready, tt + 1)
                if tt:
                    pe.wait_ge(tr_out, 3 * tt)
                else:
                    pe.wait_ge(sc_out, 4 + 2 * PH)
                for n, src in enumerate((eij[:, tt % 2, 0], eij[:, tt % 2, 1],
                                         gates[:, tt * PH:(tt + 1) * PH])):
                    last = pe.transpose(ptr[:, n * P:(n + 1) * P], src.rearrange("p a b -> p (a b)"), ident[:])
                last.then_inc(tr_done, 1)

        @block.gpsimd
        def _(pool):
            def split_u(col, b):
                pool.wait_ge(uh_ready, col + 1)
                pool.wait_ge(h_done, col + 1)
                pool.tensor_tensor(ul[:, b].rearrange("p c n -> p (c n)"), ur[:, b],
                                   uh[:, b].rearrange("p c n -> p (c n)").bitcast(F32), ALU.subtract
                                   ).then_inc(ul_ready, 1)

            pool.sem_inc(q_done, 2)
            pool.sem_inc(ul_ready, 2)
            with pool.Fori(0, TURNS) as it:
                for b in range(2):
                    pool.wait_ge(wh_ready, it * 2 + b + 1)
                    pool.wait_ge(q_done, it * 2 + b + 1)
                    pool.tensor_tensor(wl[:, b], wq[:, b], wh[:, b].bitcast(F32), ALU.subtract
                                       ).then_inc(wl_ready, 1)
                    split_u(it * 2 + b, b)
            for col in range(PH, ROUTED):
                split_u(col, col % 2)

        @block.scalar
        def _(act):
            act.sem_inc(q_out, 2)
            act.sem_inc(sc_out, 4)

            def split(head, b):
                act.wait_ge(w_loaded[b], (head - b) * 16 + 32)
                act.wait_ge(q_done, head + 1)
                act.activation(wh[:, b], wq[:, b], ACT.Copy).then_inc(wh_ready, 1)

            def split_u(col, b):
                act.wait_ge(u_loaded[b], (col - b) * 8 + 16)
                act.wait_ge(h_done, col + 1)
                act.activation(uh[:, b].rearrange("p c n -> p (c n)"), ur[:, b], ACT.Copy).then_inc(uh_ready, 1)

            def gelu(dst, col, b):
                act.wait_ge(h_done, col + 3)
                act.activation(dst, ph[b][:], ACT.Gelu).then_inc(gelu_done, 1)

            def turn(it, more):
                for b in range(2):
                    head = it * 2 + b
                    act.wait_ge(q_done, head + 3)
                    act.wait_ge(sc_done, 2 * head + 2)
                    act.activation(qT[:, b], pq[b][:], ACT.Copy).then_inc(q_out, 1)
                    if more or b == 0:
                        split(head + 1, 1 - b)
                    split_u(head + 1, 1 - b)
                    act.wait_ge(top_done, head + 1)
                    for half in range(2):
                        act.wait_ge(sc_done, 2 * head + half + 5)
                        act.activation(sc[:, b, half].rearrange("p a b -> p (a b)"), psc[2 * b + half][:],
                                       ACT.Copy).then_inc(sc_out, 1)
                    gelu(first_h[:, bass.ds(head, 1)].rearrange("p a t -> p (a t)"), head, b)

            act.sem_inc(gelu_done, 2)
            split(0, 0)
            split_u(0, 0)
            with act.Fori(0, TURNS - 1) as it:
                turn(it, True)
            turn(TURNS - 1, False)
            for tt in range(NT):
                for col in tails[tt]:
                    if col + 1 < ROUTED:
                        split_u(col + 1, (col + 1) % 2)
                    if col == PH + BEFORE:
                        act.wait_ge(exp_in, 1)
                        act.activation(gates, gates, ACT.Exp).then_inc(exp_out, 1)
                    gelu(early_h[:, col - PH], col, col % 2)
                act.wait_ge(tr_done, tt + 1)
                for n, dst in enumerate((eiT, ejT, gateT)):
                    act.activation(dst[:, tt * P:(tt + 1) * P], ptr[:, n * P:(n + 1) * P], ACT.Copy
                                   ).then_inc(tr_out, 1)

        @block.vector
        def _(dve):
            own = Chain(dve, dve_step)
            dve.sem_inc(top_done, 2)

            def top16(lists):
                seen = [own.mark(dve.max(out_top[:, 0:8], values)) for values, out_top, _, _ in lists]
                gone = []
                for n, (values, out_top, out_idx, scratch) in zip(seen, lists):
                    own.wait(n)
                    dve.max_index(out_idx[:, 0:8], out_top[:, 0:8], values)
                    gone.append(own.mark(dve.match_replace(scratch, out_top[:, 0:8], values, -3.0e38)))
                seen = []
                for n, (_, out_top, _, scratch) in zip(gone, lists):
                    own.wait(n)
                    seen.append(own.mark(dve.max(out_top[:, 8:16], scratch)))
                for n, (_, out_top, out_idx, scratch) in zip(seen, lists):
                    own.wait(n)
                    last = own.mark(dve.max_index(out_idx[:, 8:16], out_top[:, 8:16], scratch))
                return last

            with dve.Fori(0, TURNS) as it:
                for b in range(2):
                    dve.sem_clear(dve_step)
                    own.n = 0
                    dve.wait_ge(sc_out, it * 4 + 2 * b + 6)
                    own.link(dve.tensor_copy(came[:], sc[:, b, 1, 0, 0:1]))
                    last = top16([(sc[:, b, half, tt], top[:, b, tt, half], idx[:, b, tt, half], rest[:, half, tt])
                                  for tt in range(NT) for half in range(2)])
                    own.wait(last)
                    for tt in range(NT):
                        last = own.mark(dve.tensor_tensor(
                            cand[:, tt], top[:, b, tt, 0].unsqueeze(2).broadcast_to([P, K, K]),
                            top[:, b, tt, 1].unsqueeze(1).broadcast_to([P, K, K]), ALU.add))
                    own.wait(last)
                    own.wait(top16([(cand[:, tt].rearrange("p a b -> p (a b)"), tops[:, b, tt], poss[:, b, tt],
                                     crest[:, tt]) for tt in range(NT)]))
                    head = it * 2 + b
                    dve.tensor_copy(i1[:, :, head, :], idx[:, b, :, 0])
                    dve.tensor_copy(i2[:, :, head, :], idx[:, b, :, 1])
                    dve.tensor_copy(ts[:, :, head, :], tops[:, b])
                    dve.tensor_copy(pos[:, :, head, :], poss[:, b]).then_inc(top_done, 1)
            dve.wait_ge(top_done, 2 + PH)
            dve.sem_clear(dve_step)
            own.n = 0
            sums = ts[:].rearrange("p a b k -> p (a b) k")
            dve.tensor_tensor(gates, sums, sums[:, :, 0:1].broadcast_to([P, NT * PH, K]), ALU.subtract
                              ).then_inc(exp_in, 1)
            for tt in range(NT):
                if tt >= 2:
                    dve.wait_ge(tr_done, tt - 1)
                for side, (op, arg, ids) in enumerate(((ALU.logical_shift_right, 4, i1),
                                                       (ALU.bitwise_and, K - 1, i2))):
                    own.link(dve.tensor_scalar(half_u[:], pos[:, tt].rearrange("p a b -> p (a b)"), arg, None, op))
                    own.link(dve.tensor_copy(rank[:].rearrange("p a b -> p (a b)"), half_u[:]))
                    own.link(dve.tensor_tensor(
                        eq.rearrange("p h k a -> p (h k) a"),
                        rank[:].rearrange("p h k -> p (h k)").unsqueeze(2).broadcast_to([P, PH * K, K]),
                        iota_rank[:].unsqueeze(1).broadcast_to([P, PH * K, K]), ALU.is_equal))
                    own.link(dve.tensor_tensor(eq, eq, ids[:, tt].unsqueeze(2).broadcast_to([P, PH, K, K]),
                                               ALU.mult))
                    own.link(dve.tensor_reduce(eij[:, tt % 2, side], eq, AX.X, ALU.add))
                if tt == 0:
                    dve.wait_ge(exp_out, 1)
                    own.link(dve.tensor_reduce(gsum[:], gates, AX.X, ALU.add))
                    own.link(dve.reciprocal(ginv[:], gsum[:]))
                    own.link(dve.tensor_tensor(gates, gates, ginv[:].unsqueeze(2).broadcast_to([P, NT * PH, K]),
                                               ALU.mult))
                dve.sem_inc(tr_ready, 1)


def spread_gates(nc, tag, iota_keys, eiT, ejT, gateT, xh, xl, u_l, early_h, g_dram, g_stored):
    SUB = 8
    STEPS = TG // SUB
    BLOCKS = 8
    N = BLOCKS * STEPS
    TURNS = T // TG // BLOCKS
    COLS = EARLY - ROUTED
    PART = N * TURNS // COLS
    PER_TURN = COLS // TURNS
    PER_STEP = 2
    with ExitStack() as ctx:
        def sb(name, shape, dt=F32):
            return ctx.enter_context(nc.sbuf_tensor(name + tag, shape, dt))

        def sem(name):
            return ctx.enter_context(nc.semaphore(name + tag))

        stage = sb("stage", [P, 2, NK, TG])
        left = sb("left", [P, 2, SUB, NK])
        hot = sb("hot", [P, 2, SUB, NK])
        right = sb("right", [P, 2, SUB, NK])
        ur = sb("spread_u", [P, COLS, C * P])
        uh, ul = sb("spread_uh", [P, C, P], F32R), sb("spread_ul", [P, C, P], F32R)
        ph = ctx.enter_context(nc.psum_tensor("ph_spread" + tag, [P, T], F32))
        u_loaded, uh_ready, ul_ready = sem("spread_u_loaded"), sem("spread_uh_ready"), sem("spread_ul_ready")
        h_done, gelu_done = sem("spread_h_done"), sem("spread_gelu_done")
        banks = [ctx.enter_context(nc.psum_tensor(f"gbank{n}{tag}", [P, 4, NK], F32)) for n in range(4)]
        hot_ready = sem("hot_ready")
        left_ready, right_ready = sem("left_ready"), sem("right_ready")
        g_done, g_out = sem("g_done"), sem("g_out")
        block = ctx.enter_context(nc.Block())

        @block.sync
        def _(sp):
            for b in range(2):
                sp.sem_inc(g_stored[b], 16)
            for n in range(COLS):
                col = ROUTED + n
                sp.dma_start(ur[:, n], u_l[col // JG, :, col % JG]).then_inc(u_loaded, 16)
            with sp.Fori(0, TURNS) as it:
                for n in range(BLOCKS):
                    sp.wait_ge(g_out, it * 2 * N + (n + 1) * 2 * STEPS + 4)
                    sp.dma_start(g_dram[it * BLOCKS + n], stage[:, n % 2]).then_inc(g_stored[n % 2], 16)
            sp.wait_ge(g_stored[0], G_STORED)

        def columns(m, t0):
            return m[:, bass.ds(t0, SUB)].unsqueeze(2).broadcast_to([P, SUB, NK])

        @block.gpsimd
        def _(pool):
            with pool.Fori(0, TURNS) as it:
                for s in range(N):
                    if s % PART == 3:
                        n = it * PER_TURN + s // PART
                        pool.wait_ge(uh_ready, n + 1)
                        pool.wait_ge(h_done, n + 1)
                        pool.tensor_tensor(ul[:].rearrange("p c n -> p (c n)"),
                                           ur[:, bass.ds(n, 1)].rearrange("p a n -> p (a n)"),
                                           uh[:].rearrange("p c n -> p (c n)").bitcast(F32), ALU.subtract
                                           ).then_inc(ul_ready, 1)
                    pool.wait_ge(hot_ready, it * N + s + 1)
                    pool.wait_ge(g_done, it * N + s + 1)
                    pool.tensor_tensor(right[:, s % 2], hot[:, s % 2], columns(gateT, it * (BLOCKS * TG) + s * SUB),
                                       ALU.mult).then_inc(right_ready, 1)

        @block.vector
        def _(dve):
            iota = iota_keys[:].unsqueeze(1).broadcast_to([P, SUB, NK])
            dve.sem_inc(right_ready, 2)
            with dve.Fori(0, TURNS) as it:
                for s in range(N):
                    t0 = it * (BLOCKS * TG) + s * SUB
                    dve.wait_ge(right_ready, it * N + s + 1)
                    dve.tensor_tensor(hot[:, s % 2], iota, columns(ejT, t0), ALU.is_equal).then_inc(hot_ready, 1)
                    dve.wait_ge(g_done, it * N + s + 1)
                    dve.tensor_tensor(left[:, s % 2], iota, columns(eiT, t0), ALU.is_equal).then_inc(left_ready, 1)

        @block.tensor
        def _(pe):
            pe.sem_inc(g_done, 2)
            pe.sem_inc(h_done, 1)
            with pe.Fori(0, TURNS) as it:
                for s in range(N):
                    pe.wait_ge(left_ready, it * N + s + 1)
                    pe.wait_ge(right_ready, it * N + s + 3)
                    pe.wait_ge(g_out, it * 2 * N + 2 * s + 2)
                    for n in range(SUB):
                        last = pe.matmul(banks[2 * (s % 2) + n // 4][:, n % 4], left[:, s % 2, n],
                                         right[:, s % 2, n], start=True, stop=True)
                    last.then_inc(g_done, 1)
                    first = (s % PART - PART) * PER_STEP + 3 * C
                    if first >= 0:
                        n = it * PER_TURN + s // PART
                        if first == 0:
                            pe.wait_ge(ul_ready, n + 1)
                            pe.wait_ge(gelu_done, n + 1)
                        for m in range(first, first + PER_STEP):
                            u_part, x_part = ((uh, xh), (uh, xl), (ul, xh))[m % 3]
                            last = pe.matmul(ph[:], u_part[:, m // 3, :], x_part[:, m // 3, :], start=(m == 0),
                                             stop=(m == 3 * C - 1))
                        if m == 3 * C - 1:
                            last.then_inc(h_done, 1)

        @block.scalar
        def _(act):
            act.sem_inc(g_out, 4)
            act.sem_inc(gelu_done, 1)
            act.wait_ge(u_loaded, 16 * COLS)
            with act.Fori(0, TURNS) as it:
                for s in range(N):
                    col = it * PER_TURN + s // PART
                    if s % PART == 0:
                        act.wait_ge(h_done, col + 1)
                        act.activation(uh[:].rearrange("p c n -> p (c n)"),
                                       ur[:, bass.ds(col, 1)].rearrange("p a n -> p (a n)"), ACT.Copy
                                       ).then_inc(uh_ready, 1)
                    n = s // STEPS
                    b = n % 2
                    act.wait_ge(g_done, it * N + s + 3)
                    if s % STEPS == 0:
                        act.wait_ge(g_stored[b], it * (8 * BLOCKS) + 16 * (n // 2 + 1))
                    for q in range(2):
                        t0 = (s % STEPS) * SUB + 4 * q
                        act.activation(stage[:, b, :, t0:t0 + 4], banks[2 * (s % 2) + q][:].rearrange("p t j -> p j t"),
                                       ACT.Copy).then_inc(g_out, 1)
                    if s % PART == PART - 1:
                        act.wait_ge(h_done, col + 2)
                        act.activation(early_h[:, bass.ds(ROUTED - PH + col, 1)].rearrange("p a t -> p (a t)"), ph[:],
                                       ACT.Gelu).then_inc(gelu_done, 1)


def clear_semaphores(nc):
    free = sorted(nc.free_semaphores)
    assert free == list(range(free[0], free[-1] + 1))
    with nc.Block() as block:
        @block.gpsimd
        def _(pool):
            pool.sem_clear(range(free[0], free[-1] + 1))


def trunk(nc, a, out):
    g_dram = nc.dram_tensor("g_dram", [T // TG, P, NK, TG], F32, kind="Internal").ap()
    with ExitStack() as ctx:
        def sb(name, shape, dt=F32):
            return ctx.enter_context(nc.sbuf_tensor(name, shape, dt))

        xres = sb("xres", [P, NT, D])
        xh, xl = sb("xh", [P, C, T], F32R), sb("xl", [P, C, T], F32R)
        ident, masks, iota_keys, iota_rank = constants(nc, ctx)
        for layer in range(DEPTH):
            tag = f"_{layer}"
            if layer:
                clear_semaphores(nc)
            with nc.sbuf_tensor("oh" + tag, [P, C, T], F32R) as oh, nc.sbuf_tensor("ol" + tag, [P, C, T], F32R) as ol:
                if layer % 2 == 0:
                    diff_attention(nc, a["x"], a["x_t"], xres, xh, xl, a["da_w"], a["cos_t"], a["sin_t"],
                                   a["da_lambda"], a["da_subln_g"], masks, ident, oh, ol)
                    w_o, b_o = a["da_w_o"], None
                else:
                    window_attention(nc, xh, xl, a["sw_w"], a["cos_t"], a["sin_t"], a["sw_b"], a["sw_bv"],
                                     a["sw_sinks"], masks, ident, oh, ol)
                    w_o, b_o = a["sw_w_o"], a["sw_b_o"]
                add_and_norm(nc, "_m" + tag, xres, xh, xl, ident, a["ln1_g"][layer], a["ln1_b"][layer], oh=oh, ol=ol,
                             w_o=w_o, b_o=b_o)
            with nc.sbuf_tensor("acc" + tag, [P, NT, D], F32) as acc:
                first_h = acc[:].rearrange("p n d -> p (n d)").rearrange("p (c t) -> p c t", t=T)
                with nc.sbuf_tensor("early_h" + tag, [P, EARLY - PH, T], F32) as early_h, ExitStack() as stores:
                    g_stored = [stores.enter_context(nc.semaphore(f"g_stored{n}{tag}")) for n in range(2)]
                    with ExitStack() as routed:
                        eiT, ejT, gateT = (routed.enter_context(nc.sbuf_tensor(n + tag, [P, T], F32))
                                           for n in ("eiT", "ejT", "gateT"))
                        route(nc, tag, xh, xl, ident, iota_rank, a["pk_wq"][layer], a["pk_keys"][layer],
                              a["pk_u"][layer], eiT, ejT, gateT, first_h, early_h)
                        spread_gates(nc, tag, iota_keys, eiT, ejT, gateT, xh, xl, a["pk_u"][layer], early_h,
                                     g_dram, g_stored)
                    early_columns(nc, first_h, early_h, a["pk_v"][layer], g_dram, g_stored, acc, tag)
                late = EARLY // JG
                dense(nc, xh, xl, a["pk_u"][layer][late:], a["pk_v"][layer][late:], g_dram[:, :, EARLY:], acc, tag)
                last = layer == DEPTH - 1
                add_and_norm(nc, "_p" + tag, xres, xh, xl, ident, a["ln2_g"][layer], a["ln2_b"][layer], acc=acc,
                             out=out if last else None)


def lay_out(np, x, da_w_qkv, da_lambda, da_subln_g, da_w_o, sw_w_qkv, sw_b_qkv, sw_sinks, sw_w_o, sw_b_o,
            pk_w_query, pk_sub_keys, pk_u, pk_v, ln1_g, ln1_b, ln2_g, ln2_b):
    def tiled(w):
        return w.reshape(*w.shape[:-2], C, P, w.shape[-1]).swapaxes(-3, -2)

    a = {"x": x[0], "x_t": tiled(x[0].T)}
    inv = (1.0 / (10000.0 ** (np.arange(0, HD, 2, dtype=np.float32) / np.float32(HD)))).astype(np.float32)
    ang = np.arange(T, dtype=np.float32)[:, None] * inv[None, :]
    a["cos_t"] = np.tile(np.cos(ang).T, (4, 1)).astype(np.float32)
    a["sin_t"] = np.tile(np.concatenate([np.sin(ang).T, -np.sin(ang).T]), (2, 1)).astype(np.float32)

    cols = []
    for it in range(4):
        for part in range(3):
            cols += list(range(part * D + it * 2 * P, part * D + (it + 1) * 2 * P))
    a["da_w"] = tiled(da_w_qkv[0][:, cols]).reshape(P, C, 4, 6, P).transpose(2, 3, 0, 1, 4)
    a["da_lambda"] = da_lambda[0]
    a["da_subln_g"] = da_subln_g[0]
    a["da_w_o"] = da_w_o[0]

    w, b = sw_w_qkv[0], sw_b_qkv[0]
    cols = []
    for kv in range(2):
        cols += 2 * list(range((16 + kv) * HD, (17 + kv) * HD))
    cols += list(range(18 * HD, 20 * HD)) + list(range(16 * HD))
    a["sw_w"] = tiled(w[:, cols]).reshape(P, C, 11, P).transpose(2, 0, 1, 3)
    a["sw_b"] = b[cols].reshape(11, P).T
    a["sw_bv"] = b[18 * HD:]
    a["sw_sinks"] = sw_sinks[0]
    a["sw_w_o"] = sw_w_o[0]
    a["sw_b_o"] = sw_b_o[0]

    a["pk_wq"] = tiled(pk_w_query).reshape(DEPTH, P, C, PH, P).transpose(0, 3, 1, 2, 4)
    a["pk_keys"] = pk_sub_keys.transpose(0, 1, 2, 4, 3).reshape(DEPTH, PH, P, NK)
    a["pk_u"] = pk_u.reshape(DEPTH, P, NK // JG, JG, C, P).transpose(0, 2, 5, 3, 4, 1).reshape(
        DEPTH, NK // JG, P, JG, C * P)
    a["pk_v"] = pk_v.reshape(DEPTH, P, NK // JG, JG, D).transpose(0, 2, 1, 3, 4)
    a["ln1_g"], a["ln1_b"], a["ln2_g"], a["ln2_b"] = ln1_g, ln1_b, ln2_g, ln2_b
    return a


def kernel(**inputs):
    import concourse.bacc as bacc
    import numpy as np
    from concourse.bass_utils import run_bass_kernel_spmd

    nc = bacc.Bacc("TRN2", target_bir_lowering=False, num_devices=1)
    laid = lay_out(np, **{k: np.asarray(v) for k, v in inputs.items()})
    arrays, aps = {}, {}
    for name, v in laid.items():
        v = np.ascontiguousarray(v)
        arrays[f"in_{name}"] = v
        aps[name] = nc.dram_tensor(f"in_{name}", v.shape, mybir.dt.from_np(v.dtype), kind="ExternalInput").ap()
    out = nc.dram_tensor("out", [T, D], F32, kind="ExternalOutput").ap()
    trunk(nc, aps, out)
    r = run_bass_kernel_spmd(nc, [arrays], core_ids=[0])
    return r.results[0]["out"].reshape(1, T, D)
```
